# Optimizing a Trainium2 kernel written in Bass

```python
import math
import jax, jax.numpy as jnp
from jax import lax
import numpy as np
import jax
import jax.numpy as jnp

D_MODEL = 1024
BATCH = 1
SEQ = 256
DEPTH = 1

CTX_LEN = 256
GRID_W = 64
EPS = 1e-6

HG_HEADS = 4
HG_DK = 128
HG_DV = 128
HG_KDIM = HG_HEADS * HG_DK
HG_WIDTH = HG_HEADS * HG_DV
CHUNK = 32

HY_WIDTH = 512
HY_SHORT = 3
HY_EMB = 33
HY_FILTER_HIDDEN = 64
HY_FILTER_SCALE = 0.05
HY_DECAY_TARGET = 1e-2
HY_FAST_PCT = 0.3
HY_SLOW_PCT = 1.5

SPLIT_POINTS = (HG_KDIM, 2 * HG_KDIM, 3 * HG_KDIM, 3 * HG_KDIM + HG_WIDTH,
                3 * HG_KDIM + 2 * HG_WIDTH, 3 * HG_KDIM + 2 * HG_WIDTH + 3 * HY_WIDTH)
IN_WIDTH = 3 * HG_KDIM + 2 * HG_WIDTH + 3 * HY_WIDTH + 2 * D_MODEL

N_GROUPS = 4
EXPERTS_PER_GROUP = 8
TOP_K = 2
D_EXPERT = 512


F32 = jnp.float32

def rms_norm(x, g):
    xf = x.astype(F32)
    y = xf * lax.rsqrt(jnp.mean(xf * xf, axis=-1, keepdims=True) + EPS)
    return (y * g.astype(F32)).astype(x.dtype)

def adaln(cvec, w, b):
    m = jax.nn.silu(cvec) @ w + b
    return [t[..., None, :] for t in jnp.split(m, 6, axis=-1)]

def modulate(h, shift, scale):
    return h * (1.0 + scale) + shift

def sincos_2d(n_tokens):
    rows = n_tokens // GRID_W
    r = jnp.repeat(jnp.arange(rows, dtype=F32), GRID_W)
    col = jnp.tile(jnp.arange(GRID_W, dtype=F32), rows)
    quarter = D_MODEL // 4
    omega = 1.0 / (10000.0 ** (jnp.arange(quarter, dtype=F32) / quarter))

    def axis_emb(pos):
        a = pos[:, None] * omega[None, :]
        return jnp.concatenate([jnp.sin(a), jnp.cos(a)], axis=-1)

    return jnp.concatenate([axis_emb(r), axis_emb(col)], axis=-1)

def lower_bounds(lb_param):
    p = jax.nn.softmax(lb_param.astype(F32), axis=0)
    return jnp.cumsum(p, axis=0)[:DEPTH]

def heads(t, d):
    B, L, _ = t.shape
    return t.reshape(B, L, HG_HEADS, d).transpose(0, 2, 1, 3)

def flip(t):
    return jnp.flip(t, axis=2)

def hgrn2_keys(z, lb):
    z = z.astype(F32)
    log_f = jnp.log(lb + (1.0 - lb) * jax.nn.sigmoid(z))
    k = (1.0 - lb) * jax.nn.sigmoid(-z)
    return heads(k, HG_DK), heads(log_f, HG_DK)

def gla_chunk_scan(q, k, v, log_f, s0):
    B, H, L, DK = q.shape
    DV = v.shape[-1]
    n = L // CHUNK

    def to_chunks(t):
        return t.reshape(B, H, n, CHUNK, t.shape[-1]).transpose(2, 0, 1, 3, 4)

    b = to_chunks(lax.cumsum(log_f.reshape(B, H, n, CHUNK, DK), axis=3).reshape(B, H, L, DK))
    mask = jnp.tril(jnp.ones((CHUNK, CHUNK), dtype=bool))
    mid = CHUNK // 2

    def step(S, xs):
        qc, kc, vc, bc = xs
        total = bc[:, :, -1:, :]
        ref = bc[:, :, mid:mid + 1, :]
        scores = jnp.einsum('bhtk,bhsk->bhts', qc * jnp.exp(bc - ref), kc * jnp.exp(ref - bc))
        scores = jnp.where(mask, scores, 0.0)
        o = (jnp.einsum('bhtk,bhkv->bhtv', qc * jnp.exp(bc), S)
             + jnp.einsum('bhts,bhsv->bhtv', scores, vc))
        S_new = (jnp.exp(total[:, :, 0, :])[..., None] * S
                 + jnp.einsum('bhsk,bhsv->bhkv', kc * jnp.exp(total - bc), vc))
        return S_new, o

    s_fin, o = lax.scan(step, s0, (to_chunks(q), to_chunks(k), to_chunks(v), b))
    return o.transpose(1, 2, 0, 3, 4).reshape(B, H, L, DV), s_fin

def gla_final_state(k, v, log_f):
    decay = jnp.exp(lax.cumsum(log_f, axis=2, reverse=True) - log_f)
    return jnp.einsum('bhlk,bhlv->bhkv', k * decay, v)

def hgrn2_bidir(q, v, fwd, bwd, s0_f, s0_b):
    o_f, s_f = gla_chunk_scan(q, fwd[0], v, fwd[1], s0_f)
    o_b, s_b = gla_chunk_scan(flip(q), flip(bwd[0]), flip(v), flip(bwd[1]), s0_b)
    return o_f + flip(o_b), s_f, s_b

def hgrn2_readout(o, g, norm_g, dtype):
    o = o * lax.rsqrt(jnp.mean(o * o, axis=-1, keepdims=True) + EPS) * norm_g.astype(F32)
    B, H, L, DV = o.shape
    o = o.transpose(0, 2, 1, 3).reshape(B, L, H * DV)
    return (o * jax.nn.silu(g.astype(F32))).astype(dtype)

def short_conv3(u, w, b):
    up = jnp.pad(u, ((0, 0), (1, 1), (0, 0)))
    return up[:, :-2] * w[0] + up[:, 1:-1] * w[1] + up[:, 2:] * w[2] + b

def hyena_filters(L, w1, b1, fr1, w2, b2, fr2, w3):
    t = jnp.linspace(0.0, 1.0, L, dtype=F32)[:, None]
    bands = (HY_EMB - 1) // 2
    ang = (2.0 * math.pi * jnp.arange(L, dtype=F32) / L)[:, None] * \
        jnp.linspace(1e-4, bands - 1, bands, dtype=F32)[None, :]
    z = jnp.concatenate([t, jnp.cos(ang), -jnp.sin(ang)], axis=-1)
    h = jnp.sin(fr1.astype(F32) * (z @ w1.astype(F32) + b1.astype(F32)))
    h = jnp.sin(fr2.astype(F32) * (h @ w2.astype(F32) + b2.astype(F32)))
    h = h @ w3.astype(F32)
    deltas = jnp.abs(jnp.linspace(math.log(HY_DECAY_TARGET) / HY_SLOW_PCT,
                                  math.log(HY_DECAY_TARGET) / HY_FAST_PCT, HY_WIDTH, dtype=F32))
    h = h.reshape(L, 2, HY_WIDTH) * jnp.exp(-t * deltas)[:, None, :]
    return h[:, 0], h[:, 1]

def long_conv_bidir(u, h_fwd, h_bwd, d_skip):
    B, L, C = u.shape
    kern = jnp.concatenate([h_fwd, jnp.zeros((1, C), F32), jnp.flip(h_bwd[1:], axis=0)], axis=0)
    y = jnp.fft.irfft(jnp.fft.rfft(u, n=2 * L, axis=1) * jnp.fft.rfft(kern, axis=0)[None],
                      n=2 * L, axis=1)[:, :L]
    return y + u * d_skip

def hyena_branch(p_hy, conv_w, conv_b, filt, d_skip):
    L = p_hy.shape[1]
    u = short_conv3(p_hy, conv_w, conv_b).astype(F32)
    v, x1, x0 = jnp.split(u, 3, axis=-1)
    h_fwd, h_bwd = hyena_filters(L, *filt)
    y = x0 * long_conv_bidir(v * x1, h_fwd, h_bwd, d_skip.astype(F32))
    return y.astype(p_hy.dtype)

def merge_branches(y_a, y_b, g_logits, w_pa, w_pb, w_o):
    g_a, g_b = jnp.split(g_logits, 2, axis=-1)
    mixed = jax.nn.sigmoid(g_a) * (y_a @ w_pa) + jax.nn.sigmoid(g_b) * (y_b @ w_pb)
    return mixed @ w_o

def token_mixer(p, lb, s0_f, s0_b, hg_norm_g, conv_w, conv_b, filt, d_skip, w_pa, w_pb, w_o):
    q, z_f, z_b, vi, g, p_hy, g_logits = jnp.split(p, SPLIT_POINTS, axis=-1)
    fwd = hgrn2_keys(z_f, lb[0])
    bwd = hgrn2_keys(z_b, lb[1])
    o, s_f, s_b = hgrn2_bidir(heads(q.astype(F32), HG_DK), heads(vi.astype(F32), HG_DV),
                              fwd, bwd, s0_f, s0_b)
    y_a = hgrn2_readout(o, g, hg_norm_g, p.dtype)
    y_b = hyena_branch(p_hy, conv_w, conv_b, filt, d_skip)
    return merge_branches(y_a, y_b, g_logits, w_pa, w_pb, w_o), s_f, s_b

def context_states(p_c, lb):
    z_f, z_b, vi = jnp.split(p_c, (HG_KDIM, 2 * HG_KDIM), axis=-1)
    kf, lf = hgrn2_keys(z_f, lb[0])
    kb, lb_ = hgrn2_keys(z_b, lb[1])
    v = heads(vi.astype(F32), HG_DV)
    return gla_final_state(kf, v, lf), gla_final_state(flip(kb), flip(v), flip(lb_))

def hier_moe(h, wg, bg, we, be, w_gate, w_up, w_down):
    B, L, D = h.shape
    t = h.reshape(B * L, D)
    p_group = jax.nn.softmax((t @ wg + bg).astype(F32), axis=-1)
    p_top_g, g_idx = lax.top_k(p_group, 1)
    e_logits = (jnp.einsum('td,gde->tge', t, we) + be).astype(F32)
    e_logits = jnp.take_along_axis(e_logits, g_idx[:, :, None], axis=1)[:, 0]
    p_top_e, e_idx = lax.top_k(jax.nn.softmax(e_logits, axis=-1), TOP_K)
    w_sel = p_top_g * p_top_e / jnp.sum(p_top_e, axis=-1, keepdims=True)
    combine = (jnp.einsum('tk,tke->te', w_sel, jax.nn.one_hot(e_idx, EXPERTS_PER_GROUP, dtype=F32))[:, None, :]
               * jax.nn.one_hot(g_idx[:, 0], N_GROUPS, dtype=F32)[:, :, None])
    out = jnp.zeros((B * L, D), F32)
    for gi in range(N_GROUPS):
        hid = (jax.nn.silu(jnp.einsum('td,edf->tef', t, w_gate[gi]))
               * jnp.einsum('td,edf->tef', t, w_up[gi])
               * combine[:, gi, :, None].astype(t.dtype))
        out = out + jnp.einsum('tef,efd->td', hid, w_down[gi])
    return out.reshape(B, L, D).astype(h.dtype)

def first_inputs(seed: int = 0) -> dict:
    key = jax.random.key(seed)
    ks = jax.random.split(key, 32)

    def nrm(k, shape, scale):
        return scale * jax.random.normal(k, shape, F32)

    G, E, F = N_GROUPS, EXPERTS_PER_GROUP, D_EXPERT
    return {
        "x": nrm(ks[0], (BATCH, SEQ, D_MODEL), 1.0),
        "c": nrm(ks[1], (BATCH, D_MODEL), 1.0),
        "ctx": nrm(ks[2], (BATCH, CTX_LEN, D_MODEL), 1.0),
        "c_ctx": nrm(ks[3], (D_MODEL,), 1.0),
        "ada_w": nrm(ks[4], (DEPTH, D_MODEL, 6 * D_MODEL), 0.5 * D_MODEL ** -0.5),
        "ada_b": nrm(ks[5], (DEPTH, 6 * D_MODEL), 0.02),
        "norm1_g": 1.0 + nrm(ks[6], (DEPTH, D_MODEL), 0.05),
        "norm2_g": 1.0 + nrm(ks[7], (DEPTH, D_MODEL), 0.05),
        "w_in": nrm(ks[8], (DEPTH, D_MODEL, IN_WIDTH), D_MODEL ** -0.5),
        "hgrn_lb": nrm(ks[9], (DEPTH + 1, 2, HG_KDIM), 0.1),
        "hgrn_norm_g": 1.0 + nrm(ks[10], (DEPTH, HG_DV), 0.05),
        "hy_conv_w": nrm(ks[11], (DEPTH, HY_SHORT, 3 * HY_WIDTH), HY_SHORT ** -0.5),
        "hy_conv_b": nrm(ks[12], (DEPTH, 3 * HY_WIDTH), 0.02),
        "hy_filt_w1": nrm(ks[13], (DEPTH, HY_EMB, HY_FILTER_HIDDEN), HY_EMB ** -0.5),
        "hy_filt_b1": nrm(ks[14], (DEPTH, HY_FILTER_HIDDEN), 0.1),
        "hy_filt_freq1": 1.0 + nrm(ks[15], (DEPTH, HY_FILTER_HIDDEN), 0.1),
        "hy_filt_w2": nrm(ks[16], (DEPTH, HY_FILTER_HIDDEN, HY_FILTER_HIDDEN), HY_FILTER_HIDDEN ** -0.5),
        "hy_filt_b2": nrm(ks[17], (DEPTH, HY_FILTER_HIDDEN), 0.1),
        "hy_filt_freq2": 1.0 + nrm(ks[18], (DEPTH, HY_FILTER_HIDDEN), 0.1),
        "hy_filt_w3": nrm(ks[19], (DEPTH, HY_FILTER_HIDDEN, 2 * HY_WIDTH), HY_FILTER_SCALE * HY_FILTER_HIDDEN ** -0.5),
        "hy_d": nrm(ks[20], (DEPTH, HY_WIDTH), 0.1),
        "w_proj_a": nrm(ks[21], (DEPTH, HG_WIDTH, D_MODEL), HG_WIDTH ** -0.5),
        "w_proj_b": nrm(ks[22], (DEPTH, HY_WIDTH, D_MODEL), HY_WIDTH ** -0.5),
        "w_out": nrm(ks[23], (DEPTH, D_MODEL, D_MODEL), D_MODEL ** -0.5),
        "moe_router_g_w": nrm(ks[24], (DEPTH, D_MODEL, G), D_MODEL ** -0.5),
        "moe_router_g_b": nrm(ks[25], (DEPTH, G), 0.01),
        "moe_router_e_w": nrm(ks[26], (DEPTH, G, D_MODEL, E), D_MODEL ** -0.5),
        "moe_router_e_b": nrm(ks[27], (DEPTH, G, E), 0.01),
        "moe_w_gate": nrm(ks[28], (DEPTH, G, E, D_MODEL, F), D_MODEL ** -0.5),
        "moe_w_up": nrm(ks[29], (DEPTH, G, E, D_MODEL, F), D_MODEL ** -0.5),
        "moe_w_down": nrm(ks[30], (DEPTH, G, E, F, D_MODEL), F ** -0.5),
        "final_norm_g": 1.0 + nrm(ks[31], (D_MODEL,), 0.05),
    }

def first_block(x, c, ctx, c_ctx, ada_w, ada_b, norm1_g, norm2_g, w_in, hgrn_lb, hgrn_norm_g,
              hy_conv_w, hy_conv_b, hy_filt_w1, hy_filt_b1, hy_filt_freq1, hy_filt_w2, hy_filt_b2,
              hy_filt_freq2, hy_filt_w3, hy_d, w_proj_a, w_proj_b, w_out, moe_router_g_w,
              moe_router_g_b, moe_router_e_w, moe_router_e_b, moe_w_gate, moe_w_up, moe_w_down,
              final_norm_g):
    B = x.shape[0]
    x = x + sincos_2d(x.shape[1]).astype(x.dtype)
    lbs = lower_bounds(hgrn_lb)
    zero_state = jnp.zeros((B, HG_HEADS, HG_DK, HG_DV), F32)
    for l in range(DEPTH):
        last = l == DEPTH - 1
        sh1, sc1, gt1, sh2, sc2, gt2 = adaln(c, ada_w[l], ada_b[l])
        csh1, csc1, cgt1, csh2, csc2, cgt2 = adaln(c_ctx, ada_w[l], ada_b[l])
        filt = (hy_filt_w1[l], hy_filt_b1[l], hy_filt_freq1[l], hy_filt_w2[l], hy_filt_b2[l],
                hy_filt_freq2[l], hy_filt_w3[l])
        mix_args = (hgrn_norm_g[l], hy_conv_w[l], hy_conv_b[l], filt, hy_d[l],
                    w_proj_a[l], w_proj_b[l], w_out[l])
        hc = modulate(rms_norm(ctx, norm1_g[l]), csh1, csc1)
        if last:
            s_f, s_b = context_states(hc @ w_in[l][:, HG_KDIM:3 * HG_KDIM + HG_WIDTH], lbs[l])
        else:
            ctx_mix, s_f, s_b = token_mixer(hc @ w_in[l], lbs[l], zero_state, zero_state, *mix_args)
        hx = modulate(rms_norm(x, norm1_g[l]), sh1, sc1)
        x_mix, _, _ = token_mixer(hx @ w_in[l], lbs[l], s_f, s_b, *mix_args)
        x = x + gt1 * x_mix
        moe_args = (moe_router_g_w[l], moe_router_g_b[l], moe_router_e_w[l], moe_router_e_b[l],
                    moe_w_gate[l], moe_w_up[l], moe_w_down[l])
        x = x + gt2 * hier_moe(modulate(rms_norm(x, norm2_g[l]), sh2, sc2), *moe_args)
        if not last:
            ctx = ctx + cgt1 * ctx_mix
            ctx = ctx + cgt2 * hier_moe(modulate(rms_norm(ctx, norm2_g[l]), csh2, csc2), *moe_args)
    return rms_norm(x, final_norm_g)


DEPTH_2 = 2

N_RET_HEADS = 4
RET_HEAD_DIM = 128
N_GLA_HEADS = 4
GLA_KEY_DIM = 64
GLA_VAL_DIM = 128
GLA_GATE_RANK = 16
GLA_GATE_NORM = 16.0
D_FF = 4 * D_MODEL
CHUNK_2 = 64
ROPE_BASE = 10000.0
LN2 = 0.6931471805599453

RET_W = N_RET_HEADS * RET_HEAD_DIM
GLA_K = N_GLA_HEADS * GLA_KEY_DIM
GLA_V = N_GLA_HEADS * GLA_VAL_DIM
MIX_W = RET_W + GLA_V
IN_SPLITS = (RET_W, RET_W, RET_W, RET_W, GLA_K, GLA_K, GLA_V, GLA_V, GLA_GATE_RANK, GLA_GATE_RANK)
IN_W = 4 * RET_W + 2 * GLA_K + 2 * GLA_V + 2 * GLA_GATE_RANK


def rmsnorm(x, g):
    xf = x.astype(jnp.float32)
    y = xf * lax.rsqrt(jnp.mean(xf * xf, axis=-1, keepdims=True) + EPS)
    return (y * g.astype(jnp.float32)).astype(x.dtype)

def head_layernorm(o):
    of = o.astype(jnp.float32)
    mu = jnp.mean(of, axis=-1, keepdims=True)
    var = jnp.mean(jnp.square(of - mu), axis=-1, keepdims=True)
    return ((of - mu) * lax.rsqrt(var + EPS)).astype(o.dtype)

def modulate_2(h, shift, scale):
    return h * (1.0 + scale) + shift

def to_heads(t, n_heads):
    b, l, _ = t.shape
    return t.reshape(b, l, n_heads, -1).transpose(0, 2, 1, 3)

def from_heads(t):
    b, h, l, d = t.shape
    return t.transpose(0, 2, 1, 3).reshape(b, l, h * d)

def grid_positions(n_rows):
    row = jnp.repeat(jnp.arange(n_rows), GRID_W).astype(jnp.float32)
    col = jnp.tile(jnp.arange(GRID_W), n_rows).astype(jnp.float32)
    return row, col

def rotary_2d(t, row_pos, col_pos):
    d = t.shape[-1]
    half = d // 2
    nf = half // 2
    inv = ROPE_BASE ** (-jnp.arange(nf, dtype=jnp.float32) / nf)

    def rot(u, p):
        ang = p[:, None] * inv[None, :]
        cos, sin = jnp.cos(ang), jnp.sin(ang)
        u1, u2 = u[..., :nf], u[..., nf:]
        return jnp.concatenate([u1 * cos - u2 * sin, u1 * sin + u2 * cos], axis=-1)

    tf = t.astype(jnp.float32)
    out = jnp.concatenate([rot(tf[..., :half], row_pos), rot(tf[..., half:], col_pos)], axis=-1)
    return out.astype(t.dtype)

def chunked_gated_linear_attention(q, k, v, log_a, s0, strict):
    b_, h_, l_, _ = q.shape
    dv = v.shape[-1]
    n_chunks = l_ // CHUNK_2
    f32 = jnp.float32

    def blocks(t):
        return t.astype(f32).reshape(b_, h_, n_chunks, CHUNK_2, t.shape[-1]).transpose(2, 0, 1, 3, 4)

    qs, ks, vs, gs = blocks(q), blocks(k), blocks(v), blocks(log_a)
    mask = jnp.tril(jnp.ones((CHUNK_2, CHUNK_2), dtype=bool), -1 if strict else 0)

    def step(s, blk):
        qc, kc, vc, gc = blk
        cum = jnp.cumsum(gc, axis=-2)
        cum_last = cum[..., -1:, :]
        q_dec = qc * jnp.exp(cum)
        k_inv = kc * jnp.exp(-cum)
        k_end = kc * jnp.exp(cum_last - cum)
        scores = jnp.where(mask, jnp.einsum('bhtd,bhsd->bhts', q_dec, k_inv), 0.0)
        o = jnp.einsum('bhts,bhsv->bhtv', scores, vc) + jnp.einsum('bhtd,bhdv->bhtv', q_dec, s)
        s_new = jnp.exp(cum_last[..., 0, :])[..., :, None] * s + jnp.einsum('bhsd,bhsv->bhdv', k_end, vc)
        return s_new, o

    s_fin, o = lax.scan(step, s0.astype(f32), (qs, ks, vs, gs))
    o = o.transpose(1, 2, 0, 3, 4).reshape(b_, h_, l_, dv)
    return o.astype(v.dtype), s_fin

def bidirectional_scan(lat_in, ctx_in):
    q, k, v, a_f, a_b = lat_in
    cq, ck, cv, ca_f, ca_b = ctx_in
    b_, h_, _, dk = q.shape
    dv = v.shape[-1]
    zero = jnp.zeros((b_, h_, dk, dv), jnp.float32)

    def flip(t):
        return jnp.flip(t, axis=2)

    c_f, s_f = chunked_gated_linear_attention(cq, ck, cv, ca_f, zero, False)
    x_f, _ = chunked_gated_linear_attention(q, k, v, a_f, s_f, False)
    c_b, s_b = chunked_gated_linear_attention(flip(cq), flip(ck), flip(cv), flip(ca_b), zero, True)
    x_b, _ = chunked_gated_linear_attention(flip(q), flip(k), flip(v), flip(a_b), s_b, True)
    return x_f + flip(x_b), c_f + flip(c_b)

def project_in(h, w_in):
    offsets = np.cumsum(np.array(IN_SPLITS))[:-1].tolist()
    return jnp.split(h @ w_in, offsets, axis=-1)

def gla_log_gate(d, up, ub):
    return jax.nn.log_sigmoid((d @ up + ub).astype(jnp.float32)) / GLA_GATE_NORM

def hybrid_mixer(h, hc, w_in, ret_decay, gate_up, gate_b, gla_norm_g, row_pos, col_pos, need_ctx):
    lat = project_in(h, w_in)
    cx = project_in(hc, w_in)
    log_gamma = jnp.log1p(-jnp.exp(ret_decay.astype(jnp.float32)))

    def retention_inputs(parts, rotate):
        q = to_heads(parts[0], N_RET_HEADS) * (RET_HEAD_DIM ** -0.5)
        k = to_heads(parts[1], N_RET_HEADS)
        if rotate:
            q = rotary_2d(q, row_pos, col_pos)
            k = rotary_2d(k, row_pos, col_pos)
        v = to_heads(parts[2], N_RET_HEADS)
        shape = q.shape[:3] + (1,)
        a_f = jnp.broadcast_to(log_gamma[0][None, :, None, None], shape)
        a_b = jnp.broadcast_to(log_gamma[1][None, :, None, None], shape)
        return q, k, v, a_f, a_b

    def gla_inputs(parts):
        q = to_heads(parts[4], N_GLA_HEADS) * (GLA_KEY_DIM ** -0.5)
        k = to_heads(parts[5], N_GLA_HEADS)
        v = to_heads(parts[6], N_GLA_HEADS)
        a_f = to_heads(gla_log_gate(parts[8], gate_up[0], gate_b[0]), N_GLA_HEADS)
        a_b = to_heads(gla_log_gate(parts[9], gate_up[1], gate_b[1]), N_GLA_HEADS)
        return q, k, v, a_f, a_b

    r_lat, r_ctx = bidirectional_scan(retention_inputs(lat, True), retention_inputs(cx, False))
    g_lat, g_ctx = bidirectional_scan(gla_inputs(lat), gla_inputs(cx))

    def merge(r, g, parts):
        ret = from_heads(head_layernorm(r)) * jax.nn.silu(parts[3])
        gla = from_heads(rmsnorm(g, gla_norm_g)) * jax.nn.silu(parts[7])
        return jnp.concatenate([ret, gla], axis=-1)

    y_lat = merge(r_lat, g_lat, lat)
    y_ctx = merge(r_ctx, g_ctx, cx) if need_ctx else None
    return y_lat, y_ctx

def squared_relu_mlp(h, w1, w2):
    return jnp.square(jax.nn.relu(h @ w1)) @ w2

def second_inputs(seed: int = 0) -> dict:
    key = jax.random.key(seed)
    ks = jax.random.split(key, 17)
    f32 = jnp.float32

    def nrm(k, shape, s):
        return jax.random.normal(k, shape, f32) * s

    heads = jnp.arange(N_RET_HEADS, dtype=f32)
    base = jnp.stack([-(5.0 + heads) * LN2, -(5.5 + heads) * LN2], axis=0)
    ret_decay = base[None] + nrm(ks[8], (DEPTH_2, 2, N_RET_HEADS), 0.01)
    return {
        'x': nrm(ks[0], (BATCH, SEQ, D_MODEL), 1.0),
        'c': nrm(ks[1], (BATCH, D_MODEL), 1.0),
        'ctx': nrm(ks[2], (BATCH, CTX_LEN, D_MODEL), 1.0),
        'c_ctx': nrm(ks[3], (D_MODEL,), 1.0),
        'ada_w': nrm(ks[4], (DEPTH_2, D_MODEL, 6 * D_MODEL), 0.5 * D_MODEL ** -0.5),
        'ada_b': nrm(ks[5], (DEPTH_2, 6 * D_MODEL), 0.02),
        'norm1_g': 1.0 + nrm(ks[6], (DEPTH_2, D_MODEL), 0.02),
        'w_in': nrm(ks[7], (DEPTH_2, D_MODEL, IN_W), D_MODEL ** -0.5),
        'ret_decay': ret_decay,
        'gla_gate_up': nrm(ks[9], (DEPTH_2, 2, GLA_GATE_RANK, GLA_K), GLA_GATE_RANK ** -0.5),
        'gla_gate_b': nrm(ks[10], (DEPTH_2, 2, GLA_K), 0.1),
        'gla_norm_g': 1.0 + nrm(ks[11], (DEPTH_2, GLA_VAL_DIM), 0.02),
        'w_out': nrm(ks[12], (DEPTH_2, MIX_W, D_MODEL), MIX_W ** -0.5),
        'norm2_g': 1.0 + nrm(ks[13], (DEPTH_2, D_MODEL), 0.02),
        'w_mlp1': nrm(ks[14], (DEPTH_2, D_MODEL, D_FF), D_MODEL ** -0.5),
        'w_mlp2': nrm(ks[15], (DEPTH_2, D_FF, D_MODEL), D_FF ** -0.5),
        'final_g': 1.0 + nrm(ks[16], (D_MODEL,), 0.02),
    }

def second_block(x, c, ctx, c_ctx, ada_w, ada_b, norm1_g, w_in, ret_decay, gla_gate_up, gla_gate_b,
              gla_norm_g, w_out, norm2_g, w_mlp1, w_mlp2, final_g):
    n_rows = x.shape[1] // GRID_W
    row_pos, col_pos = grid_positions(n_rows)
    silu_c = jax.nn.silu(c)
    silu_cc = jax.nn.silu(c_ctx)
    for layer in range(DEPTH_2):
        need_ctx = layer < DEPTH_2 - 1
        mod_x = silu_c @ ada_w[layer] + ada_b[layer]
        mod_c = silu_cc @ ada_w[layer] + ada_b[layer]
        sh1, sc1, g1, sh2, sc2, g2 = [m[:, None, :] for m in jnp.split(mod_x, 6, axis=-1)]
        csh1, csc1, cg1, csh2, csc2, cg2 = jnp.split(mod_c, 6, axis=-1)

        hx = modulate_2(rmsnorm(x, norm1_g[layer]), sh1, sc1)
        hc = modulate_2(rmsnorm(ctx, norm1_g[layer]), csh1, csc1)
        mx, mc = hybrid_mixer(hx, hc, w_in[layer], ret_decay[layer], gla_gate_up[layer], gla_gate_b[layer],
                              gla_norm_g[layer], row_pos, col_pos, need_ctx)
        x = x + g1 * (mx @ w_out[layer])
        hx = modulate_2(rmsnorm(x, norm2_g[layer]), sh2, sc2)
        x = x + g2 * squared_relu_mlp(hx, w_mlp1[layer], w_mlp2[layer])

        if need_ctx:
            ctx = ctx + cg1 * (mc @ w_out[layer])
            hc = modulate_2(rmsnorm(ctx, norm2_g[layer]), csh2, csc2)
            ctx = ctx + cg2 * squared_relu_mlp(hc, w_mlp1[layer], w_mlp2[layer])
    return rmsnorm(x, final_g)


def setup_inputs(seed=0):
    out = dict(first_inputs(seed))
    for name, value in second_inputs(seed + 1).items():
        if name != "x":
            out[name + "_2"] = value
    return out


def reference(
    x, c, ctx, c_ctx, ada_w, ada_b, norm1_g, norm2_g, w_in, hgrn_lb, hgrn_norm_g, hy_conv_w,
    hy_conv_b, hy_filt_w1, hy_filt_b1, hy_filt_freq1, hy_filt_w2, hy_filt_b2, hy_filt_freq2,
    hy_filt_w3, hy_d, w_proj_a, w_proj_b, w_out, moe_router_g_w, moe_router_g_b, moe_router_e_w,
    moe_router_e_b, moe_w_gate, moe_w_up, moe_w_down, final_norm_g, c_2, ctx_2, c_ctx_2,
    ada_w_2, ada_b_2, norm1_g_2, w_in_2, ret_decay_2, gla_gate_up_2, gla_gate_b_2, gla_norm_g_2,
    w_out_2, norm2_g_2, w_mlp1_2, w_mlp2_2, final_g_2,
):
    x = first_block(
        x, c, ctx, c_ctx, ada_w, ada_b, norm1_g, norm2_g, w_in, hgrn_lb, hgrn_norm_g, hy_conv_w,
        hy_conv_b, hy_filt_w1, hy_filt_b1, hy_filt_freq1, hy_filt_w2, hy_filt_b2, hy_filt_freq2,
        hy_filt_w3, hy_d, w_proj_a, w_proj_b, w_out, moe_router_g_w, moe_router_g_b,
        moe_router_e_w, moe_router_e_b, moe_w_gate, moe_w_up, moe_w_down, final_norm_g,
    )
    return second_block(
        x, c_2, ctx_2, c_ctx_2, ada_w_2, ada_b_2, norm1_g_2, w_in_2, ret_decay_2, gla_gate_up_2,
        gla_gate_b_2, gla_norm_g_2, w_out_2, norm2_g_2, w_mlp1_2, w_mlp2_2, final_g_2,
    )


_drawn_inputs = setup_inputs


def setup_inputs(seed=0):
    import zlib

    import numpy as np

    out = dict(_drawn_inputs(seed))
    spreads = {}
    factors = {'ctx': 8.0,
     'c_ctx': 8.0,
     'ada_b': 3.046,
     'norm1_g': 3.208,
     'hgrn_lb': 4.907,
     'hgrn_norm_g': 6.71,
     'hy_conv_b': 8.0,
     'hy_filt_b1': 3.816,
     'hy_filt_freq1': 5.273,
     'hy_filt_freq2': 6.138,
     'moe_router_g_b': 28.287,
     'moe_router_e_b': 24.729,
     'norm1_g_2': 4.085,
     'gla_gate_b_2': 3.722,
     'gla_norm_g_2': 8.0,
     'norm2_g_2': 4.344,
     'final_g_2': 2.712,
     'norm2_g': 2.979}
    for name, (base, spread) in spreads.items():
        noise = np.random.default_rng([zlib.crc32(name.encode()), seed]).standard_normal(out[name].shape)
        drawn = base * np.exp(spread * noise) if base else spread * noise
        out[name] = jnp.asarray(drawn.astype(out[name].dtype))
    for name, factor in factors.items():
        out[name] = (out[name] * factor).astype(out[name].dtype)
    return out
```

```python
from contextlib import ExitStack

import numpy as np
import concourse.bass as bass
from concourse import mybir

F32 = mybir.dt.float32
F32R = mybir.dt.float32r
I32 = mybir.dt.int32
ALU = mybir.AluOpType
ACT = mybir.ActivationFunctionType
AX = mybir.AxisListType

P = 128
D = 1024
KT = D // P
L = 256
TB = L // P
EPS = 1e-6
GRID_W = 64
HG_H, HG_D, HG_C = 4, 128, 32
HY = 512
HYT = HY // P
NG, NE, FE = 4, 8, 512
NX = NG * NE
FT = FE // P
CAP = 64
NR = NG + NX
RT_H = 4
GL_H, GL_K = 4, 64
GL_T = GL_H * GL_K // P
RANK = 16
DFF = 4 * D
LAYERS = 2
IN2 = 3616
RING = 4

VEC = [("ada_b", 48), ("n1", 8), ("n2", 8), ("lb", 16), ("hg_g", 1), ("conv_w", 36), ("conv_b", 12),
       ("hy_d", 4), ("fin", 8), ("ada_b2", 96), ("n1_2", 16), ("n2_2", 16), ("gla_g", 2), ("gate_b", 8),
       ("fin2", 8), ("c1", 16), ("c2", 16), ("decay", 16), ("rbias", NR), ("eps", 1), ("one", 1),
       ("f1", 2), ("f2", 2)]
VOFF = {}
_n = 0
for _name, _w in VEC:
    VOFF[_name] = (_n, _n + _w)
    _n += _w
NVEC = _n


def columns(a):
    a = np.asarray(a)
    return np.ascontiguousarray(a.reshape(-1, P).T)


def tables():
    f = np.float32
    t = {}
    rows = L // GRID_W
    r = np.repeat(np.arange(rows, dtype=f), GRID_W)
    col = np.tile(np.arange(GRID_W, dtype=f), rows)
    quarter = D // 4
    omega = (f(1.0) / np.power(f(10000.0), np.arange(quarter, dtype=f) / f(quarter))).astype(f)

    def axis_emb(pos):
        a = (pos[:, None] * omega[None, :]).astype(f)
        return np.concatenate([np.sin(a), np.cos(a)], axis=-1)

    pos = np.concatenate([axis_emb(r), axis_emb(col)], axis=-1).astype(f)
    t["pos"] = np.ascontiguousarray(pos.T)
    i = np.arange(P)
    ident = np.eye(P, dtype=f)
    ones = np.ones((P, P), f)
    tok = np.arange(L)
    r32f = np.broadcast_to((tok % HG_C != 0).astype(f), (P, L))
    r32b = np.broadcast_to((tok % HG_C != HG_C - 1).astype(f), (P, L))
    t["base"] = np.ascontiguousarray(np.concatenate([ident, ones, r32f, r32b], axis=1))
    same = (i[:, None] // HG_C) == (i[None, :] // HG_C)
    t["hg_mask"] = np.ascontiguousarray(np.concatenate(
        [same & (i[:, None] <= i[None, :]), same & (i[:, None] >= i[None, :])], axis=1).astype(np.int32))
    t["moe"] = np.ascontiguousarray(np.concatenate(
        [(i[:, None] < i[None, :]).astype(f), np.broadcast_to(np.arange(CAP, dtype=f), (P, CAP))], axis=1))
    lin = np.linspace(0.0, 1.0, L, dtype=f)[:, None]
    bands = 16
    ang = (f(2.0 * np.pi) * np.arange(L, dtype=f) / f(L))[:, None] * np.linspace(1e-4, bands - 1, bands, dtype=f)[None]
    z = np.concatenate([lin, np.cos(ang), -np.sin(ang)], axis=-1).astype(f)
    t["hy_z"] = np.ascontiguousarray(z.T)
    deltas = np.abs(np.linspace(np.log(1e-2) / 1.5, np.log(1e-2) / 0.3, HY, dtype=f))
    dec = np.exp(-lin * deltas[None, :]).astype(f)
    two = lambda a: a.reshape(2, P, -1).transpose(1, 0, 2).reshape(P, -1)
    th = 2 * np.pi * ((np.arange(L)[:, None] * np.arange(L)[None, :]) % (2 * L)) / (2 * L)
    fw = np.concatenate([np.cos(th), -np.sin(th)], axis=1)
    fw[:, L] = np.cos(np.pi * np.arange(L))
    bw = np.concatenate([np.cos(th), np.sin(th)], axis=1)
    bw[:, L] = np.cos(np.pi * np.arange(L))
    bw[0] = 0.0
    inv = fw.T * (2.0 / (2 * L))
    inv[0] *= 0.5
    inv[L] *= 0.5
    four = inv.reshape(4, P, L).transpose(1, 0, 2).reshape(P, -1)
    t["hy"] = np.ascontiguousarray(np.concatenate([two(fw), four, two(bw), two(dec)], axis=1).astype(f))
    perm = np.zeros((P, P), f)
    perm[i ^ 32, i] = 1.0
    nf = 32
    invf = np.power(f(10000.0), -np.arange(nf, dtype=f) / f(nf)).astype(f)
    half = np.concatenate([invf, invf])
    angs = np.concatenate([half[:, None] * r[None, :], half[:, None] * col[None, :]], axis=0).astype(f)
    sign = np.where((i // 32) % 2 == 0, -1.0, 1.0)[:, None]
    s2 = np.arange(L)
    ef = np.maximum(s2[None, :] - s2[:, None], 0)
    eb = np.maximum(s2[:, None] - s2[None, :], 0)
    t2 = np.arange(2 * L)
    r128f = np.broadcast_to((t2 % P != 0), (P, 2 * L))
    r128b = np.broadcast_to((t2 % P != P - 1), (P, 2 * L))
    rowf = np.broadcast_to(s2 + 1, (P, L))
    rowb = np.broadcast_to(L - s2, (P, L))
    colf = (L - 1 - s2).reshape(2, P).T
    colb = s2.reshape(2, P).T
    t["b2"] = np.ascontiguousarray(np.concatenate(
        [perm, np.cos(angs), np.sin(angs) * sign, two(ef), two(eb), r128f, r128b, rowf, rowb, colf, colb],
        axis=1).astype(f))
    t["b2_mask"] = np.ascontiguousarray(np.concatenate(
        [i[:, None] <= i[None, :], i[:, None] > i[None, :]], axis=1).astype(np.int32))
    return t


def build(nc, T, out):
    ctx = ExitStack()
    with ctx:
        def sb(name, shape, dt=F32):
            return ctx.enter_context(nc.sbuf_tensor(name, shape, dt))

        sems = {}

        def S(name):
            if name not in sems:
                sems[name] = ctx.enter_context(nc.semaphore(name))
            return sems[name]

        X = sb("X", [P, KT, 2 * L])
        base = sb("base", [P, 2 * P + 2 * L])
        hmask = sb("hmask", [P, 2, P], I32)
        vecs = sb("vecs", [P, NVEC])
        silc = sb("silc", [P, 2, KT, 2])
        mod = sb("mod", [P, 3, 48, 2])
        gsc = sb("gsc", [P, 3, 2, KT, 2])
        RS = sb("RS", [P, 2 * L])
        lbc = sb("lbc", [P, 40])
        npass = sb("npass", [1, 8], I32)
        mrow = [sb("mod_rows", [2, 512])[:, :], RS[0:2, :]]
        et = sb("chunk_decay", [P, 64])
        AR = 25600
        with ExitStack() as once:
            def shared(name, shape, dt=F32):
                return once.enter_context(nc.sbuf_tensor(name, shape, dt))

            ring = [shared(f"ring{s}", [P, KT * 512]) for s in range(RING)]
            H = shared("H", [P, KT, 2 * L])
            ar = shared("arena", [P, AR])
        ring_r = [sb(f"ring_low{s}", [P, KT * 512], F32R) for s in range(RING)]
        Hl = sb("H_low", [P, KT, 2 * L], F32R)
        ar_r = sb("arena_r", [P, AR], F32R)
        ps = [ctx.enter_context(nc.psum_tensor(f"bank{b}", [P, 512], F32))[:, :] for b in range(8)]
        ident, ones = base[:, 0:P], base[:, P:2 * P]
        r32 = [base[:, 2 * P:2 * P + L], base[:, 2 * P + L:2 * P + 2 * L]]

        full = [ctx.enter_context(nc.semaphore(f"full{s}")) for s in range(RING)]
        used = S("ring_used")
        out_sem = S("out_stored")

        def vec(name, a=0, n=1):
            lo = VOFF[name][0] + a
            return vecs[:, lo:lo + n]

        def A(off, n):
            assert off + n <= AR, (off, n)
            return ar[:, off:off + n]

        def AR3(off, a, b):
            return ar_r[:, off:off + a * b].rearrange("p (a b) -> p a b", a=a)

        def A3(off, a, b):
            return A(off, a * b).rearrange("p (a b) -> p a b", a=a)

        ADA1, WIN, MERGE, MOE = 0, 12, 36, 40
        NMOE = 3 * NX
        L0 = MOE + NMOE
        MLP0 = L0 + 10
        L1 = MLP0 + 32
        MLP1 = L1 + 10
        END = MLP1 + 16
        WIN_ORDER = [1, 0, 3, 2, 4, 5, 6, 7, 8, 9, 10, 11]
        ADA_COLS = 384

        def cols(w, a, n):
            return w[:, bass.ds(a, n)].rearrange("(k p) n -> p k n", p=P)

        def rows(w, a, n):
            return w[bass.ds(a, n), :].rearrange("(k p) n -> p k n", p=P)

        def slot(n):
            return ring[n % RING][:, :]

        def low(n):
            return ring_r[n % RING][:, :]

        def as_cols(n, w=512, slot=slot):
            return slot(n)[:, 0:KT * w].rearrange("p (k n) -> p k n", k=KT)

        def as_rows(n, slot=slot):
            return slot(n).rearrange("p (k n) -> p k n", k=4)

        PHASES = ["filters", "projected", "scan_f", "scan_b", "hyena", "merged", "experts",
                  "l0_in", "l0_ret", "l0_gf", "l0_gb", "l0_out", "l0_mlp", "l1_in", "l1_ret", "l1_gf", "l1_gb", "l1_out", "l1_mlp"]

        block = ctx.enter_context(nc.Block())

        @block.sync
        def _(sp):
            def load(n, src, dst, loop=None):
                if loop is not None or n >= RING:
                    sp.wait_ge(used, (0 if loop is None else loop) + (n - RING + 1))
                sp.dma_start(dst, src).then_inc(full[n % RING], 16)

            for n in range(RING):
                load(n, cols(T["ada_w"], n * 512, 512), as_cols(n))
            with sp.Fori(1, 3) as i:
                for u in range(RING):
                    load(u, cols(T["ada_w"], (i * RING + u) * 512, 512), as_cols(u), i * RING)
            for j in range(12):
                n = WIN + 2 * j
                load(n, cols(T["w_in"], WIN_ORDER[j] * 512, 512), as_cols(n))
                load(n + 1, cols(T["ada_w_2"][0], j * 512, 512), as_cols(n + 1))
            load(MERGE, rows(T["w_proj_a"], 0, 512), as_rows(MERGE))
            load(MERGE + 1, rows(T["w_proj_b"], 0, 512), as_rows(MERGE + 1))
            for j in range(2):
                n = MERGE + 2 + j
                load(n, cols(T["w_out"], j * 512, 512), as_cols(n))
            with sp.Fori(0, NX // 4) as i:
                for u in range(4):
                    for m, (name, view) in enumerate((("moe_w_gate", as_cols), ("moe_w_up", as_cols), ("moe_w_down", as_rows))):
                        n = MOE + 3 * u + m
                        src = T[name][i * 4 + u].rearrange("(k p) n -> p k n", p=P)
                        load(n, src, view(n), i * 12)
            sp.wait_ge(S("passes_known"), 1)
            more = sp.value_load(npass[0:1, 0:1])
            with sp.If(more > 0):
                sp.wait_ge(used, MOE + NMOE)
                with sp.Fori(0, more) as q:
                    with sp.Fori(0, NX) as e:
                        for m, (name, view) in enumerate((("moe_w_gate", as_cols), ("moe_w_up", as_cols), ("moe_w_down", as_rows))):
                            sp.wait_ge(S("over_begun"), q * NX + e + 1)
                            sp.dma_start(view(m), T[name][e].rearrange("(k p) n -> p k n", p=P)).then_inc(S(f"over_w{m}"), 16)
                sp.wait_ge(S("experts_done"), 1)
            for l, first, mlp in ((0, L0, MLP0), (1, L1, MLP1)):
                for j in range(7):
                    load(first + j, cols(T["w_in_2"][l], j * 512, 512), as_cols(first + j))
                load(first + 7, cols(T["w_in_2"][l], 7 * 512, 2 * RANK), as_cols(first + 7, 2 * RANK))
                for j in range(2):
                    load(first + 8 + j, cols(T["w_out_2"][l], j * 512, 512), as_cols(first + 8 + j))
                with sp.Fori(0, 4) as i:
                    n = mlp
                    per = 8 if l == 0 else 4
                    for h in range(2):
                        load(n, cols(T["w_mlp1_2"][l], (i * 2 + h) * 512, 512), as_cols(n), i * per)
                        n += 1
                        if l == 0:
                            for a in range(2):
                                load(n, cols(T["ada_w_2"][1], (i * 4 + h * 2 + a) * ADA_COLS, ADA_COLS), as_cols(n, ADA_COLS), i * per)
                                n += 1
                        src = T["w_mlp2_2"][l].rearrange("(j k p) n -> j p k n", p=P, k=4)[i * 2 + h]
                        load(n, src, as_rows(n), i * per)
                        n += 1
            sp.wait_ge(S("phase"), 4 * len(PHASES))
            sp.dma_start(out.rearrange("(k p) n -> p k n", p=P), X[:, :, 0:L]).then_inc(out_sem, 16)
            sp.wait_ge(out_sem, 16)

        Qt = A3(0, HG_H, L)
        Vn = A3(1024, 4, 512)
        Gt = A3(3072, HG_H, L)
        K2 = [A3(4096 + 4096 * d, HG_H, 2 * L) for d in range(2)]
        L2 = [A3(6144 + 4096 * d, HG_H, 2 * L) for d in range(2)]
        KX, KC = [k[:, :, 0:L] for k in K2], [k[:, :, L:2 * L] for k in K2]
        LX, LC = [k[:, :, 0:L] for k in L2], [k[:, :, L:2 * L] for k in L2]
        HYt = A3(12288, 12, L)
        QM, KM, QD = A3(15360, HG_H, L), A3(16384, HG_H, L), A3(17408, HG_H, L)
        SC = A3(18432, 8, P)
        KEN, KDN = A3(19456, 8, P), A3(20480, 8, P)
        ST = A3(21504, 4, 512)
        KS = A3(23552, 4, 512)
        f_tab, f_dec = A(15360 + 2048, 1024), A3(15360 + 3072, 2, 512)
        f_z, f_w1, f_w2, f_w3 = A(19456, L), A(19712, 64), A(19776, 64), A(19840, 1024)
        f_h1, f_h2, f_t = A(20864, L), A(21120, L), A(21376, L)
        f_fw = A3(15360, 2, 512)
        f_inv0 = A(16384, 1024)
        f_nat = A3(21632, 2, 512)
        OS = A3(0, HG_H, L)
        OSQ = A3(1024, HG_H, L)
        ORS = A3(2048, HG_H, L)
        GL = A3(4096, 16, L)
        CV = A3(8192, 12, L)
        UV = A3(11264, HYT, L)
        UN = A3(17408, 2, 512)
        HFW, HINV = A3(15360, 2, 512), A3(16384, 4, L)
        YF = A3(18432, 4, 512)
        UT = A3(20480, 2, 512)
        UF = A3(21504, 4, 512)
        YB = A3(12288, HYT, L)
        MIX = A3(15360, KT, L)
        MT = A3(17408, KT, L)
        HN = A3(0, TB, D)
        WR = A3(2048, KT, NR)
        mtab = A(2400, P + CAP)
        SLT, IOTA = mtab[:, 0:P], mtab[:, P:P + CAP]
        LG = A3(2600, TB, NR)
        RKM = A3(2700, TB, NX + 4)
        CMB = A3(2800, TB, NX + 4)
        SELX = A3(2900, TB, NX)
        RT = A(3000, 1200)
        SG = A3(4300, 4, CAP)
        SGv = SG.rearrange("p (u b) c -> p u b c", u=2)
        SW = A3(4600, 4, P)
        SWv = SW.rearrange("p (u b) c -> p u b c", u=2)
        HG = A(5200, 512)
        SIL = A3(5712, FT, CAP)
        HID = A3(5968, FT, CAP)
        YS = A(6224, D)
        SWT = A(7248, L)
        RQ, RK = A3(0, 4, 512), A3(2048, 4, 512)
        RV, GV = A3(4096, 4, 512), A3(6144, 4, 512)
        YT = A3(8192, 8, 512)
        GQ, GK = A3(12288, 2, 512), A3(13312, 2, 512)
        DT = A(14336, 512)
        GUP = A3(14848, 2, L)
        b2t = A(15360, 3204)
        PERM, RCOS, RSIN = b2t[:, 0:128], b2t[:, 128:384], b2t[:, 384:640]
        EF, EB = b2t[:, 640:1152].rearrange("p (a b) -> p a b", a=2), b2t[:, 1152:1664].rearrange("p (a b) -> p a b", a=2)
        R128 = [b2t[:, 1664:2176], b2t[:, 2176:2688]]
        ROWT = [b2t[:, 2688:2944], b2t[:, 2944:3200]]
        COLT = b2t[:, 3200:3204]
        gmask = A(18564, 256).bitcast(I32).rearrange("p (a b) -> p a b", a=2)
        lgam = A(18820, 24)
        RB = 18848
        Wd = [A3(RB + 2048 * b, 2, L) for b in range(2)]
        RQD = [A3(RB + 512 + 2048 * b, 2, L) for b in range(2)]
        RVD = [A(RB + 1024 + 2048 * b, 512).rearrange("p (d k v) -> p d k v", d=2, k=2) for b in range(2)]
        RKN = [A3(RB + 1536 + 2048 * b, 2, P) for b in range(2)]
        RST = [A3(RB + 1792 + 2048 * b, 2, P) for b in range(2)]
        RSC = [A3(22944 + 512 * b, 2, L) for b in range(2)]
        ROT = A3(23968, 4, L)
        GLg = A3(18848, 2, 512)
        GQM, GKM, GQD = A3(0, 2, 512), A3(1024, 2, 512), A3(2048, 2, 512)
        GKE, GKN = A3(3072, 2, 512), A3(19872, 4, L)
        GST = A(20896, 768).rearrange("p (n t v) -> p n t v", n=3, t=2)
        GSC = A3(21664, 16, P)
        GT1, GT2 = A3(23712, 2, 512), A3(4096, 2, 512)
        OB = A3(0, 4, 512)
        OQ = A3(2048, 4, 512)
        HA = A3(0, 4, 512)
        HAl = AR3(0, 4, 512)
        HAh = AR3(2048, 4, 512)
        Hh = AR3(18848, KT, 512)
        W1h, W2h = ar_r[:, 4096:8192], ar_r[:, 8192:12288]
        W1h_cols, W2h_rows = W1h.rearrange("p (k n) -> p k n", k=KT), W2h.rearrange("p (k n) -> p k n", k=4)

        def mlp_chunks(l, u, m, i):
            per = (4, 2)[l]
            return (MLP0, MLP1)[l] + per * u + (per - 1) * m, i * (32 if l == 0 else 16), i * 2 * per, per


        def phase_end(eng, name):
            eng.drain().then_inc(S("phase"), 1)
            eng.wait_ge(S("phase"), 4 * (PHASES.index(name) + 1))

        @block.tensor
        def _(pe):
            pend = [False]
            tiles = [0]

            def mm(o, l, r, start=True, stop=True, inc=None):
                ins = nc.tensor.matmul(o, l, r, start=start, stop=stop, skip_group_check=True)
                if inc is not None:
                    ins.then_inc(S(inc), 1)
                elif pend[0]:
                    ins.then_inc(used, 1)
                    pend[0] = False
                return ins

            def mm3(o, w, x, start, stop, inc=None):
                mm(o, w[0], x[0], start, False)
                mm(o, w[0], x[1], False, False)
                mm(o, w[1], x[0], False, stop, inc)

            def tr(o, i, inc=None):
                ins = nc.tensor.transpose(o, i, ident)
                if inc is not None:
                    ins.then_inc(S(inc), 1)

            def flush():
                if pend[0]:
                    pe.drain().then_inc(used, 1)
                    pend[0] = False

            def chunk_in(n, turns=0):
                pe.wait_ge(full[n % RING], 16 * (n // RING + 1) + turns)

            def chunk_used():
                flush()
                pend[0] = True

            def tile_bank(nb=4):
                t = tiles[0]
                tiles[0] += 1
                if t >= 4:
                    pe.wait_ge(S("tile_free"), t - 3)
                return ps[t % 4]

            def stat(call, n=2 * L):
                for k in range(KT):
                    pe.wait_ge(S("squares"), 8 * call + k + 1)
                    mm(ps[6][:, 0:n], ones, H[:, k, 0:n], k == 0, k == KT - 1, "sum_ready" if k == KT - 1 else None)

            def ada(n, g, par, ncols=512, turns=0, blk=1):
                o = ps[6 + par]
                chunk_in(n, turns)
                pe.wait_ge(S("ada_out"), g + 1)
                for k in range(KT):
                    mm(o[0:2, 0:ncols], silc[:, blk, k, :], as_cols(n, ncols)[:, k, :], k == 0, k == KT - 1,
                       inc="ada_rows" if k == KT - 1 else None)
                chunk_used()

            def ada_turn(g, par, ncols=512):
                pe.wait_ge(S("ada_rows_out"), g + 1)
                m = ncols // P
                for t in range(m):
                    mm(ps[6 + par][:, 2 * t:2 * t + 2], mrow[par][:, t * P:(t + 1) * P], ident[0:2, 0:2],
                       inc="ada_turned" if t == m - 1 else None)

            def filters(d):
                for tb in range(2):
                    mm(ps[1 + tb], f_h2[0:64, tb * P:(tb + 1) * P], f_w3[0:64, d * 512:(d + 1) * 512], inc="filt_nat" if tb else None)

            def spectrum(d):
                pe.wait_ge(S("filt_dec"), d + 1)
                for ft in range(4):
                    o = ps[(3, 4, 5, 0)[ft]]
                    for tb in range(2):
                        tab = f_fw if d == 0 else f_tab.rearrange("p (a b) -> p a b", a=2)
                        mm(o, tab[:, tb, ft * P:(ft + 1) * P], f_nat[:, tb, :], d == 0 and tb == 0, d == 1 and tb == 1)

            pe.wait_ge(S("silu_c"), 1)
            ada(0, 0, 0, blk=0)
            pe.wait_ge(S("filter_in"), 16 * 5)
            mm(ps[0][0:64, 0:L], f_w1[0:33, :], f_z[0:33, :], inc="filt_mm")
            ada(1, 1, 1, blk=0)
            pe.wait_ge(S("base_in"), 16)
            ada_turn(0, 0)
            pe.wait_ge(S("filt_sin"), 1)
            mm(ps[0][0:64, L:2 * L], f_w2[0:64, :], f_h1[0:64, :], inc="filt_mm")
            ada(2, 2, 0, blk=0)
            ada_turn(1, 1)
            pe.wait_ge(S("filt_sin"), 2)
            filters(0)
            ada(3, 3, 1, blk=0)
            ada_turn(2, 0)
            flush()
            spectrum(0)
            filters(1)
            ada_turn(3, 1)
            with pe.Fori(1, 3) as i:
                for u in range(RING):
                    ada(u, i * RING + u, u % 2, 512, i * 16, blk=0)
                    if u:
                        ada_turn(i * RING + u - 1, (u - 1) % 2)
                flush()
                ada_turn(i * RING + 3, 1)
            spectrum(1)
            pe.drain().then_inc(S("spectrum"), 1)
            phase_end(pe, "filters")

            stat(0)

            pe.wait_ge(S("normed"), 16)
            for j, c in enumerate(WIN_ORDER[:8]):
                n = WIN + 2 * j
                if c != 3:
                    wide = 2 * L if c in (1, 2) else L
                    chunk_in(n)
                    for nt in range(4):
                        o = tile_bank()
                        for k in range(KT):
                            mm(o[:, 0:wide], as_cols(n)[:, k, nt * P:(nt + 1) * P], H[:, k, 0:wide], k == 0, k == KT - 1,
                               "tile_done" if k == KT - 1 else None)
                else:
                    chunk_in(n)
                    for tb in range(4):
                        o = tile_bank()
                        for k in range(KT):
                            mm(o, H[:, k, tb * P:(tb + 1) * P], as_cols(n)[:, k, :], k == 0, k == KT - 1,
                               "tile_done" if k == KT - 1 else None)
                chunk_used()
                if j:
                    ada_turn(12 + j - 1, (j - 1) % 2)
                ada(n + 1, 12 + j, j % 2)
            flush()
            ada_turn(12 + 7, 1)
            phase_end(pe, "projected")

            for b in (4, 5):
                mm(ps[b], SC[:, 0, :], SC[:, 0:4, :], True, False)
            for d in range(2):
                pe.wait_ge(S("kd_ready"), d + 1)
                for hh in range(2):
                    for j in range(4):
                        tb, h = hh, j
                        tr(ps[hh][:, j * P:(j + 1) * P], KC[d][:, h, tb * P:(tb + 1) * P], "turned" if j == 3 else None)
                pe.wait_ge(S("ke_ready"), d + 1)
                for hh in range(2):
                    for j in range(4):
                        tr(ps[2 + hh][:, j * P:(j + 1) * P], KX[d][:, j, hh * P:(hh + 1) * P], "turned" if j == 3 else None)
                pe.wait_ge(S("turned_out"), 4 * d + 2)
                for h in range(HG_H):
                    for tb in range(2):
                        mm(ps[0][:, h * P:(h + 1) * P], KDN[:, tb * 4 + h, :], Vn[:, 2 + tb, h * P:(h + 1) * P], tb == 0, tb == 1,
                           "ctx_state" if (h, tb) == (3, 1) else None)
                pe.wait_ge(S("qm_ready"), d + 1)
                pe.wait_ge(S("turned_out"), 4 * d + 4)
                for tb in range(2):
                    for h in range(HG_H):
                        mm(ps[6 + tb][:, h * P:(h + 1) * P], KM[:, h, tb * P:(tb + 1) * P], QM[:, h, tb * P:(tb + 1) * P],
                           inc="scores" if h == 3 else None)
                pe.wait_ge(S("states_out"), 8 * d + 1)
                for bi in range(2):
                    tb = bi if d == 0 else 1 - bi
                    if bi:
                        pe.wait_ge(S("states_out"), 8 * d + 5)
                    for j in range(4):
                        r = slice(32 * j, 32 * j + 32)
                        for h in range(HG_H):
                            mm(ps[j][:, h * P:(h + 1) * P], KEN[r, tb * 4 + h, :], Vn[r, tb, h * P:(h + 1) * P],
                               inc="updates" if (j, h) == (3, 3) else None)
                    if bi == 0:
                        pe.wait_ge(S("masked"), 2 * d + 2)
                        for h in range(HG_H):
                            for tb2 in range(2):
                                mm(ps[4 + h // 2][:, (h % 2) * L + tb2 * P:(h % 2) * L + (tb2 + 1) * P],
                                   Vn[:, tb2, h * P:(h + 1) * P], SC[:, tb2 * 4 + h, :], False, False)
                    for c in range(4):
                        n = 4 * bi + c
                        ch = n if d == 0 else 7 - n
                        pe.wait_ge(S("states_out"), 8 * d + n + 1)
                        for h in range(HG_H):
                            mm(ps[4 + h // 2][:, (h % 2) * L + ch * 32:(h % 2) * L + ch * 32 + 32],
                               ST[:, n % 4, h * P:(h + 1) * P], QD[:, h, ch * 32:ch * 32 + 32], False, False,
                               "inter" if h == 3 else None)
                phase_end(pe, "scan_f" if d == 0 else "scan_b")

            pe.wait_ge(S("o_squares"), 1)
            for b in range(2):
                mm(ps[4 + b], ones, OSQ[:, 2 * b:2 * b + 2, :], inc="o_sum" if b else None)

            for j in range(8, 12):
                n = WIN + 2 * j
                chunk_in(n)
                for nt in range(4):
                    o = tile_bank()
                    for k in range(KT):
                        mm(o[:, 0:L], as_cols(n)[:, k, nt * P:(nt + 1) * P], H[:, k, 0:L], k == 0, k == KT - 1,
                           "tile_done" if k == KT - 1 else None)
                chunk_used()
                if j > 8:
                    ada_turn(12 + j - 1, (j - 1) % 2)
                ada(n + 1, 12 + j, j % 2)
            flush()
            ada_turn(12 + 11, 1)
            pe.wait_ge(S("o_inverse"), 1)
            pe.wait_ge(S("hy_in"), 16)

            pe.wait_ge(S("uv_ready"), 1)
            for tb in range(2):
                for c in range(HYT):
                    tr(ps[4 + tb][:, c * P:(c + 1) * P], UV[:, c, tb * P:(tb + 1) * P], "un_turned" if c == 3 else None)
            pe.wait_ge(S("un_ready"), 2)
            pe.wait_ge(S("tile_free"), tiles[0])
            for ft in range(4):
                for tb in range(2):
                    mm(ps[ft], HFW[:, tb, ft * P:(ft + 1) * P], UN[:, tb, :], tb == 0, tb == 1, "u_spec" if (ft, tb) == (3, 1) else None)
            pe.wait_ge(S("y_spec"), 1)
            for c in range(HYT):
                for ft in range(4):
                    mm(ps[4 + c // 2][:, (c % 2) * L:(c % 2) * L + L], YF[:, ft, c * P:(c + 1) * P], HINV[:, ft, :], ft == 0, ft == 3,
                       "y_time" if (c, ft) == (3, 3) else None)
            phase_end(pe, "hyena")

            chunk_in(MERGE)
            chunk_in(MERGE + 1)
            for nt in range(KT):
                o = ps[nt % 4]
                if nt >= 4:
                    pe.wait_ge(S("merged"), nt - 3)
                for side, Y in ((0, OS), (1, YB)):
                    for k in range(4):
                        mm(o[:, side * L:(side + 1) * L], as_rows(MERGE + side)[:, k, nt * P:(nt + 1) * P], Y[:, k, :], k == 0, k == 3,
                           "merge_mm" if (side, k) == (1, 3) else None)
            pe.drain().then_inc(used, 1)
            pe.drain().then_inc(used, 1)
            pe.wait_ge(S("merged"), 8)
            for j in range(2):
                n = MERGE + 2 + j
                chunk_in(n)
                for nt in range(4):
                    t = j * 4 + nt
                    o = ps[4 + t % 2]
                    if t >= 2:
                        pe.wait_ge(S("out_added"), t - 1)
                    for k in range(KT):
                        mm(o[:, 0:L], as_cols(n)[:, k, nt * P:(nt + 1) * P], MIX[:, k, :], k == 0, k == KT - 1,
                           "out_mm" if k == KT - 1 else None)
                chunk_used()
            flush()
            phase_end(pe, "merged")

            stat(1, L)
            pe.wait_ge(S("normed"), 16 + 8)
            for tb in range(TB):
                for k in range(KT):
                    tr(ps[2 * tb + k // 4][:, (k % 4) * P:(k % 4 + 1) * P], H[:, k, tb * P:(tb + 1) * P], "h_turned" if k % 4 == 3 else None)
            pe.wait_ge(S("moe_in"), 32)
            for tb in range(TB):
                for k in range(KT):
                    mm(ps[4][:, tb * NR:(tb + 1) * NR], H[:, k, tb * P:(tb + 1) * P], WR[:, k, :], k == 0, k == KT - 1,
                       "logits" if (tb, k) == (1, 7) else None)
            pe.wait_ge(S("selected"), 1)
            mm(ps[5][:, 0:NX], SLT, SELX[:, 0, :])
            mm(ps[5][:, NX:2 * NX], ones, SELX[:, 0, :], True, False)
            mm(ps[5][:, NX:2 * NX], SLT, SELX[:, 1, :], False, True)
            mm(ps[5][:, 2 * NX:3 * NX], ones, SELX[:, 0, :], True, False)
            mm(ps[5][:, 2 * NX:3 * NX], ones, SELX[:, 1, :], False, True, inc="ranks")
            pe.wait_ge(S("h_natural"), 4)
            pe.wait_ge(S("sw_zero"), 1)
            for b in range(4):
                mm(ps[b], SW[:, 0, :], SW[:, 0:4, :], True, False, inc="cleared" if b == 3 else None)

            def gather(buf):
                for k in range(KT):
                    for tb in range(TB):
                        mm(ps[4][:, k * CAP:(k + 1) * CAP], HN[:, tb, k * P:(k + 1) * P], SGv[:, buf, tb, :], tb == 0, tb == 1,
                           inc="gathered" if (k, tb) == (7, 1) else None)

            pe.wait_ge(S("onehot"), 1)
            gather(0)
            with pe.Fori(0, NX // 4) as i:
                for u in range(4):
                    n = MOE + 3 * u
                    pe.wait_ge(S("gather_out"), i * 4 + u + 1)
                    for m in range(2):
                        chunk_in(n + m, i * 48)
                        for nt in range(FT):
                            for k in range(KT):
                                mm(ps[5][:, m * 256 + nt * CAP:m * 256 + (nt + 1) * CAP], as_cols(n + m)[:, k, nt * P:(nt + 1) * P],
                                   HG[:, k * CAP:(k + 1) * CAP], k == 0, k == KT - 1,
                                   inc="gate_up" if (nt, k, m) == (FT - 1, KT - 1, 1) else None)
                        if m == 0:
                            chunk_used()
                    pe.wait_ge(S("onehot"), i * 4 + u + 2)
                    chunk_used()
                    gather((u + 1) % 2)
                    chunk_in(n + 2, i * 48)
                    pe.wait_ge(S("hidden"), i * 4 + u + 1)
                    o = slice((u % 2) * CAP, (u % 2 + 1) * CAP)
                    for nb in range(2):
                        for k in range(FT):
                            mm(ps[6 + nb][o, :], HID[:, k, :], as_rows(n + 2)[:, k, nb * 512:(nb + 1) * 512], k == 0, k == FT - 1,
                               inc="down" if (nb, k) == (1, FT - 1) else None)
                    chunk_used()
                    if u % 2:
                        pe.wait_ge(S("pair_weights"), i * 2 + u // 2 + 1)
                        pe.wait_ge(S("gather_out"), i * 4 + u + 2)
                        for tb in range(TB):
                            tr(ps[4][:, tb * P:(tb + 1) * P], SWv[:, u // 2, tb, :], "weights_turned" if tb else None)
                        pe.wait_ge(S("pair_out"), i * 2 + u // 2 + 1)
                        pe.wait_ge(S("weights_out"), i * 2 + u // 2 + 1)
                        for k in range(KT):
                            mm(ps[k // 2][:, (k % 2) * L:(k % 2 + 1) * L], YS[:, k * P:(k + 1) * P], SWT, False, False,
                               inc="scattered" if k == 7 else None)
                flush()

            pe.wait_ge(S("passes_known"), 1)
            more = pe.value_load(npass[0:1, 0:1])
            with pe.If(more > 0):
                pe.drain().then_inc(S("over_begun"), 1)
                with pe.Fori(0, more) as q:
                    with pe.Fori(0, NX) as e:
                        g = q * NX + e
                        pe.wait_ge(S("over_onehot"), g + 1)
                        for k in range(KT):
                            for tb in range(TB):
                                mm(ps[4][:, k * CAP:(k + 1) * CAP], HN[:, tb, k * P:(k + 1) * P], SGv[:, 0, tb, :], tb == 0, tb == 1,
                                   inc="over_gathered" if (k, tb) == (7, 1) else None)
                        pe.wait_ge(S("over_gather_out"), g + 1)
                        for m in range(2):
                            pe.wait_ge(S(f"over_w{m}"), g * 16 + 16)
                            for nt in range(FT):
                                for k in range(KT):
                                    mm(ps[5][:, m * 256 + nt * CAP:m * 256 + (nt + 1) * CAP], as_cols(m)[:, k, nt * P:(nt + 1) * P],
                                       HG[:, k * CAP:(k + 1) * CAP], k == 0, k == KT - 1,
                                       inc="over_gate_up" if (nt, k, m) == (FT - 1, KT - 1, 1) else None)
                        for tb in range(TB):
                            tr(ps[4][0:CAP, tb * P:(tb + 1) * P], SWv[:, 0, tb, 0:CAP], "over_turned" if tb else None)
                        pe.wait_ge(S("over_hidden"), g + 1)
                        pe.wait_ge(S("over_w2"), g * 16 + 16)
                        for nb in range(2):
                            for k in range(FT):
                                mm(ps[6 + nb][0:CAP, :], HID[:, k, :], as_rows(2)[:, k, nb * 512:(nb + 1) * 512], k == 0, k == FT - 1,
                                   inc="over_down" if (nb, k) == (1, FT - 1) else None)
                        pe.wait_ge(S("over_out"), g + 1)
                        for k in range(KT):
                            mm(ps[k // 2][:, (k % 2) * L:(k % 2 + 1) * L], YS[0:CAP, k * P:(k + 1) * P], SWT[0:CAP, :], False, False,
                               inc="over_begun" if k == 7 else None)
            pe.drain().then_inc(S("experts_done"), 1)
            pe.wait_ge(S("experts_added"), 1)
            stat(2, L)
            phase_end(pe, "experts")

            ncall = 3
            for l, first, mlp in ((0, L0, MLP0), (1, L1, MLP1)):
                W = 2 * L if l == 0 else L
                stat(ncall)
                pe.wait_ge(S("normed"), (16 + 8 + 8, 16 + 8 + 8 + 32)[l] + 16)
                ncall += 1
                for j in range(7):
                    n = first + j
                    chunk_in(n)
                    if j in (2, 5):
                        for tb in range(4):
                            o = tile_bank()
                            for k in range(KT):
                                mm(o, H[:, k, tb * P:(tb + 1) * P], as_cols(n)[:, k, :], k == 0, k == KT - 1, "tile_done" if k == KT - 1 else None)
                    else:
                        for nt in range(4):
                            wide = 2 * L if j == 1 or (j == 4 and nt >= 2) else W
                            o = tile_bank()
                            for k in range(KT):
                                mm(o[:, 0:wide], as_cols(n)[:, k, nt * P:(nt + 1) * P], H[:, k, 0:wide], k == 0, k == KT - 1,
                                   "tile_done" if k == KT - 1 else None)
                    chunk_used()
                n = first + 7
                chunk_in(n)
                o = tile_bank()
                for k in range(KT):
                    mm(o[0:32, :], as_cols(n, 32)[:, k, :], H[:, k, :], k == 0, k == KT - 1, "tile_done" if k == KT - 1 else None)
                chunk_used()
                flush()
                pe.wait_ge(S("b2_in"), 16 * (3 + l))
                pe.wait_ge(S("tile_free"), tiles[0])
                for m, M in enumerate((RQ, RK)):
                    for h in range(RT_H):
                        mm(ps[4 + m * 2 + h // 2][:, (h % 2) * L:(h % 2 + 1) * L], PERM, M[:, h, 0:L],
                           inc="swapped" if h % 2 else None)
                phase_end(pe, f"l{l}_in")

                for h in range(RT_H):
                    b = h % 2
                    c = l * RT_H + h
                    for tb in range(2):
                        tr(ps[4][:, tb * P:(tb + 1) * P], RK[:, h, L + tb * P:L + (tb + 1) * P], "rk_turned" if tb else None)
                    pe.wait_ge(S("r_prep"), c + 1)
                    pe.wait_ge(S("rk_out"), c + 1)
                    for d in range(2):
                        for tb in range(2):
                            mm(ps[5][:, d * P:(d + 1) * P], RKN[b][:, tb, :], RVD[b][:, d, tb, :], tb == 0, tb == 1,
                               "r_state" if (d, tb) == (1, 1) else None)
                    sides = (0, 1) if l == 0 else (0,)
                    for side in sides:
                        for sblk in range(2):
                            mm(ps[6 + side][:, sblk * L:(sblk + 1) * L], RK[:, h, side * L + sblk * P:side * L + (sblk + 1) * P],
                               RQ[:, h, side * L:(side + 1) * L], inc="r_scores" if sblk else None)
                    for side in sides:
                        q = c * 2 + side if l == 0 else 2 * RT_H + h
                        pe.wait_ge(S("r_decayed"), q + 1)
                        o = ps[h][:, side * L:(side + 1) * L]
                        for sblk in range(2):
                            mm(o, RV[:, side * 2 + sblk, h * P:(h + 1) * P], RSC[side][:, sblk, :], sblk == 0, sblk == 1 and side == 1,
                               inc="r_head" if sblk and side else None)
                        if side == 0:
                            pe.wait_ge(S("r_state_out"), c + 1)
                            for d in range(2):
                                mm(o, RST[b][:, d, :], RQD[b][:, d, :], False, d == 1, inc="r_head" if d and l else None)
                pe.wait_ge(S("r_copied"), (4 * (l + 1)))
                for h in range(RT_H):
                    mm(ps[4 + h][:, 0:W], ones, OB[:, h, 0:W], inc="r_mean")
                pe.wait_ge(S("r_sq"), 4 * (l + 1))
                for h in range(RT_H):
                    mm(ps[h][:, 0:W], ones, OQ[:, h, 0:W], inc="r_var")
                phase_end(pe, f"l{l}_ret")

                nx = 4 if l == 0 else 2
                pe.wait_ge(S("gsc_clear"), l + 1)
                for h in range(4):
                    mm(ps[h], GSC[:, 0, :], GSC[:, 0:4, :], True, False)
                for d in range(2):
                    g = 2 * l + d
                    for t in range(2):
                        mm(ps[4 + t], GUP[0:32, d, t * P:(t + 1) * P], DT[0:32, :], inc="gate_mm")
                    pe.wait_ge(S("gke_ready"), g + 1)
                    for ch in range(4):
                        for t in range(2):
                            tr(ps[4 + ch // 2][:, (ch % 2) * L + t * P:(ch % 2) * L + (t + 1) * P], GKE[:, t, ch * P:(ch + 1) * P],
                               "gk_turned" if (ch, t) in ((1, 1), (3, 1)) else None)
                    pe.wait_ge(S("gqm_ready"), g + 1)
                    for ch in range(nx):
                        for h in range(4):
                            r = slice(64 * (h % 2), 64 * (h % 2) + 64)
                            k = ch * 2 + h // 2
                            mm(ps[6 + h % 2][:, (k % 4) * P:(k % 4 + 1) * P], GKM[r, h // 2, ch * P:(ch + 1) * P], GQM[r, h // 2, ch * P:(ch + 1) * P],
                               inc="g_scores" if h == 3 else None)
                        if ch == 1 and nx == 4:
                            pe.wait_ge(S("g_masked"), (0, 8, 16, 20)[g] + 4)
                    order = [2, 3, 0, 1] if d == 0 else [3, 2, 1, 0]
                    pe.wait_ge(S("gk_out"), 2 * (g + 1))
                    for n, ch in enumerate(order[:3]):
                        for h in range(4):
                            r = slice(64 * (h % 2), 64 * (h % 2) + 64)
                            mm(ps[4 + n // 2][r, (n % 2) * L + (h // 2) * P:(n % 2) * L + (h // 2 + 1) * P],
                               GKN[:, ch, h * 64:(h + 1) * 64], GV[:, ch, h * P:(h + 1) * P], inc="g_update" if h == 3 else None)
                    pe.wait_ge(S("g_masked"), (8, 16, 20, 24)[g])
                    for ch in range(nx):
                        for h in range(4):
                            mm(ps[h][:, ch * P:(ch + 1) * P], GV[:, ch, h * P:(h + 1) * P], GSC[:, (h % 2) * 8 + ch * 2 + h // 2, :], False, False)
                    for n, ch in enumerate(order):
                        if n == 0 or ch >= nx:
                            continue
                        pe.wait_ge(S("g_state"), 3 * g + n)
                        for h in range(4):
                            r = slice(64 * (h % 2), 64 * (h % 2) + 64)
                            mm(ps[h][:, ch * P:(ch + 1) * P], GST[r, n - 1, h // 2, :], GQD[r, h // 2, ch * P:(ch + 1) * P], False, False)
                    if d == 0:
                        phase_end(pe, f"l{l}_gf")
                pe.drain().then_inc(S("g_done"), 1)
                pe.wait_ge(S("g_sq"), 4 * (l + 1))
                for h in range(4):
                    mm(ps[4 + h][:, 0:W], ones, OQ[:, h, 0:W], inc="g_sum")
                phase_end(pe, f"l{l}_gb")

                for j in range(2):
                    n = first + 8 + j
                    chunk_in(n)
                    for nt in range(4):
                        t = j * 4 + nt
                        if t >= 4:
                            pe.wait_ge(S("w_out_added"), 8 * l + t - 3)
                        for k in range(KT):
                            mm(ps[t % 4][:, 0:W], as_cols(n)[:, k, nt * P:(nt + 1) * P], YT[:, k, 0:W], k == 0, k == KT - 1,
                               "w_out_mm" if k == KT - 1 else None)
                    chunk_used()
                flush()
                stat(ncall, W)
                ncall += 1
                phase_end(pe, f"l{l}_out")

                pe.wait_ge(S("h_split"), l + 1)
                with pe.Fori(0, 4) as i:
                    n = mlp
                    turns = i * (32 if l == 0 else 16)
                    for u in range(2):
                        j = i * 2 + u
                        pe.wait_ge(S("w1_split"), 8 * l + j + 1)
                        for nt in range(4):
                            c = slice(nt * P, (nt + 1) * P)
                            for k in range(KT):
                                mm3(ps[nt][:, 0:W], (W1h_cols[:, k, c], as_cols(n, slot=low)[:, k, c]), (Hh[:, k, 0:W], Hl[:, k, 0:W]),
                                    k == 0, k == KT - 1, "hid_mm" if k == KT - 1 else None)
                        chunk_used()
                        n += 1
                        if l == 0:
                            for a in range(2):
                                ada(n, 24 + i * 4 + u * 2 + a, a, ADA_COLS, turns)
                                n += 1
                            ada_turn(24 + i * 4 + u * 2, 0, ADA_COLS)
                        pe.wait_ge(S("w2_split"), 8 * l + j + 1)
                        pe.wait_ge(S("hid_out"), 32 * l + j * 4 + 4)
                        for nt in range(KT):
                            pe.wait_ge(S("mlp_bank_free"), (64 + 2) * l + j * 8 + nt + 1)
                            c = slice(nt * P, (nt + 1) * P)
                            for k in range(4):
                                mm3(ps[4 + nt % 2][:, 0:W], (W2h_rows[:, k, c], as_rows(n, slot=low)[:, k, c]), (HAh[:, k, 0:W], HAl[:, k, 0:W]),
                                    k == 0, k == 3, "mlp_mm" if k == 3 else None)
                        chunk_used()
                        n += 1
                        if l == 0:
                            ada_turn(24 + i * 4 + u * 2 + 1, 1, ADA_COLS)
                    flush()
                if l == 1:
                    stat(ncall, L)
                phase_end(pe, f"l{l}_mlp")

        CALLS = [(0, 0, 2 * L, (0, 1)), (0, 1, L, (0,)), ("fin", 0, L, (0,)), (1, 0, 2 * L, (0, 1)), (1, 1, 2 * L, (0, 1)),
                 (2, 0, 2 * L, (0, 1)), (2, 1, L, (0,)), ("fin2", 0, L, (0,))]

        @block.scalar
        def _(act):
            A_ = nc.scalar.activation
            own = [0]
            tiles = [0]
            done = [0]

            def link(ins):
                own[0] += 1
                ins.then_inc(S("act_own"), 1)
                act.wait_ge(S("act_own"), own[0])

            def rsqrt(o, i, n):
                link(A_(o, i, ACT.Ln, scale=1.0 / n, bias=vec("eps")))
                return A_(o, o, ACT.Exp, scale=-0.5)

            def norm(call):
                b, which, N, halves = CALLS[call]
                for k in range(KT):
                    A_(H[:, k, 0:N], X[:, k, 0:N], ACT.Square).then_inc(S("squares"), 1)
                act.wait_ge(S("sum_ready"), call + 1)
                rsqrt(RS[:, 0:N], ps[6][:, 0:N], D).then_inc(S("rms_ready"), 1)
                for k in range(KT):
                    if k % 4 == 0:
                        act.wait_ge(S("scaled"), 2 * call + k // 4 + 1)
                    for s in halves:
                        c = slice(s * L, (s + 1) * L)
                        if isinstance(b, str):
                            A_(X[:, k, c], H[:, k, c], ACT.Copy, scale=vec(b, k)).then_inc(S("normed"), 1)
                        else:
                            A_(H[:, k, c], H[:, k, c], ACT.Identity, scale=gsc[:, b, which, k, s:s + 1],
                               bias=mod[:, b, 24 * which + k, s:s + 1]).then_inc(S("normed"), 1)
                        done[0] += 1

            def tile():
                t = tiles[0]
                tiles[0] += 1
                act.wait_ge(S("tile_done"), t + 1)
                return ps[t % 4]

            def take(o, i, f=ACT.Copy, **kw):
                A_(o, i, f, **kw).then_inc(S("tile_free"), 1)

            def ada_rows(g, par, ncols=512):
                act.wait_ge(S("ada_rows"), g + 1)
                A_(mrow[par][:, 0:ncols], ps[6 + par][0:2, 0:ncols], ACT.Copy).then_inc(S("ada_rows_out"), 1)

            act.wait_ge(S("vecs_in"), 16)
            A_(silc[:, 0], vec("c1", 0, 16).rearrange("p (s k) -> p k s", s=2), ACT.Silu)
            A_(silc[:, 1], vec("c2", 0, 16).rearrange("p (s k) -> p k s", s=2), ACT.Silu).then_inc(S("silu_c"), 1)
            for i, h in enumerate((f_h1, f_h2)):
                ada_rows(i, i)
                act.wait_ge(S("filt_arg"), i + 1)
                A_(h[0:64, :], f_t[0:64, :], ACT.Sin).then_inc(S("filt_sin"), 1)
            ada_rows(2, 0)
            ada_rows(3, 1)
            with act.Fori(1, 3) as i:
                for u in range(RING):
                    ada_rows(i * RING + u, u % 2)
            act.wait_ge(S("spectrum"), 1)
            for ft in range(4):
                A_(KS[:, ft, :], ps[(3, 4, 5, 0)[ft]][:, :], ACT.Copy)
            act.wait_ge(S("lb_arg"), 1)
            A_(lbc[:, 8:24], lbc[:, 8:24], ACT.Exp).then_inc(S("lb_exp"), 1)
            phase_end(act, "filters")

            norm(0)

            def gate_log(d):
                for h in range(HG_H):
                    i = A_(L2[d][:, h, :], L2[d][:, h, :], ACT.Ln, scale=lbc[:, 32 + 4 * d + h:33 + 4 * d + h],
                           bias=lbc[:, 24 + 4 * d + h:25 + 4 * d + h])
                i.then_inc(S("lf_ready"), 1)

            def scan_exps(d):
                act.wait_ge(S("ctx_arg"), d + 1)
                A_(KM, KM, ACT.Exp).then_inc(S("ctx_exp"), 1)
                act.wait_ge(S("hg_arg"), d + 1)
                A_(KM, QM, ACT.Exp, scale=-1.0)
                A_(QM, QM, ACT.Exp)
                A_(QD, QD, ACT.Exp).then_inc(S("hg_exp"), 1)
                act.wait_ge(S("ke_ready"), d + 1)
                A_(QD, LX[d], ACT.Exp)
                end = HG_C - 1 if d == 0 else 0
                A_(et[:, 0:32].rearrange("p (h c) -> p h c", h=4), LX[d].rearrange("p h (c k) -> p h c k", k=HG_C)[:, :, :, end], ACT.Exp)\
                    .then_inc(S("hg_exp2"), 1)

            for j, c in enumerate(WIN_ORDER[:8]):
                for nt in range(4):
                    o = tile()
                    if c == 0:
                        take(Qt[:, nt, :], o[:, 0:L])
                    elif c in (1, 2):
                        d = c - 1
                        A_(K2[d][:, nt, :], o[:, :], ACT.Sigmoid, scale=-1.0)
                        take(L2[d][:, nt, :], o[:, :], ACT.Sigmoid)
                    elif c == 3:
                        take(Vn[:, nt, :], o[:, :])
                    elif c == 4:
                        take(Gt[:, nt, :], o[:, 0:L], ACT.Silu)
                    else:
                        take(HYt[:, (c - 5) * 4 + nt, :], o[:, 0:L])
                if c in (1, 2):
                    d = c - 1
                    act.wait_ge(S("tile_free"), tiles[0])
                    gate_log(d)
                ada_rows(12 + j, j % 2)
                if c == 4:
                    scan_exps(0)
            phase_end(act, "projected")

            for d in range(2):
                if d == 1:
                    scan_exps(1)
                for j in range(4):
                    act.wait_ge(S("turned"), 4 * d + j + 1)
                    o = (KDN, KEN)[j // 2][:, (j % 2) * 4:(j % 2) * 4 + 4, :]
                    A_(o, ps[j][:, :].rearrange("p (a b) -> p a b", a=4), ACT.Copy).then_inc(S("turned_out"), 1)
                phase_end(act, "scan_f" if d == 0 else "scan_b")

            for b in range(2):
                v = ps[4 + b][:, :].rearrange("p (a b) -> p a b", a=2)
                A_(OS[:, 2 * b:2 * b + 2, :], v, ACT.Copy)
                i = A_(OSQ[:, 2 * b:2 * b + 2, :], v, ACT.Square)
            i.then_inc(S("o_squares"), 1)
            act.wait_ge(S("o_sum"), 1)
            for b in range(2):
                v = ps[4 + b][:, :].rearrange("p (a b) -> p a b", a=2)
                i = rsqrt(ORS[:, 2 * b:2 * b + 2, :], v, HG_D)
            i.then_inc(S("o_inverse"), 1)
            for nt in range(16):
                take(GL[:, nt, :], tile()[:, 0:L], ACT.Sigmoid)
                if nt % 4 == 3:
                    ada_rows(20 + nt // 4, (nt // 4) % 2)
            for tb in range(2):
                act.wait_ge(S("un_turned"), tb + 1)
                A_(UN[:, tb, :], ps[4 + tb][:, :], ACT.Copy).then_inc(S("un_ready"), 1)
            phase_end(act, "hyena")
            phase_end(act, "merged")

            norm(1)
            for b in range(4):
                act.wait_ge(S("h_turned"), b + 1)
                A_(HN[:, b // 2, (b % 2) * 512:(b % 2 + 1) * 512], ps[b][:, :], ACT.Copy).then_inc(S("h_natural"), 1)
            for i in range(2):
                act.wait_ge(S("rt_arg"), i + 1)
                o = RT[:, 16:24] if i == 0 else RT[:, 200:202]
                A_(o, o, ACT.Exp).then_inc(S("rt_exp"), 1)
            act.wait_ge(S("gathered"), 1)
            A_(HG, ps[4][:, :], ACT.Copy).then_inc(S("gather_out"), 1)
            with act.Fori(0, NX // 4) as i:
                for u in range(4):
                    act.wait_ge(S("gate_up"), i * 4 + u + 1)
                    A_(SIL, ps[5][:, 0:256].rearrange("p (a b) -> p a b", a=FT), ACT.Silu).then_inc(S("silu"), 1)
                    act.wait_ge(S("gathered"), i * 4 + u + 2)
                    A_(HG, ps[4][:, :], ACT.Copy).then_inc(S("gather_out"), 1)
                    if u % 2:
                        act.wait_ge(S("down"), i * 4 + u + 1)
                        A_(YS[:, 0:512], ps[6][:, :], ACT.Copy)
                        A_(YS[:, 512:1024], ps[7][:, :], ACT.Copy).then_inc(S("pair_out"), 1)
            act.wait_ge(S("passes_known"), 1)
            more = act.value_load(npass[0:1, 0:1])
            with act.If(more > 0):
                with act.Fori(0, more) as q:
                    with act.Fori(0, NX) as e:
                        g = q * NX + e
                        act.wait_ge(S("over_gathered"), g + 1)
                        A_(HG, ps[4][:, :], ACT.Copy).then_inc(S("over_gather_out"), 1)
                        act.wait_ge(S("over_gate_up"), g + 1)
                        A_(SIL, ps[5][:, 0:256].rearrange("p (a b) -> p a b", a=FT), ACT.Silu).then_inc(S("over_silu"), 1)
                        act.wait_ge(S("over_down"), g + 1)
                        A_(YS[0:CAP, 0:512], ps[6][0:CAP, :], ACT.Copy)
                        act.wait_ge(S("over_weights"), g + 1)
                        A_(YS[0:CAP, 512:1024], ps[7][0:CAP, :], ACT.Copy).then_inc(S("over_out"), 1)
            act.wait_ge(S("experts_added"), 1)
            norm(2)
            phase_end(act, "experts")

            ncall = 3
            for l in range(LAYERS):
                W = 2 * L if l == 0 else L
                if l == 0:
                    act.wait_ge(S("normed"), done[0])
                    act.wait_ge(S("ctx2_in"), 16)
                norm(ncall)
                ncall += 1
                lg = lgam[:, 0:8]
                link(A_(lg, vec("decay", l * 8, 8), ACT.Exp))
                A_(lg, lg, ACT.Ln, scale=-1.0, bias=vec("one")).then_inc(S("lgam"), 1)
                act.wait_ge(S("col_arg"), l + 1)
                A_(lgam[:, 8:24], lgam[:, 8:24], ACT.Exp).then_inc(S("col_exp"), 1)
                for j in range(8):
                    for nt in range(1 if j == 7 else 4):
                        o = tile()
                        if j == 0:
                            take(RQ[:, nt, 0:W], o[:, 0:W], scale=float(P) ** -0.5)
                        elif j == 1:
                            take(RK[:, nt, :], o[:, :])
                        elif j == 2:
                            take(RV[:, nt, :], o[:, :])
                        elif j == 3:
                            take(YT[:, nt, 0:W], o[:, 0:W], ACT.Silu)
                        elif j == 4 and nt < 2:
                            take(GQ[:, nt, 0:W], o[:, 0:W], scale=float(GL_K) ** -0.5)
                        elif j == 4:
                            take(GK[:, nt - 2, :], o[:, :])
                        elif j == 5:
                            take(GV[:, nt, :], o[:, :])
                        elif j == 6:
                            take(YT[:, 4 + nt, 0:W], o[:, 0:W], ACT.Silu)
                        else:
                            take(DT[0:32, :], o[0:32, :])
                phase_end(act, f"l{l}_in")

                def head_exps(h):
                    c = l * RT_H + h
                    act.wait_ge(S("r_arg"), c + 1)
                    A_(Wd[h % 2], Wd[h % 2], ACT.Exp)
                    A_(RQD[h % 2], RQD[h % 2], ACT.Exp).then_inc(S("r_exp"), 1)

                head_exps(0)
                for h in range(RT_H):
                    c = l * RT_H + h
                    b = h % 2
                    if h < RT_H - 1:
                        head_exps(h + 1)
                    act.wait_ge(S("rk_turned"), c + 1)
                    A_(RKN[b], ps[4][:, 0:2 * P].rearrange("p (a b) -> p a b", a=2), ACT.Copy).then_inc(S("rk_out"), 1)
                    act.wait_ge(S("r_state"), c + 1)
                    A_(RST[b], ps[5][:, 0:2 * P].rearrange("p (a b) -> p a b", a=2), ACT.Copy).then_inc(S("r_state_out"), 1)
                    act.wait_ge(S("r_head"), c + 1)
                    A_(OB[:, h, 0:W], ps[h][:, 0:W], ACT.Copy).then_inc(S("r_copied"), 1)
                for h in range(RT_H):
                    act.wait_ge(S("r_centred"), l * 4 + h + 1)
                    A_(OQ[:, h, 0:W], OB[:, h, 0:W], ACT.Square).then_inc(S("r_sq"), 1)
                for h in range(RT_H):
                    act.wait_ge(S("r_var"), l * 4 + h + 1)
                    rsqrt(OQ[:, h, 0:W], ps[h][:, 0:W], P).then_inc(S("r_inverse"), 1)
                phase_end(act, f"l{l}_ret")

                for d in range(2):
                    g = 2 * l + d
                    for t in range(2):
                        act.wait_ge(S("gate_mm"), 2 * g + t + 1)
                        i = A_(GT1[:, t, :], ps[4 + t][:, :], ACT.Identity, bias=vec("gate_b", l * 4 + d * 2 + t))
                    link(i)
                    link(A_(GT2, GT1, ACT.Abs))
                    link(A_(GT2, GT2, ACT.Exp, scale=-1.0))
                    A_(GT2, GT2, ACT.Ln, bias=vec("one")).then_inc(S("g_soft"), 1)
                    act.wait_ge(S("g_arg"), g + 1)
                    A_(GKE, GT2, ACT.Exp, scale=1.0 / 16).then_inc(S("g_exp"), 1)
                    A_(GKM, GT1, ACT.Exp, scale=-1.0 / 16)
                    A_(GQM, GT1, ACT.Exp, scale=1.0 / 16).then_inc(S("g_exp"), 1)
                    A_(GQD, GLg, ACT.Exp, scale=1.0 / 16)
                    end = P - 1 if d == 0 else 0
                    A_(et[:, 32:40], GLg.rearrange("p t (c k) -> p (t c) k", k=P)[:, :, end], ACT.Exp, scale=1.0 / 16).then_inc(S("g_exp"), 1)
                    for b in range(2):
                        act.wait_ge(S("gk_turned"), 2 * g + b + 1)
                        A_(GKN[:, 2 * b:2 * b + 2, :], ps[4 + b][:, :].rearrange("p (a b) -> p a b", a=2), ACT.Copy).then_inc(S("gk_out"), 1)
                    if d == 0:
                        phase_end(act, f"l{l}_gf")
                act.wait_ge(S("g_done"), l + 1)
                for h in range(4):
                    A_(OB[:, h, 0:W], ps[h][:, 0:W], ACT.Copy)
                    A_(OQ[:, h, 0:W], ps[h][:, 0:W], ACT.Square).then_inc(S("g_sq"), 1)
                for h in range(4):
                    act.wait_ge(S("g_sum"), 4 * l + h + 1)
                    rsqrt(OQ[:, h, 0:W], ps[4 + h][:, 0:W], P).then_inc(S("g_inverse"), 1)
                phase_end(act, f"l{l}_gb")

                act.wait_ge(S("w_out_added"), 8 * (l + 1))
                norm(ncall)
                ncall += 1
                phase_end(act, f"l{l}_out")

                with act.Fori(0, 4) as i:
                    for u in range(2):
                        n, turns, chunks, back = mlp_chunks(l, u, 0, i)
                        act.wait_ge(full[n % RING], 16 * (n // RING + 1) + turns)
                        act.wait_ge(used, n - back + 1 + chunks)
                        A_(W1h, slot(n), ACT.Copy).then_inc(S("w1_high"), 1)
                        n, turns, chunks, back = mlp_chunks(l, u, 1, i)
                        act.wait_ge(full[n % RING], 16 * (n // RING + 1) + turns)
                        act.wait_ge(used, n - back + 1 + chunks)
                        A_(W2h, slot(n), ACT.Copy).then_inc(S("w2_high"), 1)
                        for nt in range(4):
                            n = 32 * l + (i * 2 + u) * 4 + nt + 1
                            act.wait_ge(S("hid_mm"), n)
                            A_(HA[:, nt, 0:W], ps[nt][:, 0:W], ACT.Relu).then_inc(S("hid_relu"), 1)
                            act.wait_ge(S("hid_relu"), n)
                            A_(HAh[:, nt, 0:W], HA[:, nt, 0:W], ACT.Square)
                            A_(HA[:, nt, 0:W], HA[:, nt, 0:W], ACT.Square).then_inc(S("hid_square"), 1)
                        if l == 0:
                            for a in range(2):
                                ada_rows(24 + i * 4 + u * 2 + a, a, ADA_COLS)
                if l == 1:
                    act.wait_ge(S("mlp_bank_free"), 66 * 2)
                    norm(ncall)
                phase_end(act, f"l{l}_mlp")

        @block.gpsimd
        def _(pool):
            G = nc.gpsimd

            def bring(dst, src, sem):
                pool.dma_start(dst, src).then_inc(S(sem), 16)

            tall = lambda a: a.rearrange("(k p) n -> p k n", p=P)
            bring(vecs[:, :], T["vecs"], "vecs_in")
            bring(base[:, :], T["base"], "base_in")
            bring(A(15360, 4096), T["hy"], "filter_in")
            bring(f_z[0:33, :], T["hy_z"], "filter_in")
            bring(f_w1[0:33, :], T["hy_filt_w1"], "filter_in")
            bring(f_w2[0:64, :], T["hy_filt_w2"], "filter_in")
            bring(f_w3[0:64, :], T["hy_filt_w3"], "filter_in")
            bring(X[:, :, 0:L], tall(T["x"]), "x_in")
            bring(X[:, :, L:2 * L], tall(T["ctx"]), "x_in")
            bring(A3(0, KT, L), tall(T["pos"]), "x_in")
            bring(hmask[:, :, :], T["hg_mask"].rearrange("p (a b) -> p a b", a=2), "x_in")
            for name in ("filters", "projected", "scan_f", "scan_b"):
                phase_end(pool, name)
                if name == "projected":
                    bring(X[:, :, L:2 * L], tall(T["ctx_2"]), "ctx2_in")
            bring(A(15360, 2048), T["hy"][:, 0:2048], "hy_in")
            phase_end(pool, "hyena")
            phase_end(pool, "merged")
            bring(mtab, T["moe"], "moe_in")
            bring(WR, tall(T["wr"]), "moe_in")
            bring(b2t, T["b2"], "b2_in")
            bring(gmask, T["b2_mask"].rearrange("p (a b) -> p a b", a=2), "b2_in")
            for l in range(LAYERS):
                bring(GUP[0:32, :, :], T["gup"][l].rearrange("d r n -> r d n"), "b2_in")
                phase_end(pool, "experts" if l == 0 else "l0_mlp")
                W = 2 * L if l == 0 else L
                for name in ("in", "ret", "gf", "gb", "out"):
                    phase_end(pool, f"l{l}_{name}")
                with pool.Fori(0, 4) as i:
                    for u in range(2):
                        j = i * 2 + u
                        pool.wait_ge(S("w1_high"), 8 * l + j + 1)
                        n = mlp_chunks(l, u, 0, i)[0]
                        G.tensor_tensor(low(n), slot(n), W1h.bitcast(F32), ALU.subtract).then_inc(S("w1_split"), 1)
                        for nt in range(4):
                            pool.wait_ge(S("hid_square"), 32 * l + j * 4 + nt + 1)
                            G.tensor_tensor(HAl[:, nt, 0:W], HA[:, nt, 0:W], HAh[:, nt, 0:W].bitcast(F32), ALU.subtract)\
                                .then_inc(S("hid_out"), 1)
                if l:
                    phase_end(pool, "l1_mlp")

        @block.vector
        def _(dve):
            V = nc.vector
            own = [0]

            def link(ins):
                own[0] += 1
                ins.then_inc(S("dve_own"), 1)
                dve.wait_ge(S("dve_own"), own[0])

            def bc(ap, shape):
                return ap.broadcast_to(shape)

            def take_chunk(b, g, par, c0, ncols=512):
                dve.wait_ge(S("ada_turned"), g + 1)
                m = ncols // P
                lo = VOFF["ada_b" if b == 0 else "ada_b2"][0] + (48 if b == 2 else 0)
                V.tensor_tensor(mod[:, b, bass.ds(c0, m), :], ps[6 + par][:, 0:2 * m].rearrange("p (a b) -> p a b", b=2),
                                bc(vecs[:, bass.ds(c0 + lo, m)].unsqueeze(2), [P, m, 2]), ALU.add).then_inc(S("ada_out"), 1)

            def gains(b):
                for w in range(2):
                    g = vec(("n1", "n1_2", "n1_2")[b] if w == 0 else ("n2", "n2_2", "n2_2")[b], 8 if b == 2 else 0, 8)
                    link(V.scalar_tensor_tensor(gsc[:, b, w], mod[:, b, 24 * w + 8:24 * w + 16, :], 1.0,
                                                bc(g.unsqueeze(2), [P, KT, 2]), ALU.add, ALU.mult))

            def norm(call):
                N = CALLS[call][2]
                dve.wait_ge(S("rms_ready"), call + 1)
                for a in range(2):
                    V.tensor_tensor(H[:, 4 * a:4 * a + 4, 0:N], X[:, 4 * a:4 * a + 4, 0:N],
                                    bc(RS[:, 0:N].unsqueeze(1), [P, 4, N]), ALU.mult).then_inc(S("scaled"), 1)

            def two(ap):
                return ap.rearrange("p (a b) -> p a b", a=2)

            dve.wait_ge(S("vecs_in"), 16)
            link(V.tensor_tensor(lbc[:, 0:8], vec("lb", 0, 8), vec("lb", 8, 8), ALU.max))
            V.tensor_tensor(lbc[:, 8:16], vec("lb", 0, 8), lbc[:, 0:8], ALU.subtract)
            V.tensor_tensor(lbc[:, 16:24], vec("lb", 8, 8), lbc[:, 0:8], ALU.subtract).then_inc(S("lb_arg"), 1)
            for k in range(2):
                dve.drain().then_inc(S("ada_out"), 1)
            TWO_PI, ROUND = 2 * np.pi, 12582912.0
            HI = 6.28125
            for i in range(2):
                dve.wait_ge(S("filt_mm"), i + 1)
                a, k = f_t[0:64, :], f_nat[0:64, 0, 0:L]
                if i:
                    dve.wait_ge(S("filt_sin"), 1)
                f = vec("f1" if i == 0 else "f2", 0, 2)
                link(V.tensor_scalar(a, ps[0][0:64, i * L:(i + 1) * L], f[0:64, 0:1], f[0:64, 1:2], ALU.add, ALU.mult))
                link(V.tensor_scalar(k, a, 1.0 / TWO_PI, ROUND, ALU.mult, ALU.add))
                link(V.tensor_scalar(k, k, ROUND, None, ALU.subtract))
                link(V.scalar_tensor_tensor(a, k, -HI, a, ALU.mult, ALU.add))
                link(V.scalar_tensor_tensor(a, k, -(TWO_PI - HI), a, ALU.mult, ALU.add))
                V.tensor_scalar(a, a, 3.1415925, -3.1415925, ALU.min, ALU.max).then_inc(S("filt_arg"), 1)
                take_chunk(0, i, i, 4 * i)
            for d in range(2):
                dve.wait_ge(S("filt_nat"), d + 1)
                for tb in range(2):
                    i = V.tensor_tensor(f_nat[:, tb, :], f_dec[:, tb, :], ps[1 + tb][:, :], ALU.mult)
                i.then_inc(S("filt_dec"), 1)
                take_chunk(0, 2 + d, d, 8 + 4 * d)
            with dve.Fori(1, 3) as i:
                for u in range(RING):
                    take_chunk(0, i * RING + u, u % 2, (i * RING + u) * 4)
            dve.wait_ge(S("x_in"), 16 * 4)
            dve.wait_ge(S("base_in"), 16)
            V.tensor_tensor(X[:, :, 0:L], X[:, :, 0:L], A3(0, KT, L), ALU.add)
            dve.wait_ge(S("lb_exp"), 1)
            link(V.tensor_tensor(lbc[:, 0:8], lbc[:, 8:16], lbc[:, 16:24], ALU.add))
            link(V.reciprocal(lbc[:, 0:8], lbc[:, 0:8]))
            link(V.tensor_tensor(lbc[:, 24:32], lbc[:, 8:16], lbc[:, 0:8], ALU.mult))
            V.tensor_scalar(lbc[:, 32:40], lbc[:, 24:32], -1.0, 1.0, ALU.mult, ALU.add)
            dve.wait_ge(S("ada_out"), 14)
            gains(0)
            phase_end(dve, "filters")
            norm(0)

            def scan_prep(d):
                dve.wait_ge(S("lf_ready"), d + 1)
                for h in range(HG_H):
                    V.tensor_scalar(K2[d][:, h, :], K2[d][:, h, :], lbc[:, 32 + 4 * d + h:33 + 4 * d + h], None, ALU.mult)
                one = bc(ones[:, 0:1], [P, L])
                for h in range(HG_H):
                    lc, o, lx = LC[d][:, h, :], KM[:, h, :], LX[d][:, h, :]
                    if d == 0:
                        V.tensor_tensor_scan(o[:, ::-1], one, lc[:, ::-1], 0.0, ALU.mult, ALU.add)
                        i = V.tensor_tensor_scan(lx, r32[0], lx, 0.0, ALU.mult, ALU.add)
                    else:
                        V.tensor_tensor_scan(o, one, lc, 0.0, ALU.mult, ALU.add)
                        i = V.tensor_tensor_scan(lx[:, ::-1], r32[1][:, ::-1], lx[:, ::-1], 0.0, ALU.mult, ALU.add)
                link(i)
                V.tensor_tensor(KM, KM, LC[d], ALU.subtract).then_inc(S("ctx_arg"), 1)
                v = lambda a: a.rearrange("p h (c k) -> p h c k", k=HG_C)
                mid, end = (16, 31) if d == 0 else (15, 0)
                for h in range(HG_H):
                    B = LX[d][:, h, :].rearrange("p (c k) -> p c k", k=HG_C)
                    m = bc(B[:, :, mid:mid + 1], [P, 8, HG_C])
                    e = bc(B[:, :, end:end + 1], [P, 8, HG_C])
                    V.tensor_tensor(QM[:, h, :].rearrange("p (c k) -> p c k", k=HG_C), B, m, ALU.subtract)
                    i = V.tensor_tensor(QD[:, h, :].rearrange("p (c k) -> p c k", k=HG_C), e, B, ALU.subtract)
                link(i)
                dve.wait_ge(S("ctx_exp"), d + 1)
                V.tensor_tensor(KC[d], KC[d], KM, ALU.mult).then_inc(S("kd_ready"), 1)
                dve.wait_ge(S("kd_ready"), d + 1)
                dve.drain().then_inc(S("hg_arg"), 1)
                dve.wait_ge(S("hg_exp"), d + 1)
                V.tensor_tensor(KM, KM, KX[d], ALU.mult)
                V.tensor_tensor(QM, QM, Qt, ALU.mult).then_inc(S("qm_ready"), 1)
                dve.wait_ge(S("qm_ready"), d + 1)
                V.tensor_tensor(KX[d], KX[d], QD, ALU.mult).then_inc(S("ke_ready"), 1)
                dve.wait_ge(S("hg_exp2"), d + 1)
                link(V.tensor_tensor(QD, QD, Qt, ALU.mult))

            for j in range(4):
                take_chunk(1, 12 + j, j % 2, 4 * j)
            scan_prep(0)
            link(V.memset(SC, 0.0))
            for j in range(4, 8):
                take_chunk(1, 12 + j, j % 2, 4 * j)
            phase_end(dve, "projected")

            for d in range(2):
                if d == 1:
                    link(V.memset(SC, 0.0))
                    scan_prep(1)
                dve.wait_ge(S("ctx_state"), d + 1)
                V.tensor_copy(ST[:, 0, :], ps[0][:, :]).then_inc(S("states_out"), 1)
                for tb in range(2):
                    dve.wait_ge(S("scores"), 2 * d + tb + 1)
                    V.copy_predicated(SC[:, tb * 4:tb * 4 + 4, :], bc(hmask[:, d, :].unsqueeze(1), [P, 4, P]),
                                      ps[6 + tb][:, :].rearrange("p (a b) -> p a b", a=4)).then_inc(S("masked"), 1)
                for n in range(7):
                    ch = n if d == 0 else 7 - n
                    dve.wait_ge(S("updates"), 2 * d + n // 4 + 1)
                    dve.wait_ge(S("states_out"), 8 * d + n + 1)
                    if n + 1 >= 4:
                        dve.wait_ge(S("inter"), 8 * d + n - 2)
                    o, s = [ST[:, k % 4, :].rearrange("p (h v) -> p h v", h=4) for k in (n + 1, n)]
                    e = et[:, 0:32].rearrange("p (h c) -> p h c", h=4)[:, :, ch:ch + 1]
                    link(V.tensor_tensor(o, s, bc(e, [P, 4, P]), ALU.mult))
                    V.tensor_tensor(o, o, ps[ch % 4][:, :].rearrange("p (h v) -> p h v", h=4), ALU.add).then_inc(S("states_out"), 1)
                phase_end(dve, "scan_f" if d == 0 else "scan_b")

            for j in range(8, 12):
                take_chunk(1, 12 + j, j % 2, 4 * j)
            for i in range(12):
                link(V.tensor_scalar(CV[:, i, :], HYt[:, i, :], vec("conv_w", 12 + i), vec("conv_b", i), ALU.mult, ALU.add))
                link(V.scalar_tensor_tensor(CV[:, i, 1:L], HYt[:, i, 0:L - 1], vec("conv_w", i), CV[:, i, 1:L], ALU.mult, ALU.add))
                link(V.scalar_tensor_tensor(CV[:, i, 0:L - 1], HYt[:, i, 1:L], vec("conv_w", 24 + i), CV[:, i, 0:L - 1], ALU.mult, ALU.add))
            V.tensor_tensor(UV, CV[:, 0:4, :], CV[:, 4:8, :], ALU.mult).then_inc(S("uv_ready"), 1)
            dve.wait_ge(S("o_inverse"), 1)
            link(V.tensor_tensor(OS, OS, ORS, ALU.mult))
            link(V.scalar_tensor_tensor(OS, OS, vec("hg_g"), Gt, ALU.mult, ALU.mult))
            dve.wait_ge(S("ada_out"), 2 + 24)
            gains(1)
            dve.wait_ge(S("u_spec"), 1)
            for f in range(2):
                re, im = ps[f][:, :], ps[2 + f][:, :]
                V.tensor_tensor(YF[:, f, :], KS[:, f, :], re, ALU.mult)
                V.tensor_tensor(UT[:, 0, :], KS[:, 2 + f, :], im, ALU.mult)
                V.tensor_tensor(YF[:, 2 + f, :], KS[:, 2 + f, :], re, ALU.mult)
                link(V.tensor_tensor(UT[:, 1, :], KS[:, f, :], im, ALU.mult))
                V.tensor_tensor(YF[:, f, :], YF[:, f, :], UT[:, 0, :], ALU.subtract)
                link(V.tensor_tensor(YF[:, 2 + f, :], YF[:, 2 + f, :], UT[:, 1, :], ALU.add))
            V.tensor_tensor(YF[0:1, 0, :], KS[0:1, 0, :], ps[0][0:1, :], ALU.mult)
            V.tensor_tensor(YF[0:1, 2, :], KS[0:1, 2, :], ps[2][0:1, :], ALU.mult).then_inc(S("y_spec"), 1)
            dve.wait_ge(S("y_time"), 1)
            for c in range(HYT):
                i = V.scalar_tensor_tensor(UV[:, c, :], UV[:, c, :], vec("hy_d", c), ps[4 + c // 2][:, (c % 2) * L:(c % 2 + 1) * L],
                                           ALU.mult, ALU.add)
            link(i)
            link(V.tensor_tensor(YB, UV, CV[:, 8:12, :], ALU.mult))
            phase_end(dve, "hyena")

            for nt in range(KT):
                dve.wait_ge(S("merge_mm"), nt + 1)
                o = ps[nt % 4]
                V.tensor_tensor(MIX[:, nt, :], GL[:, nt, :], o[:, 0:L], ALU.mult)
                link(V.tensor_tensor(MT[:, nt, :], GL[:, 8 + nt, :], o[:, L:2 * L], ALU.mult))
                V.tensor_tensor(MIX[:, nt, :], MIX[:, nt, :], MT[:, nt, :], ALU.add).then_inc(S("merged"), 1)
            for t in range(KT):
                dve.wait_ge(S("out_mm"), t + 1)
                V.scalar_tensor_tensor(X[:, t, 0:L], ps[4 + t % 2][:, 0:L], mod[:, 0, 16 + t, 0:1], X[:, t, 0:L],
                                       ALU.mult, ALU.add).then_inc(S("out_added"), 1)
            phase_end(dve, "merged")

            norm(1)
            V.memset(SW, 0.0).then_inc(S("sw_zero"), 1)
            V.memset(RKM[:, :, NX:NX + 4], -1.0)
            V.memset(CMB[:, :, NX:NX + 4], 0.0)
            dve.wait_ge(S("logits"), 1)
            link(V.tensor_tensor(LG, ps[4][:, 0:2 * NR].rearrange("p (a b) -> p a b", a=2),
                                 bc(vec("rbias", 0, NR).unsqueeze(1), [P, TB, NR]), ALU.add))

            def r3(off, n):
                return RT[:, off:off + 2 * n].rearrange("p (a b) -> p a b", a=2)

            def onehot_of_max(x, n, mx, cum, oh):
                link(V.tensor_reduce(mx, x, AX.X, ALU.max))
                link(V.tensor_tensor(oh, x, bc(mx, [P, TB, n]), ALU.is_equal))
                for b in range(TB):
                    i = V.tensor_tensor_scan(cum[:, b, :], bc(ones[:, 0:1], [P, n]), oh[:, b, :], 0.0, ALU.mult, ALU.add)
                link(i)
                link(V.scalar_tensor_tensor(oh, cum, 1.0, oh, ALU.is_equal, ALU.mult))

            gm, gcum, goh = r3(0, 1), r3(24, 4), r3(32, 4)
            gl_ = LG[:, :, 0:NG]
            onehot_of_max(gl_, NG, gm, gcum, goh)
            V.tensor_tensor(r3(16, 4), gl_, bc(gm, [P, TB, NG]), ALU.subtract).then_inc(S("rt_arg"), 1)
            prod = RT[:, 48:112].rearrange("p (b g e) -> p b g e", b=TB, g=NG)
            for b in range(TB):
                i = V.tensor_tensor(prod[:, b], LG[:, b, NG:NR].rearrange("p (g e) -> p g e", g=NG),
                                    bc(goh[:, b, :].unsqueeze(2), [P, NG, NE]), ALU.mult)
            link(i)
            el = r3(112, NE)
            for b in range(TB):
                i = V.tensor_reduce(el[:, b, :], prod[:, b].rearrange("p g e -> p e g"), AX.X, ALU.add)
            link(i)
            m1, c1, o1 = r3(128, 1), r3(130, NE), r3(146, NE)
            m2, c2, o2, el2 = r3(162, 1), r3(164, NE), r3(180, NE), r3(220, NE)
            onehot_of_max(el, NE, m1, c1, o1)
            link(V.scalar_tensor_tensor(el2, o1, -1e30, el, ALU.mult, ALU.add))
            onehot_of_max(el2, NE, m2, c2, o2)
            ex = r3(200, 1)
            V.tensor_tensor(ex, m2, m1, ALU.subtract).then_inc(S("rt_arg"), 1)
            dve.wait_ge(S("rt_exp"), 2)
            zs, one_e, w1, w2 = r3(240, 1), r3(242, 1), r3(244, 1), r3(246, 1)
            V.tensor_reduce(zs, r3(16, 4), AX.X, ALU.add)
            link(V.tensor_scalar(one_e, ex, 1.0, None, ALU.add))
            link(V.tensor_tensor(zs, zs, one_e, ALU.mult))
            link(V.reciprocal(w1, zs))
            link(V.tensor_tensor(w2, w1, ex, ALU.mult))
            s8, c8, t8 = r3(250, NE), r3(266, NE), r3(282, NE)
            V.tensor_tensor(s8, o1, o2, ALU.add)
            V.tensor_tensor(c8, o1, bc(w1, [P, TB, NE]), ALU.mult)
            link(V.tensor_tensor(t8, o2, bc(w2, [P, TB, NE]), ALU.mult))
            link(V.tensor_tensor(c8, c8, t8, ALU.add))
            for b in range(TB):
                ohb = bc(goh[:, b, :].unsqueeze(2), [P, NG, NE])
                V.tensor_tensor(CMB[:, b, 0:NX].rearrange("p (g e) -> p g e", g=NG), bc(c8[:, b:b + 1, :], [P, NG, NE]), ohb, ALU.mult)
                i = V.tensor_tensor(SELX[:, b, :].rearrange("p (g e) -> p g e", g=NG), bc(s8[:, b:b + 1, :], [P, NG, NE]), ohb, ALU.mult)
            i.then_inc(S("selected"), 1)
            dve.wait_ge(S("ranks"), 1)
            dve.wait_ge(S("selected"), 1)
            link(V.scalar_tensor_tensor(RKM[:, :, 0:NX], ps[5][:, 0:2 * NX].rearrange("p (a b) -> p a b", a=2), 1.0, SELX, ALU.add, ALU.mult))
            link(V.tensor_scalar(RKM[:, :, 0:NX], RKM[:, :, 0:NX], -1.0, None, ALU.add))
            cnt, over = RT[0:1, 300:301], RT[0:1, 301:304]
            link(V.tensor_reduce(cnt, ps[5][0:1, 2 * NX:3 * NX], AX.X, ALU.max))
            for k in range(3):
                i = V.tensor_scalar(over[:, k:k + 1], cnt, float(CAP * (k + 1)), None, ALU.is_gt)
            link(i)
            link(V.tensor_reduce(RT[0:1, 304:305], over, AX.X, ALU.add))
            V.tensor_copy(npass[0:1, 0:1], RT[0:1, 304:305]).then_inc(S("passes_known"), 1)

            def onehots(e, buf, pair, half, sem, also=None):
                for tb in range(TB):
                    i = V.tensor_scalar(SGv[:, buf, tb, :], IOTA, RKM[:, tb, bass.ds(e, 1)], None, ALU.is_equal)
                if sem:
                    i.then_inc(S(sem), 1)
                for tb in range(TB):
                    i = V.tensor_scalar(SWv[:, pair, tb, half * CAP:(half + 1) * CAP], IOTA, RKM[:, tb, bass.ds(e, 1)],
                                        CMB[:, tb, bass.ds(e, 1)], ALU.is_equal, ALU.mult)
                if also:
                    i.then_inc(S(also), 1)

            dve.wait_ge(S("cleared"), 1)
            onehots(0, 0, 0, 0, "onehot")
            with dve.Fori(0, NX // 4) as i:
                for u in range(4):
                    v = u + 1
                    onehots(i * 4 + v, v % 2, (v // 2) % 2, v % 2, "onehot", "pair_weights" if v % 2 else None)
                    dve.wait_ge(S("silu"), i * 4 + u + 1)
                    V.tensor_tensor(HID, SIL, ps[5][:, 256:512].rearrange("p (a b) -> p a b", a=FT), ALU.mult).then_inc(S("hidden"), 1)
                    if u % 2:
                        dve.wait_ge(S("weights_turned"), i * 2 + u // 2 + 1)
                        V.tensor_copy(SWT, ps[4][:, 0:L]).then_inc(S("weights_out"), 1)
            dve.wait_ge(S("passes_known"), 1)
            more = dve.value_load(npass[0:1, 0:1])
            with dve.If(more > 0):
                with dve.Fori(0, more) as q:
                    dve.wait_ge(S("over_begun"), q * NX + 1)
                    V.tensor_scalar(RKM, RKM, -float(CAP), None, ALU.add).then_inc(S("over_ranked"), 1)
                    with dve.Fori(0, NX) as e:
                        g = q * NX + e
                        dve.wait_ge(S("over_ranked"), q + 1)
                        dve.wait_ge(S("over_begun"), g + 1)
                        onehots(e, 0, 0, 0, None, "over_onehot")
                        dve.wait_ge(S("over_silu"), g + 1)
                        V.tensor_tensor(HID, SIL, ps[5][:, 256:512].rearrange("p (a b) -> p a b", a=FT), ALU.mult).then_inc(S("over_hidden"), 1)
                        dve.wait_ge(S("over_turned"), g + 1)
                        V.tensor_copy(SWT[0:CAP, :], ps[4][0:CAP, 0:L]).then_inc(S("over_weights"), 1)
            dve.wait_ge(S("experts_done"), 1)
            for k in range(KT):
                i = V.scalar_tensor_tensor(X[:, k, 0:L], ps[k // 2][:, (k % 2) * L:(k % 2 + 1) * L], mod[:, 0, 40 + k, 0:1], X[:, k, 0:L],
                                           ALU.mult, ALU.add)
            i.then_inc(S("experts_added"), 1)
            dve.wait_ge(S("experts_added"), 1)
            norm(2)
            phase_end(dve, "experts")

            ncall = 3
            for l in range(LAYERS):
                W = 2 * L if l == 0 else L
                norm(ncall)
                ncall += 1
                dve.wait_ge(S("lgam"), l + 1)
                dve.wait_ge(S("b2_in"), 16 * (3 + l))
                for k in range(4):
                    i = V.tensor_scalar(lgam[:, 8 + 4 * k:12 + 4 * k], lgam[:, 4 * (k // 2):4 * (k // 2) + 4], COLT[:, k:k + 1], None, ALU.mult)
                i.then_inc(S("col_arg"), 1)
                for m, M in enumerate((RQ, RK)):
                    for a in range(2):
                        dve.wait_ge(S("swapped"), 4 * l + 2 * m + a + 1)
                        i = V.tensor_tensor(ROT[:, 2 * a:2 * a + 2, :], bc(RSIN.unsqueeze(1), [P, 2, L]),
                                            ps[4 + 2 * m + a][:, :].rearrange("p (a b) -> p a b", a=2), ALU.mult)
                    link(i)
                    link(V.tensor_tensor(M[:, :, 0:L], M[:, :, 0:L], bc(RCOS.unsqueeze(1), [P, 4, L]), ALU.mult))
                    link(V.tensor_tensor(M[:, :, 0:L], M[:, :, 0:L], ROT, ALU.add))
                phase_end(dve, f"l{l}_in")

                def head_prep(h):
                    c = l * RT_H + h
                    b = h % 2
                    if h >= 2:
                        dve.wait_ge(S("r_head"), c - 1)
                    lf, lb_ = lgam[:, h:h + 1], lgam[:, 4 + h:5 + h]
                    link(V.tensor_scalar(Wd[b], EF, lf, None, ALU.mult))
                    V.scalar_tensor_tensor(Wd[b], EB, lb_, Wd[b], ALU.mult, ALU.add)
                    V.tensor_scalar(RQD[b][:, 0, :], ROWT[0], lf, None, ALU.mult)
                    V.tensor_scalar(RQD[b][:, 1, :], ROWT[1], lb_, None, ALU.mult).then_inc(S("r_arg"), 1)
                    for d in range(2):
                        for tb in range(2):
                            k = 8 + (2 * d + tb) * 4 + h
                            V.tensor_scalar(RVD[b][:, d, tb, :], RV[:, 2 + tb, h * P:(h + 1) * P], lgam[:, k:k + 1], None, ALU.mult)
                    dve.wait_ge(S("r_exp"), c + 1)
                    V.tensor_tensor(RQD[b], RQD[b], bc(RQ[:, h, 0:L].unsqueeze(1), [P, 2, L]), ALU.mult).then_inc(S("r_prep"), 1)

                dve.wait_ge(S("col_exp"), l + 1)
                head_prep(0)
                for h in range(RT_H):
                    c = l * RT_H + h
                    if h < RT_H - 1:
                        head_prep(h + 1)
                    for side in ((0, 1) if l == 0 else (0,)):
                        q = c * 2 + side if l == 0 else 2 * RT_H + h
                        dve.wait_ge(S("r_scores"), q + 1)
                        V.tensor_tensor(RSC[side], Wd[h % 2], ps[6 + side][:, :].rearrange("p (a b) -> p a b", a=2), ALU.mult)\
                            .then_inc(S("r_decayed"), 1)
                for h in range(RT_H):
                    dve.wait_ge(S("r_mean"), l * 4 + h + 1)
                    V.scalar_tensor_tensor(OB[:, h, 0:W], ps[4 + h][:, 0:W], -1.0 / P, OB[:, h, 0:W], ALU.mult, ALU.add).then_inc(S("r_centred"), 1)
                for h in range(RT_H):
                    dve.wait_ge(S("r_inverse"), l * 4 + h + 1)
                    link(V.tensor_tensor(OB[:, h, 0:W], OB[:, h, 0:W], OQ[:, h, 0:W], ALU.mult))
                    V.tensor_tensor(YT[:, h, 0:W], YT[:, h, 0:W], OB[:, h, 0:W], ALU.mult)
                phase_end(dve, f"l{l}_ret")

                nx = 4 if l == 0 else 2
                for d in range(2):
                    g = 2 * l + d
                    i = V.memset(GSC, 0.0)
                    if d == 0:
                        i.then_inc(S("gsc_clear"), 1)
                    dve.wait_ge(S("g_soft"), g + 1)
                    link(V.scalar_tensor_tensor(GLg, GT1, 0.0, GT2, ALU.min, ALU.subtract))
                    for t in range(2):
                        lg, r = GLg[:, t, :], R128[d]
                        if d:
                            lg, r = lg[:, ::-1], r[:, ::-1]
                        i = V.tensor_tensor_scan(lg, r, lg, 0.0, ALU.mult, ALU.add)
                    link(i)
                    v = lambda a: a.rearrange("p t (c k) -> p (t c) k", k=P)
                    mid, end = (63, 127) if d == 0 else (64, 0)
                    V.tensor_tensor(v(GT1), v(GLg), bc(v(GLg)[:, :, mid:mid + 1], [P, 8, P]), ALU.subtract)
                    V.tensor_tensor(v(GT2), bc(v(GLg)[:, :, end:end + 1], [P, 8, P]), v(GLg), ALU.subtract).then_inc(S("g_arg"), 1)
                    dve.wait_ge(S("g_exp"), 3 * g + 1)
                    V.tensor_tensor(GKE, GKE, GK, ALU.mult).then_inc(S("gke_ready"), 1)
                    dve.wait_ge(S("g_exp"), 3 * g + 2)
                    V.tensor_tensor(GKM, GKM, GK, ALU.mult)
                    V.tensor_tensor(GQM[:, :, 0:W], GQM[:, :, 0:W], GQ[:, :, 0:W], ALU.mult).then_inc(S("gqm_ready"), 1)
                    dve.wait_ge(S("g_exp"), 3 * g + 3)
                    link(V.tensor_tensor(GQD[:, :, 0:W], GQD[:, :, 0:W], GQ[:, :, 0:W], ALU.mult))
                    for ch in range(nx):
                        dve.wait_ge(S("g_scores"), (0, 4, 8, 10)[g] + (ch | 1) + 1)
                        for par in range(2):
                            V.copy_predicated(GSC[:, par * 8 + ch * 2:par * 8 + ch * 2 + 2, :], bc(gmask[:, d, :].unsqueeze(1), [P, 2, P]),
                                              ps[6 + par][:, (ch % 2) * 2 * P:(ch % 2 + 1) * 2 * P].rearrange("p (a b) -> p a b", a=2))\
                                .then_inc(S("g_masked"), 1)
                    order = [2, 3, 0, 1] if d == 0 else [3, 2, 1, 0]
                    for n in range(3):
                        dve.wait_ge(S("g_update"), 3 * g + max(n + 1, 2))
                        U = ps[4 + n // 2][:, (n % 2) * L:(n % 2 + 1) * L].rearrange("p (t v) -> p t v", t=2)
                        if n == 0:
                            V.tensor_copy(GST[:, 0], U).then_inc(S("g_state"), 1)
                            continue
                        dve.wait_ge(S("g_state"), 3 * g + n)
                        e = et[:, 32:40].rearrange("p (t c) -> p t c", t=2)[:, :, order[n]:order[n] + 1]
                        link(V.tensor_tensor(GST[:, n], GST[:, n - 1], bc(e, [P, 2, P]), ALU.mult))
                        V.tensor_tensor(GST[:, n], GST[:, n], U, ALU.add).then_inc(S("g_state"), 1)
                    if d == 0:
                        phase_end(dve, f"l{l}_gf")
                for h in range(4):
                    dve.wait_ge(S("g_inverse"), 4 * l + h + 1)
                    link(V.tensor_tensor(OB[:, h, 0:W], OB[:, h, 0:W], OQ[:, h, 0:W], ALU.mult))
                    V.scalar_tensor_tensor(YT[:, 4 + h, 0:W], OB[:, h, 0:W], vec("gla_g", l), YT[:, 4 + h, 0:W], ALU.mult, ALU.mult)
                phase_end(dve, f"l{l}_gb")

                def add(t, o, gate):
                    for s in range(W // L):
                        i = V.scalar_tensor_tensor(X[:, t, s * L:(s + 1) * L], o[:, s * L:(s + 1) * L], mod[:, 1 + l, gate + t, s:s + 1],
                                                   X[:, t, s * L:(s + 1) * L], ALU.mult, ALU.add)
                    return i

                for t in range(KT):
                    dve.wait_ge(S("w_out_mm"), 8 * l + t + 1)
                    add(t, ps[t % 4], 16).then_inc(S("w_out_added"), 1)
                norm(ncall)
                ncall += 1
                for k in range(2):
                    dve.drain().then_inc(S("mlp_bank_free"), 1)
                for k in range(KT):
                    dve.wait_ge(S("normed"), 48 + 2 * k + 2 if l == 0 else 80 + k + 1)
                    link(V.tensor_copy(Hh[:, k, 0:W], H[:, k, 0:W]))
                    i = V.tensor_tensor(Hl[:, k, 0:W], H[:, k, 0:W], Hh[:, k, 0:W].bitcast(F32), ALU.subtract)
                i.then_inc(S("h_split"), 1)
                phase_end(dve, f"l{l}_out")

                with dve.Fori(0, 4) as i:
                    for u in range(2):
                        dve.wait_ge(S("w2_high"), 8 * l + i * 2 + u + 1)
                        n = mlp_chunks(l, u, 1, i)[0]
                        V.tensor_tensor(low(n), slot(n), W2h.bitcast(F32), ALU.subtract).then_inc(S("w2_split"), 1)
                        if l == 0:
                            c = i * 4 + u * 2
                            take_chunk(2, 24 + c, 0, c * 3, ADA_COLS)
                        for t in range(KT):
                            dve.wait_ge(S("mlp_mm"), 64 * l + (i * 2 + u) * 8 + t + 1)
                            add(t, ps[4 + t % 2], 40).then_inc(S("mlp_bank_free"), 1)
                        if l == 0:
                            take_chunk(2, 24 + c + 1, 1, (c + 1) * 3, ADA_COLS)
                if l == 0:
                    dve.wait_ge(S("ada_out"), 2 + 40)
                    gains(2)
                else:
                    norm(ncall)
                    dve.wait_ge(S("normed"), 96)
                phase_end(dve, f"l{l}_mlp")


_OUTS = [((1, L, D), "float32")]


def kernel(**inputs):
    import concourse.bacc as _bacc
    from concourse.bass_utils import run_bass_kernel_spmd as _run

    I = {k: np.asarray(v) for k, v in inputs.items()}
    nc = _bacc.Bacc("TRN2", target_bir_lowering=False, num_devices=1)
    arrays = dict(tables())
    for name in ("x", "ctx", "ctx_2"):
        arrays[name] = np.ascontiguousarray(I[name][0].T)
    for name in ("ada_w", "w_in", "w_proj_a", "w_proj_b", "w_out", "hy_filt_w1", "hy_filt_w2", "hy_filt_w3"):
        arrays[name] = I[name][0]
    for name in ("moe_w_gate", "moe_w_up", "moe_w_down"):
        a = I[name]
        arrays[name] = a.reshape(NX, *a.shape[3:])
    for name in ("ada_w_2", "w_in_2", "w_out_2", "w_mlp1_2", "w_mlp2_2"):
        arrays[name] = I[name]
    arrays["wr"] = np.concatenate([I["moe_router_g_w"][0], I["moe_router_e_w"][0].transpose(1, 0, 2).reshape(D, NX)], axis=1)
    gup = np.zeros((LAYERS, 2, 2 * RANK, GL_H * GL_K), np.float32)
    gup[:, 0, 0:RANK] = I["gla_gate_up_2"][:, 0]
    gup[:, 1, RANK:] = I["gla_gate_up_2"][:, 1]
    arrays["gup"] = gup

    def pad(*vs):
        a = np.zeros((P, len(vs)), np.float32)
        for n, v in enumerate(vs):
            a[0:v.size, n] = v.reshape(-1)
        return a

    def spread(v):
        return np.broadcast_to(v.reshape(1, -1), (P, v.size))

    parts = {
        "ada_b": columns(I["ada_b"]), "n1": columns(I["norm1_g"]), "n2": columns(I["norm2_g"]), "lb": columns(I["hgrn_lb"]),
        "hg_g": columns(I["hgrn_norm_g"]), "conv_w": columns(I["hy_conv_w"]), "conv_b": columns(I["hy_conv_b"]),
        "hy_d": columns(I["hy_d"]), "fin": columns(I["final_norm_g"]), "ada_b2": columns(I["ada_b_2"]),
        "n1_2": columns(I["norm1_g_2"]), "n2_2": columns(I["norm2_g_2"]), "gla_g": columns(I["gla_norm_g_2"]),
        "gate_b": columns(I["gla_gate_b_2"]), "fin2": columns(I["final_g_2"]),
        "c1": np.concatenate([columns(I["c"]), columns(I["c_ctx"])], axis=1),
        "c2": np.concatenate([columns(I["c_2"]), columns(I["c_ctx_2"])], axis=1),
        "decay": spread(I["ret_decay_2"]),
        "rbias": np.concatenate([spread(I["moe_router_g_b"]), spread(I["moe_router_e_b"])], axis=1),
        "eps": np.full((P, 1), EPS, np.float32), "one": np.ones((P, 1), np.float32),
        "f1": pad(I["hy_filt_b1"], I["hy_filt_freq1"]), "f2": pad(I["hy_filt_b2"], I["hy_filt_freq2"]),
    }
    arrays["vecs"] = np.ascontiguousarray(np.concatenate([parts[name] for name, _ in VEC], axis=1))
    T = {}
    feed = {}
    for name, a in arrays.items():
        feed["in_" + name] = a
        T[name] = nc.dram_tensor("in_" + name, a.shape, mybir.dt.from_np(a.dtype), kind="ExternalInput").ap()
    out = nc.dram_tensor("out_0", (D, L), F32, kind="ExternalOutput").ap()
    build(nc, T, out)
    r = _run(nc, [feed], core_ids=[0])
    return np.ascontiguousarray(r.results[0]["out_0"].T).reshape(1, L, D)
```

```python
from contextlib import ExitStack

import numpy as np
import concourse.bass as bass
from concourse import mybir

F32 = mybir.dt.float32
F32R = mybir.dt.float32r
BF16 = mybir.dt.bfloat16
I32 = mybir.dt.int32
ALU = mybir.AluOpType
ACT = mybir.ActivationFunctionType
AX = mybir.AxisListType

P = 128
D = 1024
KT = D // P
L = 256
TB = L // P
EPS = 1e-6
GRID_W = 64
HG_H, HG_D, HG_C = 4, 128, 32
HY = 512
HYT = HY // P
NG, NE, FE = 4, 8, 512
NX = NG * NE
FT = FE // P
CAP = 64
NR = NG + NX
RT_H = 4
GL_H, GL_K = 4, 64
GL_T = GL_H * GL_K // P
RANK = 16
DFF = 4 * D
LAYERS = 2
IN2 = 3616
RING = 4
MRING = 6

VEC = [("ada_b", 48), ("n1", 8), ("n2", 8), ("lb", 16), ("hg_g", 1), ("conv_w", 36), ("conv_b", 12),
       ("hy_d", 4), ("fin", 8), ("ada_b2", 96), ("n1_2", 16), ("n2_2", 16), ("gla_g", 2), ("gate_b", 8),
       ("fin2", 8), ("c1", 16), ("c2", 16), ("decay", 16), ("rbias", NR), ("eps", 1), ("one", 1),
       ("f1", 2), ("f2", 2)]
VOFF = {}
_n = 0
for _name, _w in VEC:
    VOFF[_name] = (_n, _n + _w)
    _n += _w
NVEC = _n


def columns(a):
    a = np.asarray(a)
    return np.ascontiguousarray(a.reshape(-1, P).T)


def tables():
    f = np.float32
    t = {}
    rows = L // GRID_W
    r = np.repeat(np.arange(rows, dtype=f), GRID_W)
    col = np.tile(np.arange(GRID_W, dtype=f), rows)
    quarter = D // 4
    omega = (f(1.0) / np.power(f(10000.0), np.arange(quarter, dtype=f) / f(quarter))).astype(f)

    def axis_emb(pos):
        a = (pos[:, None] * omega[None, :]).astype(f)
        return np.concatenate([np.sin(a), np.cos(a)], axis=-1)

    pos = np.concatenate([axis_emb(r), axis_emb(col)], axis=-1).astype(f)
    t["pos"] = np.ascontiguousarray(pos.T)
    i = np.arange(P)
    ident = np.eye(P, dtype=f)
    ones = np.ones((P, P), f)
    tok = np.arange(L)
    r32f = np.broadcast_to((tok % HG_C != 0).astype(f), (P, L))
    r32b = np.broadcast_to((tok % HG_C != HG_C - 1).astype(f), (P, L))
    t["base"] = np.ascontiguousarray(np.concatenate([ident, ones, r32f, r32b], axis=1))
    same = (i[:, None] // HG_C) == (i[None, :] // HG_C)
    t["hg_mask"] = np.ascontiguousarray(np.concatenate(
        [same & (i[:, None] <= i[None, :]), same & (i[:, None] >= i[None, :])], axis=1).astype(np.int32))
    slots = np.broadcast_to(np.arange(CAP, dtype=f), (P, CAP))
    t["moe"] = np.ascontiguousarray(np.concatenate(
        [(i[:, None] < i[None, :]).astype(f), slots, slots, (i[:, None] % CAP == np.arange(CAP)[None, :]).astype(f)], axis=1))
    lin = np.linspace(0.0, 1.0, L, dtype=f)[:, None]
    bands = 16
    ang = (f(2.0 * np.pi) * np.arange(L, dtype=f) / f(L))[:, None] * np.linspace(1e-4, bands - 1, bands, dtype=f)[None]
    z = np.concatenate([lin, np.cos(ang), -np.sin(ang)], axis=-1).astype(f)
    t["hy_z"] = np.ascontiguousarray(z.T)
    deltas = np.abs(np.linspace(np.log(1e-2) / 1.5, np.log(1e-2) / 0.3, HY, dtype=f))
    dec = np.exp(-lin * deltas[None, :]).astype(f)
    two = lambda a: a.reshape(2, P, -1).transpose(1, 0, 2).reshape(P, -1)
    th = 2 * np.pi * ((np.arange(L)[:, None] * np.arange(L)[None, :]) % (2 * L)) / (2 * L)
    fw = np.concatenate([np.cos(th), -np.sin(th)], axis=1)
    fw[:, L] = np.cos(np.pi * np.arange(L))
    bw = np.concatenate([np.cos(th), np.sin(th)], axis=1)
    bw[:, L] = np.cos(np.pi * np.arange(L))
    bw[0] = 0.0
    inv = fw.T * (2.0 / (2 * L))
    inv[0] *= 0.5
    inv[L] *= 0.5
    four = inv.reshape(4, P, L).transpose(1, 0, 2).reshape(P, -1)
    t["hy"] = np.ascontiguousarray(np.concatenate([two(fw), four, two(bw), two(dec)], axis=1).astype(f))
    perm = np.zeros((P, P), f)
    perm[i ^ 32, i] = 1.0
    nf = 32
    invf = np.power(f(10000.0), -np.arange(nf, dtype=f) / f(nf)).astype(f)
    half = np.concatenate([invf, invf])
    angs = np.concatenate([half[:, None] * r[None, :], half[:, None] * col[None, :]], axis=0).astype(f)
    sign = np.where((i // 32) % 2 == 0, -1.0, 1.0)[:, None]
    s2 = np.arange(L)
    ef = np.maximum(s2[None, :] - s2[:, None], 0)
    eb = np.maximum(s2[:, None] - s2[None, :], 0)
    t2 = np.arange(2 * L)
    r128f = np.broadcast_to((t2 % P != 0), (P, 2 * L))
    r128b = np.broadcast_to((t2 % P != P - 1), (P, 2 * L))
    rowf = np.broadcast_to(s2 + 1, (P, L))
    rowb = np.broadcast_to(L - s2, (P, L))
    colf = (L - 1 - s2).reshape(2, P).T
    colb = s2.reshape(2, P).T
    t["b2"] = np.ascontiguousarray(np.concatenate(
        [perm, np.cos(angs), np.sin(angs) * sign, two(ef), two(eb), r128f, r128b, rowf, rowb, colf, colb],
        axis=1).astype(f))
    t["b2_mask"] = np.ascontiguousarray(np.concatenate(
        [i[:, None] <= i[None, :], i[:, None] > i[None, :]], axis=1).astype(np.int32))
    return t


def build(nc, T, out):
    ctx = ExitStack()
    with ctx:
        def sb(name, shape, dt=F32):
            return ctx.enter_context(nc.sbuf_tensor(name, shape, dt))

        sems = {}

        def S(name):
            if name not in sems:
                sems[name] = ctx.enter_context(nc.semaphore(name))
            return sems[name]

        base = sb("base", [P, 2 * P + 2 * L])
        hmask = sb("hmask", [P, 2, P], I32)
        vecs = sb("vecs", [P, NVEC])
        silc = sb("silc", [P, 2, KT, 2])
        mod = sb("mod", [P, 3, 48, 2])
        gsc = sb("gsc", [P, 3, 2, KT, 2])
        RS = sb("RS", [P, 2 * L])
        lbc = sb("lbc", [P, 40])
        npass = sb("npass", [1, 8], I32)
        mrow = [sb("mod_rows", [2, 512])[:, :], RS[0:2, :]]
        et = sb("chunk_decay", [P, 64])
        AR = 25600
        with ExitStack() as once:
            def shared(name, shape, dt=F32):
                return once.enter_context(nc.sbuf_tensor(name, shape, dt))

            ring = [shared(f"ring{s}", [P, KT * 512]) for s in range(RING)]
            X = shared("X", [P, KT, 2 * L])
            H = shared("H", [P, KT, 2 * L])
            ar = shared("arena", [P, AR])
        ring_r = [sb(f"ring_low{s}", [P, KT * 512], F32R) for s in range(RING)]
        Xr = sb("X_r", [P, KT, 2 * L], F32R)
        Hl = sb("H_low", [P, KT, 2 * L], F32R)
        ar_r = sb("arena_r", [P, AR], F32R)
        ps = [ctx.enter_context(nc.psum_tensor(f"bank{b}", [P, 512], F32))[:, :] for b in range(8)]
        ident, ones = base[:, 0:P], base[:, P:2 * P]
        r32 = [base[:, 2 * P:2 * P + L], base[:, 2 * P + L:2 * P + 2 * L]]

        full = [ctx.enter_context(nc.semaphore(f"full{s}")) for s in range(MRING)]
        used = S("ring_used")
        out_sem = S("out_stored")

        def vec(name, a=0, n=1):
            lo = VOFF[name][0] + a
            return vecs[:, lo:lo + n]

        def A(off, n):
            assert off + n <= AR, (off, n)
            return ar[:, off:off + n]

        def AR3(off, a, b):
            return ar_r[:, off:off + a * b].rearrange("p (a b) -> p a b", a=a)

        def A3(off, a, b):
            return A(off, a * b).rearrange("p (a b) -> p a b", a=a)

        ADA1, WIN, MERGE, MOE = 0, 12, 36, 40
        NMOE = 3 * NX
        L0 = MOE + NMOE
        MLP0 = L0 + 18
        L1 = MLP0 + 32
        MLP1 = L1 + 18
        END = MLP1 + 16
        WIN_ORDER = [1, 0, 3, 2, 4, 5, 6, 7, 8, 9, 10, 11]
        ADA_COLS = 384

        def cols(w, a, n):
            return w[:, bass.ds(a, n)].rearrange("(k p) n -> p k n", p=P)

        def rows(w, a, n):
            return w[bass.ds(a, n), :].rearrange("(k p) n -> p k n", p=P)

        def slot(n):
            return ring[n % RING][:, :]

        def arrived(n):
            return 16 * (n // RING + 1) - (0 if n < MOE else 16 * (NMOE // RING - NMOE // MRING))

        def low(n):
            return ring_r[n % RING][:, :]

        def as_cols(n, w=512, slot=slot):
            return slot(n)[:, 0:KT * w].rearrange("p (k n) -> p k n", k=KT)

        def as_rows(n, slot=slot):
            return slot(n).rearrange("p (k n) -> p k n", k=4)

        E5 = 8328 + 3 * 4096

        def eslot(c):
            s = c % MRING
            return ring[s][:, :] if s < RING else H[:, :, :].rearrange("p k n -> p (k n)") if s == 4 else A(E5, 4096)

        def elow(c):
            s = c % MRING
            return ring_r[s][:, :] if s < RING else Hl[:, :, :].rearrange("p k n -> p (k n)") if s == 4 else ar_r[:, E5:E5 + 4096]

        def earrived(c, turns=0):
            return 16 * (c // MRING + 1 + (MOE // RING if c % MRING < RING else 0)) + turns

        PHASES = ["filters", "projected", "scan_f", "scan_b", "hyena", "merged", "experts",
                  "l0_in", "l0_ret", "l0_gf", "l0_gb", "l0_out", "l0_mlp", "l1_in", "l1_ret", "l1_gf", "l1_gb", "l1_out", "l1_mlp"]

        block = ctx.enter_context(nc.Block())

        @block.sync
        def _(sp):
            def load(n, src, dst, loop=None):
                if loop is not None or n >= RING:
                    sp.wait_ge(used, (0 if loop is None else loop) + (n - RING + 1))
                sp.dma_start(dst, src).then_inc(full[n % RING], 16)

            for n in range(RING):
                load(n, cols(T["ada_w"], n * 512, 512), as_cols(n))
            with sp.Fori(1, 3) as i:
                for u in range(RING):
                    load(u, cols(T["ada_w"], (i * RING + u) * 512, 512), as_cols(u), i * RING)
            for j in range(12):
                n = WIN + 2 * j
                load(n, cols(T["w_in"], WIN_ORDER[j] * 512, 512), as_cols(n))
                load(n + 1, cols(T["ada_w_2"][0], j * 512, 512), as_cols(n + 1))
            load(MERGE, rows(T["w_proj_a"], 0, 512), as_rows(MERGE))
            load(MERGE + 1, rows(T["w_proj_b"], 0, 512), as_rows(MERGE + 1))
            for j in range(2):
                n = MERGE + 2 + j
                load(n, cols(T["w_out"], j * 512, 512), as_cols(n))
            def expert(c, name, e, turns=None):
                if c < 4 and turns is None:
                    sp.wait_ge(used, MOE + c - RING + 1)
                elif c == 4 and turns is None:
                    sp.wait_ge(S("logits"), 1)
                elif c == 5 and turns is None:
                    sp.wait_ge(S("phase"), 4 * (PHASES.index("merged") + 1))
                else:
                    sp.wait_ge(used, MOE + c - MRING + 1 + (0 if turns is None else turns))
                k = 4 if name == "moe_w_down" else KT
                sp.dma_start(eslot(c).rearrange("p (k n) -> p k n", k=k), T[name][e].rearrange("(k p) n -> p k n", p=P))\
                    .then_inc(full[c % MRING], 16)

            expert(0, "moe_w_up", 0)
            expert(1, "moe_w_gate", 0)
            for e in range(2):
                expert(3 * e + 2, "moe_w_up", e + 1)
                expert(3 * e + 3, "moe_w_gate", e + 1)
                expert(3 * e + 4, "moe_w_down", e)
            with sp.Fori(1, NX // 2 - 1) as i:
                for u in range(2):
                    expert(3 * u + 2, "moe_w_up", i * 2 + u + 1, i * 6)
                    expert(3 * u + 3, "moe_w_gate", i * 2 + u + 1, i * 6)
                    expert(3 * u + 4, "moe_w_down", i * 2 + u, i * 6)
            e = NX - 2
            expert(3 * e + 2, "moe_w_up", e + 1)
            expert(3 * e + 3, "moe_w_gate", e + 1)
            expert(3 * e + 4, "moe_w_down", e)
            expert(3 * e + 5, "moe_w_down", e + 1)
            sp.wait_ge(S("passes_known"), 1)
            more = sp.value_load(npass[0:1, 0:1])
            with sp.If(more > 0):
                sp.wait_ge(used, MOE + NMOE)
                with sp.Fori(0, more) as q:
                    with sp.Fori(0, NX) as e:
                        for m, (name, view) in enumerate((("moe_w_gate", as_cols), ("moe_w_up", as_cols), ("moe_w_down", as_rows))):
                            sp.wait_ge(S("over_begun"), q * NX + e + 1)
                            sp.dma_start(view(m), T[name][e].rearrange("(k p) n -> p k n", p=P)).then_inc(S("over_in"), 16)
                sp.wait_ge(S("experts_done"), 1)
            for l, first, mlp in ((0, L0, MLP0), (1, L1, MLP1)):
                for j in range(7):
                    load(first + 2 * j, cols(T["w_in_2"][l], j * 512, 512), as_cols(first + 2 * j))
                load(first + 14, cols(T["w_in_2"][l], 7 * 512, 2 * RANK), as_cols(first + 14, 2 * RANK))
                for j in range(2):
                    load(first + 16 + j, cols(T["w_out_2"][l], j * 512, 512), as_cols(first + 16 + j))
                with sp.Fori(0, 4) as i:
                    n = mlp
                    per = 8 if l == 0 else 4
                    for h in range(2):
                        load(n, cols(T["w_mlp1_2"][l], (i * 2 + h) * 512, 512), as_cols(n), i * per)
                        n += 1
                        if l == 0:
                            for a in range(2):
                                load(n, cols(T["ada_w_2"][1], (i * 4 + h * 2 + a) * ADA_COLS, ADA_COLS), as_cols(n, ADA_COLS), i * per)
                                n += 1
                        src = T["w_mlp2_2"][l].rearrange("(j k p) n -> j p k n", p=P, k=4)[i * 2 + h]
                        load(n, src, as_rows(n), i * per)
                        n += 1
            sp.wait_ge(S("phase"), 4 * len(PHASES))
            sp.dma_start(out.rearrange("(k p) n -> p k n", p=P), X[:, :, 0:L]).then_inc(out_sem, 16)
            sp.wait_ge(out_sem, 16)

        Qt = A3(0, HG_H, L)
        Vn = A3(1024, 4, 512)
        Gt = A3(3072, HG_H, L)
        K2 = [A3(4096 + 4096 * d, HG_H, 2 * L) for d in range(2)]
        L2 = [A3(6144 + 4096 * d, HG_H, 2 * L) for d in range(2)]
        KX, KC = [k[:, :, 0:L] for k in K2], [k[:, :, L:2 * L] for k in K2]
        LX, LC = [k[:, :, 0:L] for k in L2], [k[:, :, L:2 * L] for k in L2]
        HYt = A3(12288, 12, L)
        QM, KM, QD = A3(15360, HG_H, L), A3(16384, HG_H, L), A3(17408, HG_H, L)
        SC = A3(18432, 8, P)
        KEN, KDN = A3(19456, 8, P), A3(20480, 8, P)
        ST = A3(21504, 4, 512)
        KS = A3(23552, 4, 512)
        f_tab, f_dec = A(15360 + 2048, 1024), A3(15360 + 3072, 2, 512)
        f_z, f_w1, f_w2, f_w3 = A(19456, L), A(19712, 64), A(19776, 64), A(19840, 1024)
        f_h1, f_h2, f_t = A(20864, L), A(21120, L), A(21376, L)
        f_fw = A3(15360, 2, 512)
        f_inv0 = A(16384, 1024)
        f_nat = A3(21632, 2, 512)
        OS = A3(0, HG_H, L)
        OSQ = A3(1024, HG_H, L)
        ORS = A3(2048, HG_H, L)
        GL = A3(4096, 16, L)
        CV = A3(8192, 12, L)
        UV = A3(11264, HYT, L)
        UN = A3(17408, 2, 512)
        HFW, HINV = A3(15360, 2, 512), A3(16384, 4, L)
        YF = A3(18432, 4, 512)
        UT = A3(20480, 2, 512)
        UF = A3(21504, 4, 512)
        YB = A3(12288, HYT, L)
        MIX = A3(15360, KT, L)
        MT = A3(17408, KT, L)
        HB = A(0, 3072).bitcast(BF16).rearrange("p (n b d) -> p n b d", n=3, b=TB)
        WR = A3(3072, KT, NR)
        mtab = A(3360, P + 3 * CAP)
        SLT, IOTA, PAIR = mtab[:, 0:P], mtab[:, P:P + 2 * CAP], mtab[:, P + 2 * CAP:P + 3 * CAP]
        LG = A3(3680, TB, NR)
        RKM = A3(3752, TB, NX + 4)
        CMB = A3(3824, TB, NX + 4)
        SELX = A3(3896, TB, NX)
        RT = A(3960, 400)
        SGv = A(4360, 128).bitcast(BF16).rearrange("p (u b c) -> p u b c", u=2, b=TB)
        SW = A3(4488, 4, P)
        SWv = SW.rearrange("p (u b) c -> p u b c", u=2)
        HGs = [Xr[:, :, L + P * b:L + P * (b + 1)] for b in range(2)]
        UPR, GTR = A(5000, 512), A(5512, 512)
        HG = UPR
        SIL, HID = A3(6024, FT, CAP), A3(6280, FT, CAP)
        HIDs = AR3(6536, FT, 2 * CAP)
        YS = A(7048, D)
        SWT = A(8072, L)
        EH = [ar_r[:, 8328 + 4096 * h:8328 + 4096 * (h + 1)] for h in range(3)]
        HN = A3(8328, TB, D)
        RQ, RK = A3(0, 4, 512), A3(2048, 4, 512)
        RV, GV = A3(4096, 4, 512), A3(6144, 4, 512)
        YT = A3(8192, 8, 512)
        GQ, GK = A3(12288, 2, 512), A3(13312, 2, 512)
        DT = A(14336, 512)
        GUP = A3(14848, 2, L)
        b2t = A(15360, 3204)
        PERM, RCOS, RSIN = b2t[:, 0:128], b2t[:, 128:384], b2t[:, 384:640]
        EF, EB = b2t[:, 640:1152].rearrange("p (a b) -> p a b", a=2), b2t[:, 1152:1664].rearrange("p (a b) -> p a b", a=2)
        R128 = [b2t[:, 1664:2176], b2t[:, 2176:2688]]
        ROWT = [b2t[:, 2688:2944], b2t[:, 2944:3200]]
        COLT = b2t[:, 3200:3204]
        gmask = A(18564, 256).bitcast(I32).rearrange("p (a b) -> p a b", a=2)
        lgam = A(18820, 24)
        RB = 18848
        Wd = [A3(RB + 2048 * b, 2, L) for b in range(2)]
        RQD = [A3(RB + 512 + 2048 * b, 2, L) for b in range(2)]
        RVD = [A(RB + 1024 + 2048 * b, 512).rearrange("p (d k v) -> p d k v", d=2, k=2) for b in range(2)]
        RKN = [A3(RB + 1536 + 2048 * b, 2, P) for b in range(2)]
        RST = [A3(RB + 1792 + 2048 * b, 2, P) for b in range(2)]
        RSC = [A3(22944 + 512 * b, 2, L) for b in range(2)]
        ROT = A3(23968, 4, L)
        GLg = A3(18848, 2, 512)
        GQM, GKM, GQD = A3(0, 2, 512), A3(1024, 2, 512), A3(2048, 2, 512)
        GKE, GKN = A3(3072, 2, 512), A3(19872, 4, L)
        GST = A(20896, 768).rearrange("p (n t v) -> p n t v", n=3, t=2)
        GSC = A3(21664, 16, P)
        GT1, GT2 = A3(23712, 2, 512), A3(4096, 2, 512)
        OB = A3(0, 4, 512)
        OQ = A3(2048, 4, 512)
        HA = A3(0, 4, 512)
        HAl = AR3(0, 4, 512)
        HAh = AR3(2048, 4, 512)
        Hh = AR3(18848, KT, 512)
        W1h, W2h = ar_r[:, 4096:8192], ar_r[:, 8192:12288]
        W1h_cols, W2h_rows = W1h.rearrange("p (k n) -> p k n", k=KT), W2h.rearrange("p (k n) -> p k n", k=4)

        def follow(i, u, n):
            return not isinstance(i, int) or u + n < 2

        def mlp_chunks(l, u, m, i):
            per = (4, 2)[l]
            return (MLP0, MLP1)[l] + per * u + (per - 1) * m, i * (32 if l == 0 else 16), i * 2 * per, per


        def phase_end(eng, name):
            eng.drain().then_inc(S("phase"), 1)
            eng.wait_ge(S("phase"), 4 * (PHASES.index(name) + 1))

        @block.tensor
        def _(pe):
            pend = [0]
            tiles = [0]

            def mm(o, l, r, start=True, stop=True, inc=None):
                ins = nc.tensor.matmul(o, l, r, start=start, stop=stop, skip_group_check=True)
                if inc is not None:
                    ins.then_inc(S(inc), 1)
                elif pend[0]:
                    ins.then_inc(used, pend[0])
                    pend[0] = 0
                return ins

            def mm3(o, w, x, start, stop, inc=None):
                mm(o, w[0], x[0], start, False)
                mm(o, w[0], x[1], False, False)
                mm(o, w[1], x[0], False, stop, inc)

            def tr(o, i, inc=None):
                ins = nc.tensor.transpose(o, i, ident)
                if inc is not None:
                    ins.then_inc(S(inc), 1)

            def flush():
                if pend[0]:
                    pe.drain().then_inc(used, pend[0])
                    pend[0] = 0

            def chunk_in(n, turns=0):
                pe.wait_ge(full[n % RING], arrived(n) + turns)

            def chunk_used(slots=1):
                flush()
                pend[0] = slots

            def tile_bank(nb=4):
                t = tiles[0]
                tiles[0] += 1
                if t >= 4:
                    pe.wait_ge(S("tile_free"), t - 3)
                return ps[t % 4]

            def stat(call, n=2 * L):
                for k in range(KT):
                    pe.wait_ge(S("squares"), 8 * call + k + 1)
                    mm(ps[6][:, 0:n], ones, H[:, k, 0:n], k == 0, k == KT - 1, "sum_ready" if k == KT - 1 else None)

            def ada(n, g, par, ncols=512, turns=0, blk=1):
                o = ps[6 + par]
                chunk_in(n, turns)
                pe.wait_ge(S("ada_out"), g + 1)
                for k in range(KT):
                    mm(o[0:2, 0:ncols], silc[:, blk, k, :], as_cols(n, ncols)[:, k, :], k == 0, k == KT - 1,
                       inc="ada_rows" if k == KT - 1 else None)
                chunk_used()

            def ada_turn(g, par, ncols=512):
                pe.wait_ge(S("ada_rows_out"), g + 1)
                m = ncols // P
                for t in range(m):
                    mm(ps[6 + par][:, 2 * t:2 * t + 2], mrow[par][:, t * P:(t + 1) * P], ident[0:2, 0:2],
                       inc="ada_turned" if t == m - 1 else None)

            def filters(d):
                for tb in range(2):
                    mm(ps[1 + tb], f_h2[0:64, tb * P:(tb + 1) * P], f_w3[0:64, d * 512:(d + 1) * 512], inc="filt_nat" if tb else None)

            def spectrum(d):
                pe.wait_ge(S("filt_dec"), d + 1)
                for ft in range(4):
                    o = ps[(3, 4, 5, 0)[ft]]
                    for tb in range(2):
                        tab = f_fw if d == 0 else f_tab.rearrange("p (a b) -> p a b", a=2)
                        mm(o, tab[:, tb, ft * P:(ft + 1) * P], f_nat[:, tb, :], d == 0 and tb == 0, d == 1 and tb == 1)

            pe.wait_ge(S("silu_c"), 1)
            ada(0, 0, 0, blk=0)
            pe.wait_ge(S("filter_in"), 16 * 5)
            mm(ps[0][0:64, 0:L], f_w1[0:33, :], f_z[0:33, :], inc="filt_mm")
            ada(1, 1, 1, blk=0)
            pe.wait_ge(S("base_in"), 16)
            ada_turn(0, 0)
            pe.wait_ge(S("filt_sin"), 1)
            mm(ps[0][0:64, L:2 * L], f_w2[0:64, :], f_h1[0:64, :], inc="filt_mm")
            ada(2, 2, 0, blk=0)
            ada_turn(1, 1)
            pe.wait_ge(S("filt_sin"), 2)
            filters(0)
            ada(3, 3, 1, blk=0)
            ada_turn(2, 0)
            flush()
            spectrum(0)
            filters(1)
            ada_turn(3, 1)
            with pe.Fori(1, 3) as i:
                for u in range(RING):
                    ada(u, i * RING + u, u % 2, 512, i * 16, blk=0)
                    if u:
                        ada_turn(i * RING + u - 1, (u - 1) % 2)
                flush()
                ada_turn(i * RING + 3, 1)
            spectrum(1)
            pe.drain().then_inc(S("spectrum"), 1)
            phase_end(pe, "filters")

            stat(0)

            pe.wait_ge(S("normed"), 16)
            for j, c in enumerate(WIN_ORDER[:8]):
                n = WIN + 2 * j
                if c != 3:
                    wide = 2 * L if c in (1, 2) else L
                    chunk_in(n)
                    for nt in range(4):
                        o = tile_bank()
                        for k in range(KT):
                            mm(o[:, 0:wide], as_cols(n)[:, k, nt * P:(nt + 1) * P], H[:, k, 0:wide], k == 0, k == KT - 1,
                               "tile_done" if k == KT - 1 else None)
                else:
                    chunk_in(n)
                    for tb in range(4):
                        o = tile_bank()
                        for k in range(KT):
                            mm(o, H[:, k, tb * P:(tb + 1) * P], as_cols(n)[:, k, :], k == 0, k == KT - 1,
                               "tile_done" if k == KT - 1 else None)
                chunk_used()
                if j:
                    ada_turn(12 + j - 1, (j - 1) % 2)
                ada(n + 1, 12 + j, j % 2)
            flush()
            ada_turn(12 + 7, 1)
            phase_end(pe, "projected")

            for b in (4, 5):
                mm(ps[b], SC[:, 0, :], SC[:, 0:4, :], True, False)
            for d in range(2):
                pe.wait_ge(S("kd_ready"), d + 1)
                for hh in range(2):
                    for j in range(4):
                        tb, h = hh, j
                        tr(ps[hh][:, j * P:(j + 1) * P], KC[d][:, h, tb * P:(tb + 1) * P], "turned" if j == 3 else None)
                pe.wait_ge(S("ke_ready"), d + 1)
                for hh in range(2):
                    for j in range(4):
                        tr(ps[2 + hh][:, j * P:(j + 1) * P], KX[d][:, j, hh * P:(hh + 1) * P], "turned" if j == 3 else None)
                pe.wait_ge(S("turned_out"), 4 * d + 2)
                for h in range(HG_H):
                    for tb in range(2):
                        mm(ps[0][:, h * P:(h + 1) * P], KDN[:, tb * 4 + h, :], Vn[:, 2 + tb, h * P:(h + 1) * P], tb == 0, tb == 1,
                           "ctx_state" if (h, tb) == (3, 1) else None)
                pe.wait_ge(S("qm_ready"), d + 1)
                pe.wait_ge(S("turned_out"), 4 * d + 4)
                for tb in range(2):
                    for h in range(HG_H):
                        mm(ps[6 + tb][:, h * P:(h + 1) * P], KM[:, h, tb * P:(tb + 1) * P], QM[:, h, tb * P:(tb + 1) * P],
                           inc="scores" if h == 3 else None)
                pe.wait_ge(S("states_out"), 8 * d + 1)
                for bi in range(2):
                    tb = bi if d == 0 else 1 - bi
                    if bi:
                        pe.wait_ge(S("states_out"), 8 * d + 5)
                    for j in range(4):
                        r = slice(32 * j, 32 * j + 32)
                        for h in range(HG_H):
                            mm(ps[j][:, h * P:(h + 1) * P], KEN[r, tb * 4 + h, :], Vn[r, tb, h * P:(h + 1) * P],
                               inc="updates" if (j, h) == (3, 3) else None)
                    if bi == 0:
                        pe.wait_ge(S("masked"), 2 * d + 2)
                        for h in range(HG_H):
                            for tb2 in range(2):
                                mm(ps[4 + h // 2][:, (h % 2) * L + tb2 * P:(h % 2) * L + (tb2 + 1) * P],
                                   Vn[:, tb2, h * P:(h + 1) * P], SC[:, tb2 * 4 + h, :], False, False)
                    for c in range(4):
                        n = 4 * bi + c
                        ch = n if d == 0 else 7 - n
                        pe.wait_ge(S("states_out"), 8 * d + n + 1)
                        for h in range(HG_H):
                            mm(ps[4 + h // 2][:, (h % 2) * L + ch * 32:(h % 2) * L + ch * 32 + 32],
                               ST[:, n % 4, h * P:(h + 1) * P], QD[:, h, ch * 32:ch * 32 + 32], False, False,
                               "inter" if h == 3 else None)
                phase_end(pe, "scan_f" if d == 0 else "scan_b")

            pe.wait_ge(S("o_squares"), 1)
            for b in range(2):
                mm(ps[4 + b], ones, OSQ[:, 2 * b:2 * b + 2, :], inc="o_sum" if b else None)

            for j in range(8, 12):
                n = WIN + 2 * j
                chunk_in(n)
                for nt in range(4):
                    o = tile_bank()
                    for k in range(KT):
                        mm(o[:, 0:L], as_cols(n)[:, k, nt * P:(nt + 1) * P], H[:, k, 0:L], k == 0, k == KT - 1,
                           "tile_done" if k == KT - 1 else None)
                chunk_used()
                if j > 8:
                    ada_turn(12 + j - 1, (j - 1) % 2)
                ada(n + 1, 12 + j, j % 2)
            flush()
            ada_turn(12 + 11, 1)
            pe.wait_ge(S("o_inverse"), 1)
            pe.wait_ge(S("tables_in"), 16)

            pe.wait_ge(S("uv_ready"), 1)
            for tb in range(2):
                for c in range(HYT):
                    tr(ps[4 + tb][:, c * P:(c + 1) * P], UV[:, c, tb * P:(tb + 1) * P], "tokens_turned" if c == 3 else None)
            pe.wait_ge(S("un_ready"), 2)
            pe.wait_ge(S("tile_free"), tiles[0])
            for ft in range(4):
                for tb in range(2):
                    mm(ps[ft], HFW[:, tb, ft * P:(ft + 1) * P], UN[:, tb, :], tb == 0, tb == 1, "u_spec" if (ft, tb) == (3, 1) else None)
            pe.wait_ge(S("y_spec"), 1)
            for c in range(HYT):
                for ft in range(4):
                    mm(ps[4 + c // 2][:, (c % 2) * L:(c % 2) * L + L], YF[:, ft, c * P:(c + 1) * P], HINV[:, ft, :], ft == 0, ft == 3,
                       "y_time" if (c, ft) == (3, 3) else None)
            phase_end(pe, "hyena")

            chunk_in(MERGE)
            chunk_in(MERGE + 1)
            for nt in range(KT):
                o = ps[nt % 4]
                if nt >= 4:
                    pe.wait_ge(S("merged"), nt - 3)
                for side, Y in ((0, OS), (1, YB)):
                    for k in range(4):
                        mm(o[:, side * L:(side + 1) * L], as_rows(MERGE + side)[:, k, nt * P:(nt + 1) * P], Y[:, k, :], k == 0, k == 3,
                           "merge_mm" if (side, k) == (1, 3) else None)
            pe.drain().then_inc(used, 1)
            pe.drain().then_inc(used, 1)
            pe.wait_ge(S("merged"), 8)
            for j in range(2):
                n = MERGE + 2 + j
                chunk_in(n)
                for nt in range(4):
                    t = j * 4 + nt
                    o = ps[4 + t % 2]
                    if t >= 2:
                        pe.wait_ge(S("out_added"), t - 1)
                    for k in range(KT):
                        mm(o[:, 0:L], as_cols(n)[:, k, nt * P:(nt + 1) * P], MIX[:, k, :], k == 0, k == KT - 1,
                           "out_mm" if k == KT - 1 else None)
                chunk_used()
            flush()
            phase_end(pe, "merged")

            stat(1, L)
            pe.wait_ge(S("normed"), 16 + 8)
            for tb in range(TB):
                for k in range(KT):
                    tr(ps[2 * tb + k // 4][:, (k % 4) * P:(k % 4 + 1) * P], H[:, k, tb * P:(tb + 1) * P], "tokens_turned" if k % 4 == 3 else None)
            pe.wait_ge(S("tables_in"), 48)
            for tb in range(TB):
                for k in range(KT):
                    mm(ps[4][:, tb * NR:(tb + 1) * NR], H[:, k, tb * P:(tb + 1) * P], WR[:, k, :], k == 0, k == KT - 1,
                       "logits" if (tb, k) == (1, 7) else None)
            pe.wait_ge(S("selected"), 1)
            mm(ps[5][:, 0:NX], SLT, SELX[:, 0, :])
            mm(ps[5][:, NX:2 * NX], ones, SELX[:, 0, :], True, False)
            mm(ps[5][:, NX:2 * NX], SLT, SELX[:, 1, :], False, True)
            mm(ps[5][:, 2 * NX:3 * NX], ones, SELX[:, 0, :], True, False)
            mm(ps[5][:, 2 * NX:3 * NX], ones, SELX[:, 1, :], False, True, inc="ranks")
            pe.wait_ge(S("sw_zero"), 1)
            for b in range(4):
                mm(ps[b], SW[:, 0, :], SW[:, 0:4, :], True, False, inc="cleared" if b == 3 else None)

            def gather(buf, bank, inc):
                for k in range(KT):
                    for part in range(3):
                        for tb in range(TB):
                            mm(ps[bank][:, k * CAP:(k + 1) * CAP], HB[:, part, tb, k * P:(k + 1) * P], SGv[:, buf, tb, :],
                               (part, tb) == (0, 0), (part, tb) == (2, 1), inc=inc if (k, part, tb) == (7, 2, 1) else None)

            def rows(c, cu, b, bank):
                pe.wait_ge(S("w_split"), c + 1)
                hi, lo = EH[cu % 3].rearrange("p (k n) -> p k n", k=KT), elow(cu).rearrange("p (k n) -> p k n", k=KT)
                for k in range(KT):
                    mm(ps[bank], HGs[b][:, k, :], hi[:, k, :], k == 0, False)
                    mm(ps[bank], HGs[b][:, k, :], lo[:, k, :], False, k == KT - 1, inc="row_sums" if k == KT - 1 else None)
                chunk_used()

            def expert(i, u):
                e = i * 2 + u
                more1, more2 = follow(i, u, 1), follow(i, u, 2)
                pe.wait_ge(S("sw_ready"), e + 1)
                pe.wait_ge(S("rows_out"), 2 * e + 2)
                for tb in range(TB):
                    tr(ps[5][:, tb * P:(tb + 1) * P], SWv[:, u % 2, tb, :], "weights_turned" if tb else None)
                for m, R in enumerate((UPR, GTR)):
                    for nt in range(FT):
                        mm(ps[6][:, m * 256 + nt * CAP:m * 256 + (nt + 1) * CAP], R[:, nt * P:(nt + 1) * P], PAIR,
                           inc="gate_up" if (m, nt) == (1, FT - 1) else None)
                if more2:
                    pe.wait_ge(S("onehot"), e + 3)
                    pe.wait_ge(S("hg_low"), e + 2)
                    gather(u % 2, 7, "gathered")
                pe.wait_ge(S("weights_out"), e + 1)
                if more1:
                    pe.wait_ge(S("hg_low"), e + 2)
                    rows(i * 6 + 3 * u + 2, 3 * u + 2, (u + 1) % 2, 5)
                    rows(i * 6 + 3 * u + 3, 3 * u + 3, (u + 1) % 2, 4)
                du = 3 * u + (4 if more1 else 2)
                pe.wait_ge(S("hidden"), e + 1)
                pe.wait_ge(S("w_split"), i * 6 + du + 1)
                hi, lo = EH[du % 3].rearrange("p (k n) -> p k n", k=4), elow(du).rearrange("p (k n) -> p k n", k=4)
                for nb in range(2):
                    s = slice(nb * 512, (nb + 1) * 512)
                    if nb and more2:
                        pe.wait_ge(S("hg_low"), e + 3)
                    for k in range(FT):
                        mm(ps[6 + nb], HIDs[:, k, :], hi[:, k, s], k == 0, False)
                        mm(ps[6 + nb], HIDs[:, k, :], lo[:, k, s], False, k == FT - 1, inc="down" if k == FT - 1 else None)
                chunk_used()
                for k in range(KT):
                    if k % 4 == 0:
                        pe.wait_ge(S("ys_out"), 2 * e + k // 4 + 1)
                    mm(ps[k // 2][:, (k % 2) * L:(k % 2 + 1) * L], YS[:, k * P:(k + 1) * P], SWT, False, False)

            pe.wait_ge(S("h_parts"), 1)
            for e in range(2):
                pe.wait_ge(S("onehot"), e + 1)
                if e:
                    pe.wait_ge(S("hg_low"), e)
                gather(e, 7, "gathered")
            rows(0, 0, 0, 5)
            rows(1, 1, 0, 4)
            flush()
            with pe.Fori(0, NX // 2 - 1) as i:
                for u in range(2):
                    expert(i, u)
            for u in range(2):
                expert(NX // 2 - 1, u)
            flush()

            pe.wait_ge(S("passes_known"), 1)
            more = pe.value_load(npass[0:1, 0:1])
            with pe.If(more > 0):
                pe.drain().then_inc(S("over_begun"), 1)
                with pe.Fori(0, more) as q:
                    with pe.Fori(0, NX) as e:
                        g = q * NX + e
                        pe.wait_ge(S("over_onehot"), g + 1)
                        gather(0, 4, "over_gathered")
                        pe.wait_ge(S("over_gather_out"), g + 1)
                        pe.wait_ge(S("over_in"), g * 48 + 48)
                        for m in range(2):
                            for nt in range(FT):
                                for k in range(KT):
                                    mm(ps[5][:, m * 256 + nt * CAP:m * 256 + (nt + 1) * CAP], as_cols(m)[:, k, nt * P:(nt + 1) * P],
                                       HG[:, k * CAP:(k + 1) * CAP], k == 0, k == KT - 1,
                                       inc="over_gate_up" if (nt, k, m) == (FT - 1, KT - 1, 1) else None)
                        for tb in range(TB):
                            tr(ps[4][0:CAP, tb * P:(tb + 1) * P], SWv[:, 0, tb, 0:CAP], "over_turned" if tb else None)
                        pe.wait_ge(S("over_hidden"), g + 1)
                        for nb in range(2):
                            for k in range(FT):
                                mm(ps[6 + nb][0:CAP, :], HID[:, k, :], as_rows(2)[:, k, nb * 512:(nb + 1) * 512], k == 0, k == FT - 1,
                                   inc="over_down" if (nb, k) == (1, FT - 1) else None)
                        pe.wait_ge(S("over_out"), g + 1)
                        for k in range(KT):
                            mm(ps[k // 2][:, (k % 2) * L:(k % 2 + 1) * L], YS[0:CAP, k * P:(k + 1) * P], SWT[0:CAP, :], False, False,
                               inc="over_begun" if k == 7 else None)
            pe.drain().then_inc(S("experts_done"), 1)
            pe.wait_ge(S("experts_added"), 1)
            stat(2, L)
            phase_end(pe, "experts")

            ncall = 3
            for l, first, mlp in ((0, L0, MLP0), (1, L1, MLP1)):
                W = 2 * L if l == 0 else L
                stat(ncall)
                pe.wait_ge(S("h_split"), 2 * l + 1)
                ncall += 1
                for j in range(7):
                    n = first + 2 * j
                    chunk_in(n + 1)
                    wh, wl = as_cols(n + 1, slot=low), as_cols(n, slot=low)
                    if j in (2, 5):
                        for tb in range(4):
                            o = tile_bank()
                            c = slice(tb * P, (tb + 1) * P)
                            for k in range(KT):
                                mm3(o, (Hh[:, k, c], Hl[:, k, c]), (wh[:, k, :], wl[:, k, :]), k == 0, k == KT - 1,
                                    "tile_done" if k == KT - 1 else None)
                    else:
                        for nt in range(4):
                            wide = 2 * L if j == 1 or (j == 4 and nt >= 2) else W
                            o = tile_bank()
                            c = slice(nt * P, (nt + 1) * P)
                            for k in range(KT):
                                mm3(o[:, 0:wide], (wh[:, k, c], wl[:, k, c]), (Hh[:, k, 0:wide], Hl[:, k, 0:wide]), k == 0, k == KT - 1,
                                    "tile_done" if k == KT - 1 else None)
                    chunk_used(2)
                n = first + 14
                chunk_in(n + 1)
                wh, wl = as_cols(n + 1, 32, slot=low), as_cols(n, 32, slot=low)
                o = tile_bank()
                for k in range(KT):
                    mm3(o[0:32, :], (wh[:, k, :], wl[:, k, :]), (Hh[:, k, :], Hl[:, k, :]), k == 0, k == KT - 1,
                        "tile_done" if k == KT - 1 else None)
                chunk_used(2)
                flush()
                pe.wait_ge(S("b2_in"), 16 * (3 + l))
                pe.wait_ge(S("tile_free"), tiles[0])
                for m, M in enumerate((RQ, RK)):
                    for h in range(RT_H):
                        mm(ps[4 + m * 2 + h // 2][:, (h % 2) * L:(h % 2 + 1) * L], PERM, M[:, h, 0:L],
                           inc="swapped" if h % 2 else None)
                phase_end(pe, f"l{l}_in")

                for h in range(RT_H):
                    b = h % 2
                    c = l * RT_H + h
                    for tb in range(2):
                        tr(ps[4][:, tb * P:(tb + 1) * P], RK[:, h, L + tb * P:L + (tb + 1) * P], "rk_turned" if tb else None)
                    pe.wait_ge(S("r_prep"), c + 1)
                    pe.wait_ge(S("rk_out"), c + 1)
                    for d in range(2):
                        for tb in range(2):
                            mm(ps[5][:, d * P:(d + 1) * P], RKN[b][:, tb, :], RVD[b][:, d, tb, :], tb == 0, tb == 1,
                               "r_state" if (d, tb) == (1, 1) else None)
                    sides = (0, 1) if l == 0 else (0,)
                    for side in sides:
                        for sblk in range(2):
                            mm(ps[6 + side][:, sblk * L:(sblk + 1) * L], RK[:, h, side * L + sblk * P:side * L + (sblk + 1) * P],
                               RQ[:, h, side * L:(side + 1) * L], inc="r_scores" if sblk else None)
                    for side in sides:
                        q = c * 2 + side if l == 0 else 2 * RT_H + h
                        pe.wait_ge(S("r_decayed"), q + 1)
                        o = ps[h][:, side * L:(side + 1) * L]
                        for sblk in range(2):
                            mm(o, RV[:, side * 2 + sblk, h * P:(h + 1) * P], RSC[side][:, sblk, :], sblk == 0, sblk == 1 and side == 1,
                               inc="r_head" if sblk and side else None)
                        if side == 0:
                            pe.wait_ge(S("r_state_out"), c + 1)
                            for d in range(2):
                                mm(o, RST[b][:, d, :], RQD[b][:, d, :], False, d == 1, inc="r_head" if d and l else None)
                pe.wait_ge(S("r_copied"), (4 * (l + 1)))
                for h in range(RT_H):
                    mm(ps[4 + h][:, 0:W], ones, OB[:, h, 0:W], inc="r_mean")
                pe.wait_ge(S("r_sq"), 4 * (l + 1))
                for h in range(RT_H):
                    mm(ps[h][:, 0:W], ones, OQ[:, h, 0:W], inc="r_var")
                phase_end(pe, f"l{l}_ret")

                nx = 4 if l == 0 else 2
                pe.wait_ge(S("gsc_clear"), l + 1)
                for h in range(4):
                    mm(ps[h], GSC[:, 0, :], GSC[:, 0:4, :], True, False)
                for d in range(2):
                    g = 2 * l + d
                    for t in range(2):
                        mm(ps[4 + t], GUP[0:32, d, t * P:(t + 1) * P], DT[0:32, :], inc="gate_mm")
                    pe.wait_ge(S("gke_ready"), g + 1)
                    for ch in range(4):
                        for t in range(2):
                            tr(ps[4 + ch // 2][:, (ch % 2) * L + t * P:(ch % 2) * L + (t + 1) * P], GKE[:, t, ch * P:(ch + 1) * P],
                               "gk_turned" if (ch, t) in ((1, 1), (3, 1)) else None)
                    pe.wait_ge(S("gqm_ready"), g + 1)
                    for ch in range(nx):
                        for h in range(4):
                            r = slice(64 * (h % 2), 64 * (h % 2) + 64)
                            k = ch * 2 + h // 2
                            mm(ps[6 + h % 2][:, (k % 4) * P:(k % 4 + 1) * P], GKM[r, h // 2, ch * P:(ch + 1) * P], GQM[r, h // 2, ch * P:(ch + 1) * P],
                               inc="g_scores" if h == 3 else None)
                        if ch == 1 and nx == 4:
                            pe.wait_ge(S("g_masked"), (0, 8, 16, 20)[g] + 4)
                    order = [2, 3, 0, 1] if d == 0 else [3, 2, 1, 0]
                    pe.wait_ge(S("gk_out"), 2 * (g + 1))
                    for n, ch in enumerate(order[:3]):
                        for h in range(4):
                            r = slice(64 * (h % 2), 64 * (h % 2) + 64)
                            mm(ps[4 + n // 2][r, (n % 2) * L + (h // 2) * P:(n % 2) * L + (h // 2 + 1) * P],
                               GKN[:, ch, h * 64:(h + 1) * 64], GV[:, ch, h * P:(h + 1) * P], inc="g_update" if h == 3 else None)
                    pe.wait_ge(S("g_masked"), (8, 16, 20, 24)[g])
                    for ch in range(nx):
                        for h in range(4):
                            mm(ps[h][:, ch * P:(ch + 1) * P], GV[:, ch, h * P:(h + 1) * P], GSC[:, (h % 2) * 8 + ch * 2 + h // 2, :], False, False)
                    for n, ch in enumerate(order):
                        if n == 0 or ch >= nx:
                            continue
                        pe.wait_ge(S("g_state"), 3 * g + n)
                        for h in range(4):
                            r = slice(64 * (h % 2), 64 * (h % 2) + 64)
                            mm(ps[h][:, ch * P:(ch + 1) * P], GST[r, n - 1, h // 2, :], GQD[r, h // 2, ch * P:(ch + 1) * P], False, False)
                    if d == 0:
                        phase_end(pe, f"l{l}_gf")
                pe.drain().then_inc(S("g_done"), 1)
                pe.wait_ge(S("g_sq"), 4 * (l + 1))
                for h in range(4):
                    mm(ps[4 + h][:, 0:W], ones, OQ[:, h, 0:W], inc="g_sum")
                phase_end(pe, f"l{l}_gb")

                for j in range(2):
                    n = first + 16 + j
                    chunk_in(n)
                    for nt in range(4):
                        t = j * 4 + nt
                        if t >= 4:
                            pe.wait_ge(S("w_out_added"), 8 * l + t - 3)
                        for k in range(KT):
                            mm(ps[t % 4][:, 0:W], as_cols(n)[:, k, nt * P:(nt + 1) * P], YT[:, k, 0:W], k == 0, k == KT - 1,
                               "w_out_mm" if k == KT - 1 else None)
                    chunk_used()
                flush()
                stat(ncall, W)
                ncall += 1
                phase_end(pe, f"l{l}_out")

                pe.wait_ge(S("h_split"), 2 * l + 2)
                with pe.Fori(0, 4) as i:
                    n = mlp
                    turns = i * (32 if l == 0 else 16)
                    for u in range(2):
                        j = i * 2 + u
                        pe.wait_ge(S("w1_split"), 8 * l + j + 1)
                        for nt in range(4):
                            c = slice(nt * P, (nt + 1) * P)
                            for k in range(KT):
                                mm3(ps[nt][:, 0:W], (W1h_cols[:, k, c], as_cols(n, slot=low)[:, k, c]), (Hh[:, k, 0:W], Hl[:, k, 0:W]),
                                    k == 0, k == KT - 1, "hid_mm" if k == KT - 1 else None)
                        chunk_used()
                        if l == 1:
                            flush()
                        n += 1
                        if l == 0:
                            for a in range(2):
                                ada(n, 24 + i * 4 + u * 2 + a, a, ADA_COLS, turns)
                                n += 1
                            ada_turn(24 + i * 4 + u * 2, 0, ADA_COLS)
                        pe.wait_ge(S("w_split"), NMOE + 8 * l + j + 1)
                        for nt, ks in [(0, (0, 1, 2)), (1, (0, 1, 2)), (0, (3,)), (1, (3,))] + [(t, (0, 1, 2, 3)) for t in range(2, KT)]:
                            if ks[0] == 0:
                                pe.wait_ge(S("mlp_bank_free"), (64 + 2) * l + j * 8 + nt + 1)
                            if nt == 0:
                                pe.wait_ge(S("hid_out"), 32 * l + j * 4 + ks[-1] + 1)
                            c = slice(nt * P, (nt + 1) * P)
                            for k in ks:
                                mm3(ps[4 + nt % 2][:, 0:W], (W2h_rows[:, k, c], as_rows(n, slot=low)[:, k, c]), (HAh[:, k, 0:W], HAl[:, k, 0:W]),
                                    k == 0, k == 3, "mlp_mm" if k == 3 else None)
                        chunk_used()
                        n += 1
                        if l == 0:
                            ada_turn(24 + i * 4 + u * 2 + 1, 1, ADA_COLS)
                    flush()
                if l == 1:
                    stat(ncall, L)
                phase_end(pe, f"l{l}_mlp")

        CALLS = [(0, 0, 2 * L, (0, 1)), (0, 1, L, (0,)), ("fin", 0, L, (0,)), (1, 0, 2 * L, (0, 1)), (1, 1, 2 * L, (0, 1)),
                 (2, 0, 2 * L, (0, 1)), (2, 1, L, (0,)), ("fin2", 0, L, (0,))]

        @block.scalar
        def _(act):
            A_ = nc.scalar.activation
            own = [0]
            tiles = [0]
            done = [0]

            def link(ins):
                own[0] += 1
                ins.then_inc(S("act_own"), 1)
                act.wait_ge(S("act_own"), own[0])

            def rsqrt(o, i, n):
                link(A_(o, i, ACT.Ln, scale=1.0 / n, bias=vec("eps")))
                return A_(o, o, ACT.Exp, scale=-0.5)

            def norm(call):
                b, which, N, halves = CALLS[call]
                for k in range(KT):
                    A_(H[:, k, 0:N], X[:, k, 0:N], ACT.Square).then_inc(S("squares"), 1)
                act.wait_ge(S("sum_ready"), call + 1)
                rsqrt(RS[:, 0:N], ps[6][:, 0:N], D).then_inc(S("rms_ready"), 1)
                for k in range(KT):
                    if k % 4 == 0:
                        act.wait_ge(S("scaled"), 2 * call + k // 4 + 1)
                    for s in halves:
                        c = slice(s * L, (s + 1) * L)
                        if isinstance(b, str):
                            A_(X[:, k, c], H[:, k, c], ACT.Copy, scale=vec(b, k)).then_inc(S("normed"), 1)
                        else:
                            A_(H[:, k, c], H[:, k, c], ACT.Identity, scale=gsc[:, b, which, k, s:s + 1],
                               bias=mod[:, b, 24 * which + k, s:s + 1]).then_inc(S("normed"), 1)
                        done[0] += 1

            def tile():
                t = tiles[0]
                tiles[0] += 1
                act.wait_ge(S("tile_done"), t + 1)
                return ps[t % 4]

            def take(o, i, f=ACT.Copy, **kw):
                A_(o, i, f, **kw).then_inc(S("tile_free"), 1)

            def ada_rows(g, par, ncols=512):
                act.wait_ge(S("ada_rows"), g + 1)
                A_(mrow[par][:, 0:ncols], ps[6 + par][0:2, 0:ncols], ACT.Copy).then_inc(S("ada_rows_out"), 1)

            act.wait_ge(S("vecs_in"), 16)
            A_(silc[:, 0], vec("c1", 0, 16).rearrange("p (s k) -> p k s", s=2), ACT.Silu)
            A_(silc[:, 1], vec("c2", 0, 16).rearrange("p (s k) -> p k s", s=2), ACT.Silu).then_inc(S("silu_c"), 1)
            for i, h in enumerate((f_h1, f_h2)):
                ada_rows(i, i)
                act.wait_ge(S("filt_arg"), i + 1)
                A_(h[0:64, :], f_t[0:64, :], ACT.Sin).then_inc(S("filt_sin"), 1)
            ada_rows(2, 0)
            ada_rows(3, 1)
            with act.Fori(1, 3) as i:
                for u in range(RING):
                    ada_rows(i * RING + u, u % 2)
            act.wait_ge(S("spectrum"), 1)
            for ft in range(4):
                A_(KS[:, ft, :], ps[(3, 4, 5, 0)[ft]][:, :], ACT.Copy)
            act.wait_ge(S("lb_arg"), 1)
            A_(lbc[:, 8:24], lbc[:, 8:24], ACT.Exp).then_inc(S("lb_exp"), 1)
            phase_end(act, "filters")

            norm(0)

            def gate_log(d):
                for h in range(HG_H):
                    i = A_(L2[d][:, h, :], L2[d][:, h, :], ACT.Ln, scale=lbc[:, 32 + 4 * d + h:33 + 4 * d + h],
                           bias=lbc[:, 24 + 4 * d + h:25 + 4 * d + h])
                i.then_inc(S("lf_ready"), 1)

            def scan_exps(d):
                act.wait_ge(S("ctx_arg"), d + 1)
                A_(KM, KM, ACT.Exp).then_inc(S("ctx_exp"), 1)
                act.wait_ge(S("hg_arg"), d + 1)
                A_(KM, QM, ACT.Exp, scale=-1.0)
                A_(QM, QM, ACT.Exp)
                A_(QD, QD, ACT.Exp).then_inc(S("hg_exp"), 1)
                act.wait_ge(S("ke_ready"), d + 1)
                A_(QD, LX[d], ACT.Exp)
                end = HG_C - 1 if d == 0 else 0
                A_(et[:, 0:32].rearrange("p (h c) -> p h c", h=4), LX[d].rearrange("p h (c k) -> p h c k", k=HG_C)[:, :, :, end], ACT.Exp)\
                    .then_inc(S("hg_exp2"), 1)

            for j, c in enumerate(WIN_ORDER[:8]):
                for nt in range(4):
                    o = tile()
                    if c == 0:
                        take(Qt[:, nt, :], o[:, 0:L])
                    elif c in (1, 2):
                        d = c - 1
                        A_(K2[d][:, nt, :], o[:, :], ACT.Sigmoid, scale=-1.0)
                        take(L2[d][:, nt, :], o[:, :], ACT.Sigmoid)
                    elif c == 3:
                        take(Vn[:, nt, :], o[:, :])
                    elif c == 4:
                        take(Gt[:, nt, :], o[:, 0:L], ACT.Silu)
                    else:
                        take(HYt[:, (c - 5) * 4 + nt, :], o[:, 0:L])
                if c in (1, 2):
                    d = c - 1
                    act.wait_ge(S("tile_free"), tiles[0])
                    gate_log(d)
                ada_rows(12 + j, j % 2)
                if c == 4:
                    scan_exps(0)
            phase_end(act, "projected")

            for d in range(2):
                if d == 1:
                    scan_exps(1)
                for j in range(4):
                    act.wait_ge(S("turned"), 4 * d + j + 1)
                    o = (KDN, KEN)[j // 2][:, (j % 2) * 4:(j % 2) * 4 + 4, :]
                    A_(o, ps[j][:, :].rearrange("p (a b) -> p a b", a=4), ACT.Copy).then_inc(S("turned_out"), 1)
                phase_end(act, "scan_f" if d == 0 else "scan_b")

            for b in range(2):
                v = ps[4 + b][:, :].rearrange("p (a b) -> p a b", a=2)
                A_(OS[:, 2 * b:2 * b + 2, :], v, ACT.Copy)
                i = A_(OSQ[:, 2 * b:2 * b + 2, :], v, ACT.Square)
            i.then_inc(S("o_squares"), 1)
            act.wait_ge(S("o_sum"), 1)
            for b in range(2):
                v = ps[4 + b][:, :].rearrange("p (a b) -> p a b", a=2)
                i = rsqrt(ORS[:, 2 * b:2 * b + 2, :], v, HG_D)
            i.then_inc(S("o_inverse"), 1)
            for nt in range(16):
                take(GL[:, nt, :], tile()[:, 0:L], ACT.Sigmoid)
                if nt % 4 == 3:
                    ada_rows(20 + nt // 4, (nt // 4) % 2)
            for tb in range(2):
                act.wait_ge(S("tokens_turned"), tb + 1)
                A_(UN[:, tb, :], ps[4 + tb][:, :], ACT.Copy).then_inc(S("un_ready"), 1)
            phase_end(act, "hyena")
            phase_end(act, "merged")

            norm(1)
            for b in range(4):
                act.wait_ge(S("tokens_turned"), 2 + b + 1)
                A_(HN[:, b // 2, (b % 2) * 512:(b % 2 + 1) * 512], ps[b][:, :], ACT.Copy).then_inc(S("h_natural"), 1)
            for i in range(2):
                act.wait_ge(S("rt_arg"), i + 1)
                o = RT[:, 16:24] if i == 0 else RT[:, 200:202]
                A_(o, o, ACT.Exp).then_inc(S("rt_exp"), 1)
            def high(c, cu, i16=0):
                act.wait_ge(full[cu % MRING], earrived(cu, i16))
                if not isinstance(c, int) or c >= 3:
                    act.wait_ge(used, MOE + c - 2)
                A_(EH[cu % 3], eslot(cu), ACT.Copy).then_inc(S("w_high"), 1)

            def gathered_high(b, e):
                act.wait_ge(S("gathered"), e + 1)
                A_(HGs[b][:, :, 0:CAP], ps[7][:, :].rearrange("p (a b) -> p a b", a=KT), ACT.Copy).then_inc(S("hg_high"), 1)

            def rows_out(m, e):
                act.wait_ge(S("row_sums"), 2 * e + m + 1)
                A_((UPR, GTR)[m], ps[5 - m][:, :], ACT.Copy).then_inc(S("rows_out"), 1)

            def expert(i, u):
                e = i * 2 + u
                turns = i * 6
                act.wait_ge(S("gate_up"), e + 1)
                A_(SIL, ps[6][:, 256:512].rearrange("p (a b) -> p a b", a=FT), ACT.Silu).then_inc(S("silu"), 1)
                if follow(i, u, 2):
                    gathered_high(u % 2, e + 2)
                if follow(i, u, 1):
                    rows_out(0, e + 1)
                    if follow(i, u, 2):
                        high(turns + 3 * u + 5, 3 * u + 5, i * 16)
                    rows_out(1, e + 1)
                for nb in range(2):
                    act.wait_ge(S("down"), 2 * e + nb + 1)
                    A_(YS[:, nb * 512:(nb + 1) * 512], ps[6 + nb][:, :], ACT.Copy).then_inc(S("ys_out"), 1)
                if follow(i, u, 2):
                    high(turns + 3 * u + 6, 3 * u + 6, i * 16)
                if follow(i, u, 1):
                    c = 3 * u + (7 if follow(i, u, 2) else 5)
                    high(turns + c, c, i * 16)

            act.wait_ge(S("h_parts"), 1)
            for c in range(3):
                high(c, c)
            for e in range(2):
                gathered_high(e, e)
            for m in range(2):
                rows_out(m, 0)
                high(3 + m, 3 + m)
            with act.Fori(0, NX // 2 - 1) as i:
                for u in range(2):
                    expert(i, u)
            for u in range(2):
                expert(NX // 2 - 1, u)
            act.wait_ge(S("passes_known"), 1)
            more = act.value_load(npass[0:1, 0:1])
            with act.If(more > 0):
                with act.Fori(0, more) as q:
                    with act.Fori(0, NX) as e:
                        g = q * NX + e
                        act.wait_ge(S("over_gathered"), g + 1)
                        A_(HG, ps[4][:, :], ACT.Copy).then_inc(S("over_gather_out"), 1)
                        act.wait_ge(S("over_gate_up"), g + 1)
                        A_(SIL, ps[5][:, 0:256].rearrange("p (a b) -> p a b", a=FT), ACT.Silu).then_inc(S("over_silu"), 1)
                        act.wait_ge(S("over_down"), g + 1)
                        A_(YS[0:CAP, 0:512], ps[6][0:CAP, :], ACT.Copy)
                        act.wait_ge(S("over_weights"), g + 1)
                        A_(YS[0:CAP, 512:1024], ps[7][0:CAP, :], ACT.Copy).then_inc(S("over_out"), 1)
            act.wait_ge(S("experts_added"), 1)
            norm(2)
            phase_end(act, "experts")

            ncall = 3
            for l in range(LAYERS):
                W = 2 * L if l == 0 else L
                if l == 0:
                    act.wait_ge(S("normed"), done[0])
                    act.wait_ge(S("ctx2_in"), 16)
                norm(ncall)
                ncall += 1
                lg = lgam[:, 0:8]
                link(A_(lg, vec("decay", l * 8, 8), ACT.Exp))
                A_(lg, lg, ACT.Ln, scale=-1.0, bias=vec("one")).then_inc(S("lgam"), 1)
                for j in range(8):
                    for nt in range(1 if j == 7 else 4):
                        o = tile()
                        if j == 0:
                            take(RQ[:, nt, 0:W], o[:, 0:W], scale=float(P) ** -0.5)
                        elif j == 1:
                            take(RK[:, nt, :], o[:, :])
                        elif j == 2:
                            take(RV[:, nt, :], o[:, :])
                        elif j == 3:
                            take(YT[:, nt, 0:W], o[:, 0:W], ACT.Silu)
                        elif j == 4 and nt < 2:
                            take(GQ[:, nt, 0:W], o[:, 0:W], scale=float(GL_K) ** -0.5)
                        elif j == 4:
                            take(GK[:, nt - 2, :], o[:, :])
                        elif j == 5:
                            take(GV[:, nt, :], o[:, :])
                        elif j == 6:
                            take(YT[:, 4 + nt, 0:W], o[:, 0:W], ACT.Silu)
                        else:
                            take(DT[0:32, :], o[0:32, :])
                act.wait_ge(S("col_arg"), l + 1)
                A_(lgam[:, 8:24], lgam[:, 8:24], ACT.Exp).then_inc(S("col_exp"), 1)
                phase_end(act, f"l{l}_in")

                def head_exps(h):
                    c = l * RT_H + h
                    act.wait_ge(S("r_arg"), c + 1)
                    A_(Wd[h % 2], Wd[h % 2], ACT.Exp)
                    A_(RQD[h % 2], RQD[h % 2], ACT.Exp).then_inc(S("r_exp"), 1)

                head_exps(0)
                for h in range(RT_H):
                    c = l * RT_H + h
                    b = h % 2
                    if h < RT_H - 1:
                        head_exps(h + 1)
                    act.wait_ge(S("rk_turned"), c + 1)
                    A_(RKN[b], ps[4][:, 0:2 * P].rearrange("p (a b) -> p a b", a=2), ACT.Copy).then_inc(S("rk_out"), 1)
                    act.wait_ge(S("r_state"), c + 1)
                    A_(RST[b], ps[5][:, 0:2 * P].rearrange("p (a b) -> p a b", a=2), ACT.Copy).then_inc(S("r_state_out"), 1)
                    act.wait_ge(S("r_head"), c + 1)
                    A_(OB[:, h, 0:W], ps[h][:, 0:W], ACT.Copy).then_inc(S("r_copied"), 1)
                for h in range(RT_H):
                    act.wait_ge(S("r_centred"), l * 4 + h + 1)
                    A_(OQ[:, h, 0:W], OB[:, h, 0:W], ACT.Square).then_inc(S("r_sq"), 1)
                for h in range(RT_H):
                    act.wait_ge(S("r_var"), l * 4 + h + 1)
                    rsqrt(OQ[:, h, 0:W], ps[h][:, 0:W], P).then_inc(S("r_inverse"), 1)
                phase_end(act, f"l{l}_ret")

                for d in range(2):
                    g = 2 * l + d
                    for t in range(2):
                        act.wait_ge(S("gate_mm"), 2 * g + t + 1)
                        i = A_(GT1[:, t, :], ps[4 + t][:, :], ACT.Identity, bias=vec("gate_b", l * 4 + d * 2 + t))
                    link(i)
                    link(A_(GT2, GT1, ACT.Abs))
                    link(A_(GT2, GT2, ACT.Exp, scale=-1.0))
                    A_(GT2, GT2, ACT.Ln, bias=vec("one")).then_inc(S("g_soft"), 1)
                    act.wait_ge(S("g_arg"), g + 1)
                    A_(GKE, GT2, ACT.Exp, scale=1.0 / 16).then_inc(S("g_exp"), 1)
                    A_(GKM, GT1, ACT.Exp, scale=-1.0 / 16)
                    A_(GQM, GT1, ACT.Exp, scale=1.0 / 16).then_inc(S("g_exp"), 1)
                    A_(GQD, GLg, ACT.Exp, scale=1.0 / 16)
                    end = P - 1 if d == 0 else 0
                    A_(et[:, 32:40], GLg.rearrange("p t (c k) -> p (t c) k", k=P)[:, :, end], ACT.Exp, scale=1.0 / 16).then_inc(S("g_exp"), 1)
                    for b in range(2):
                        act.wait_ge(S("gk_turned"), 2 * g + b + 1)
                        A_(GKN[:, 2 * b:2 * b + 2, :], ps[4 + b][:, :].rearrange("p (a b) -> p a b", a=2), ACT.Copy).then_inc(S("gk_out"), 1)
                    if d == 0:
                        phase_end(act, f"l{l}_gf")
                act.wait_ge(S("g_done"), l + 1)
                for h in range(4):
                    A_(OB[:, h, 0:W], ps[h][:, 0:W], ACT.Copy)
                    A_(OQ[:, h, 0:W], ps[h][:, 0:W], ACT.Square).then_inc(S("g_sq"), 1)
                for h in range(4):
                    act.wait_ge(S("g_sum"), 4 * l + h + 1)
                    rsqrt(OQ[:, h, 0:W], ps[4 + h][:, 0:W], P).then_inc(S("g_inverse"), 1)
                phase_end(act, f"l{l}_gb")

                act.wait_ge(S("w_out_added"), 8 * (l + 1))
                norm(ncall)
                ncall += 1
                phase_end(act, f"l{l}_out")

                with act.Fori(0, 4) as i:
                    for u in range(2):
                        n, turns, chunks, back = mlp_chunks(l, u, 0, i)
                        act.wait_ge(full[n % RING], arrived(n) + turns)
                        act.wait_ge(used, n - back + 1 + chunks)
                        A_(W1h, slot(n), ACT.Copy).then_inc(S("w_high"), 1)
                        n, turns, chunks, back = mlp_chunks(l, u, 1, i)
                        act.wait_ge(full[n % RING], arrived(n) + turns)
                        act.wait_ge(used, n - back + 1 + chunks)
                        A_(W2h, slot(n), ACT.Copy).then_inc(S("w_high"), 1)
                        for nt in range(4):
                            n = 32 * l + (i * 2 + u) * 4 + nt + 1
                            act.wait_ge(S("hid_mm"), n)
                            A_(HA[:, nt, 0:W], ps[nt][:, 0:W], ACT.Relu).then_inc(S("hid_relu"), 1)
                            act.wait_ge(S("hid_relu"), n)
                            A_(HAh[:, nt, 0:W], HA[:, nt, 0:W], ACT.Square)
                            A_(HA[:, nt, 0:W], HA[:, nt, 0:W], ACT.Square).then_inc(S("hid_square"), 1)
                        if l == 0:
                            for a in range(2):
                                ada_rows(24 + i * 4 + u * 2 + a, a, ADA_COLS)
                if l == 1:
                    act.wait_ge(S("mlp_bank_free"), 66 * 2)
                    norm(ncall)
                phase_end(act, f"l{l}_mlp")

        @block.gpsimd
        def _(pool):
            G = nc.gpsimd

            def bring(dst, src, sem):
                pool.dma_start(dst, src).then_inc(S(sem), 16)

            tall = lambda a: a.rearrange("(k p) n -> p k n", p=P)
            bring(vecs[:, :], T["vecs"], "vecs_in")
            bring(base[:, :], T["base"], "base_in")
            bring(A(15360, 4096), T["hy"], "filter_in")
            bring(f_z[0:33, :], T["hy_z"], "filter_in")
            bring(f_w1[0:33, :], T["hy_filt_w1"], "filter_in")
            bring(f_w2[0:64, :], T["hy_filt_w2"], "filter_in")
            bring(f_w3[0:64, :], T["hy_filt_w3"], "filter_in")
            bring(X[:, :, 0:L], tall(T["x"]), "x_in")
            bring(X[:, :, L:2 * L], tall(T["ctx"]), "x_in")
            bring(A3(0, KT, L), tall(T["pos"]), "x_in")
            bring(hmask[:, :, :], T["hg_mask"].rearrange("p (a b) -> p a b", a=2), "x_in")
            for name in ("filters", "projected", "scan_f", "scan_b"):
                phase_end(pool, name)
            bring(A(15360, 2048), T["hy"][:, 0:2048], "tables_in")
            phase_end(pool, "hyena")
            phase_end(pool, "merged")
            bring(mtab, T["moe"], "tables_in")
            bring(WR, tall(T["wr"]), "tables_in")
            phase_end(pool, "experts")
            bring(X[:, :, L:2 * L], tall(T["ctx_2"]), "ctx2_in")
            bring(b2t, T["b2"], "b2_in")
            bring(gmask, T["b2_mask"].rearrange("p (a b) -> p a b", a=2), "b2_in")
            for l in range(LAYERS):
                bring(GUP[0:32, :, :], T["gup"][l].rearrange("d r n -> r d n"), "b2_in")
                if l:
                    phase_end(pool, "l0_mlp")
                W = 2 * L if l == 0 else L
                for name in ("in", "ret", "gf", "gb", "out"):
                    phase_end(pool, f"l{l}_{name}")
                with pool.Fori(0, 4) as i:
                    for u in range(2):
                        j = i * 2 + u
                        pool.wait_ge(S("w_high"), NMOE + 16 * l + j * 2 + 1)
                        n = mlp_chunks(l, u, 0, i)[0]
                        G.tensor_tensor(low(n), slot(n), W1h.bitcast(F32), ALU.subtract).then_inc(S("w1_split"), 1)
                        for nt in range(4):
                            pool.wait_ge(S("hid_square"), 32 * l + j * 4 + nt + 1)
                            G.tensor_tensor(HAl[:, nt, 0:W], HA[:, nt, 0:W], HAh[:, nt, 0:W].bitcast(F32), ALU.subtract)\
                                .then_inc(S("hid_out"), 1)
                if l:
                    phase_end(pool, "l1_mlp")

        @block.vector
        def _(dve):
            V = nc.vector
            own = [0]

            def link(ins):
                own[0] += 1
                ins.then_inc(S("dve_own"), 1)
                dve.wait_ge(S("dve_own"), own[0])

            def bc(ap, shape):
                return ap.broadcast_to(shape)

            def take_chunk(b, g, par, c0, ncols=512):
                dve.wait_ge(S("ada_turned"), g + 1)
                m = ncols // P
                lo = VOFF["ada_b" if b == 0 else "ada_b2"][0] + (48 if b == 2 else 0)
                V.tensor_tensor(mod[:, b, bass.ds(c0, m), :], ps[6 + par][:, 0:2 * m].rearrange("p (a b) -> p a b", b=2),
                                bc(vecs[:, bass.ds(c0 + lo, m)].unsqueeze(2), [P, m, 2]), ALU.add).then_inc(S("ada_out"), 1)

            def gains(b):
                for w in range(2):
                    g = vec(("n1", "n1_2", "n1_2")[b] if w == 0 else ("n2", "n2_2", "n2_2")[b], 8 if b == 2 else 0, 8)
                    link(V.scalar_tensor_tensor(gsc[:, b, w], mod[:, b, 24 * w + 8:24 * w + 16, :], 1.0,
                                                bc(g.unsqueeze(2), [P, KT, 2]), ALU.add, ALU.mult))

            def norm(call):
                N = CALLS[call][2]
                dve.wait_ge(S("rms_ready"), call + 1)
                for a in range(2):
                    V.tensor_tensor(H[:, 4 * a:4 * a + 4, 0:N], X[:, 4 * a:4 * a + 4, 0:N],
                                    bc(RS[:, 0:N].unsqueeze(1), [P, 4, N]), ALU.mult).then_inc(S("scaled"), 1)

            def two(ap):
                return ap.rearrange("p (a b) -> p a b", a=2)

            dve.wait_ge(S("vecs_in"), 16)
            link(V.tensor_tensor(lbc[:, 0:8], vec("lb", 0, 8), vec("lb", 8, 8), ALU.max))
            V.tensor_tensor(lbc[:, 8:16], vec("lb", 0, 8), lbc[:, 0:8], ALU.subtract)
            V.tensor_tensor(lbc[:, 16:24], vec("lb", 8, 8), lbc[:, 0:8], ALU.subtract).then_inc(S("lb_arg"), 1)
            for k in range(2):
                dve.drain().then_inc(S("ada_out"), 1)
            TWO_PI, ROUND = 2 * np.pi, 12582912.0
            HI = 6.28125
            for i in range(2):
                dve.wait_ge(S("filt_mm"), i + 1)
                a, k = f_t[0:64, :], f_nat[0:64, 0, 0:L]
                if i:
                    dve.wait_ge(S("filt_sin"), 1)
                f = vec("f1" if i == 0 else "f2", 0, 2)
                link(V.tensor_scalar(a, ps[0][0:64, i * L:(i + 1) * L], f[0:64, 0:1], f[0:64, 1:2], ALU.add, ALU.mult))
                link(V.tensor_scalar(k, a, 1.0 / TWO_PI, ROUND, ALU.mult, ALU.add))
                link(V.tensor_scalar(k, k, ROUND, None, ALU.subtract))
                link(V.scalar_tensor_tensor(a, k, -HI, a, ALU.mult, ALU.add))
                link(V.scalar_tensor_tensor(a, k, -(TWO_PI - HI), a, ALU.mult, ALU.add))
                V.tensor_scalar(a, a, 3.1415925, -3.1415925, ALU.min, ALU.max).then_inc(S("filt_arg"), 1)
                take_chunk(0, i, i, 4 * i)
            for d in range(2):
                dve.wait_ge(S("filt_nat"), d + 1)
                for tb in range(2):
                    i = V.tensor_tensor(f_nat[:, tb, :], f_dec[:, tb, :], ps[1 + tb][:, :], ALU.mult)
                i.then_inc(S("filt_dec"), 1)
                take_chunk(0, 2 + d, d, 8 + 4 * d)
            with dve.Fori(1, 3) as i:
                for u in range(RING):
                    take_chunk(0, i * RING + u, u % 2, (i * RING + u) * 4)
            dve.wait_ge(S("x_in"), 16 * 4)
            dve.wait_ge(S("base_in"), 16)
            V.tensor_tensor(X[:, :, 0:L], X[:, :, 0:L], A3(0, KT, L), ALU.add)
            dve.wait_ge(S("lb_exp"), 1)
            link(V.tensor_tensor(lbc[:, 0:8], lbc[:, 8:16], lbc[:, 16:24], ALU.add))
            link(V.reciprocal(lbc[:, 0:8], lbc[:, 0:8]))
            link(V.tensor_tensor(lbc[:, 24:32], lbc[:, 8:16], lbc[:, 0:8], ALU.mult))
            V.tensor_scalar(lbc[:, 32:40], lbc[:, 24:32], -1.0, 1.0, ALU.mult, ALU.add)
            dve.wait_ge(S("ada_out"), 14)
            gains(0)
            phase_end(dve, "filters")
            norm(0)

            def scan_prep(d):
                dve.wait_ge(S("lf_ready"), d + 1)
                for h in range(HG_H):
                    V.tensor_scalar(K2[d][:, h, :], K2[d][:, h, :], lbc[:, 32 + 4 * d + h:33 + 4 * d + h], None, ALU.mult)
                one = bc(ones[:, 0:1], [P, L])
                for h in range(HG_H):
                    lc, o, lx = LC[d][:, h, :], KM[:, h, :], LX[d][:, h, :]
                    if d == 0:
                        V.tensor_tensor_scan(o[:, ::-1], one, lc[:, ::-1], 0.0, ALU.mult, ALU.add)
                        i = V.tensor_tensor_scan(lx, r32[0], lx, 0.0, ALU.mult, ALU.add)
                    else:
                        V.tensor_tensor_scan(o, one, lc, 0.0, ALU.mult, ALU.add)
                        i = V.tensor_tensor_scan(lx[:, ::-1], r32[1][:, ::-1], lx[:, ::-1], 0.0, ALU.mult, ALU.add)
                link(i)
                V.tensor_tensor(KM, KM, LC[d], ALU.subtract).then_inc(S("ctx_arg"), 1)
                v = lambda a: a.rearrange("p h (c k) -> p h c k", k=HG_C)
                mid, end = (16, 31) if d == 0 else (15, 0)
                for h in range(HG_H):
                    B = LX[d][:, h, :].rearrange("p (c k) -> p c k", k=HG_C)
                    m = bc(B[:, :, mid:mid + 1], [P, 8, HG_C])
                    e = bc(B[:, :, end:end + 1], [P, 8, HG_C])
                    V.tensor_tensor(QM[:, h, :].rearrange("p (c k) -> p c k", k=HG_C), B, m, ALU.subtract)
                    i = V.tensor_tensor(QD[:, h, :].rearrange("p (c k) -> p c k", k=HG_C), e, B, ALU.subtract)
                link(i)
                dve.wait_ge(S("ctx_exp"), d + 1)
                V.tensor_tensor(KC[d], KC[d], KM, ALU.mult).then_inc(S("kd_ready"), 1)
                dve.wait_ge(S("kd_ready"), d + 1)
                dve.drain().then_inc(S("hg_arg"), 1)
                dve.wait_ge(S("hg_exp"), d + 1)
                V.tensor_tensor(KM, KM, KX[d], ALU.mult)
                V.tensor_tensor(QM, QM, Qt, ALU.mult).then_inc(S("qm_ready"), 1)
                dve.wait_ge(S("qm_ready"), d + 1)
                V.tensor_tensor(KX[d], KX[d], QD, ALU.mult).then_inc(S("ke_ready"), 1)
                dve.wait_ge(S("hg_exp2"), d + 1)
                link(V.tensor_tensor(QD, QD, Qt, ALU.mult))

            for j in range(4):
                take_chunk(1, 12 + j, j % 2, 4 * j)
            scan_prep(0)
            link(V.memset(SC, 0.0))
            for j in range(4, 8):
                take_chunk(1, 12 + j, j % 2, 4 * j)
            phase_end(dve, "projected")

            for d in range(2):
                if d == 1:
                    link(V.memset(SC, 0.0))
                    scan_prep(1)
                dve.wait_ge(S("ctx_state"), d + 1)
                V.tensor_copy(ST[:, 0, :], ps[0][:, :]).then_inc(S("states_out"), 1)
                for tb in range(2):
                    dve.wait_ge(S("scores"), 2 * d + tb + 1)
                    V.copy_predicated(SC[:, tb * 4:tb * 4 + 4, :], bc(hmask[:, d, :].unsqueeze(1), [P, 4, P]),
                                      ps[6 + tb][:, :].rearrange("p (a b) -> p a b", a=4)).then_inc(S("masked"), 1)
                for n in range(7):
                    ch = n if d == 0 else 7 - n
                    dve.wait_ge(S("updates"), 2 * d + n // 4 + 1)
                    dve.wait_ge(S("states_out"), 8 * d + n + 1)
                    if n + 1 >= 4:
                        dve.wait_ge(S("inter"), 8 * d + n - 2)
                    o, s = [ST[:, k % 4, :].rearrange("p (h v) -> p h v", h=4) for k in (n + 1, n)]
                    e = et[:, 0:32].rearrange("p (h c) -> p h c", h=4)[:, :, ch:ch + 1]
                    link(V.tensor_tensor(o, s, bc(e, [P, 4, P]), ALU.mult))
                    V.tensor_tensor(o, o, ps[ch % 4][:, :].rearrange("p (h v) -> p h v", h=4), ALU.add).then_inc(S("states_out"), 1)
                phase_end(dve, "scan_f" if d == 0 else "scan_b")

            for j in range(8, 12):
                take_chunk(1, 12 + j, j % 2, 4 * j)
            for i in range(12):
                link(V.tensor_scalar(CV[:, i, :], HYt[:, i, :], vec("conv_w", 12 + i), vec("conv_b", i), ALU.mult, ALU.add))
                link(V.scalar_tensor_tensor(CV[:, i, 1:L], HYt[:, i, 0:L - 1], vec("conv_w", i), CV[:, i, 1:L], ALU.mult, ALU.add))
                link(V.scalar_tensor_tensor(CV[:, i, 0:L - 1], HYt[:, i, 1:L], vec("conv_w", 24 + i), CV[:, i, 0:L - 1], ALU.mult, ALU.add))
            V.tensor_tensor(UV, CV[:, 0:4, :], CV[:, 4:8, :], ALU.mult).then_inc(S("uv_ready"), 1)
            dve.wait_ge(S("o_inverse"), 1)
            link(V.tensor_tensor(OS, OS, ORS, ALU.mult))
            link(V.scalar_tensor_tensor(OS, OS, vec("hg_g"), Gt, ALU.mult, ALU.mult))
            dve.wait_ge(S("ada_out"), 2 + 24)
            gains(1)
            dve.wait_ge(S("u_spec"), 1)
            for f in range(2):
                re, im = ps[f][:, :], ps[2 + f][:, :]
                V.tensor_tensor(YF[:, f, :], KS[:, f, :], re, ALU.mult)
                V.tensor_tensor(UT[:, 0, :], KS[:, 2 + f, :], im, ALU.mult)
                V.tensor_tensor(YF[:, 2 + f, :], KS[:, 2 + f, :], re, ALU.mult)
                link(V.tensor_tensor(UT[:, 1, :], KS[:, f, :], im, ALU.mult))
                V.tensor_tensor(YF[:, f, :], YF[:, f, :], UT[:, 0, :], ALU.subtract)
                link(V.tensor_tensor(YF[:, 2 + f, :], YF[:, 2 + f, :], UT[:, 1, :], ALU.add))
            V.tensor_tensor(YF[0:1, 0, :], KS[0:1, 0, :], ps[0][0:1, :], ALU.mult)
            V.tensor_tensor(YF[0:1, 2, :], KS[0:1, 2, :], ps[2][0:1, :], ALU.mult).then_inc(S("y_spec"), 1)
            dve.wait_ge(S("y_time"), 1)
            for c in range(HYT):
                i = V.scalar_tensor_tensor(UV[:, c, :], UV[:, c, :], vec("hy_d", c), ps[4 + c // 2][:, (c % 2) * L:(c % 2 + 1) * L],
                                           ALU.mult, ALU.add)
            link(i)
            link(V.tensor_tensor(YB, UV, CV[:, 8:12, :], ALU.mult))
            phase_end(dve, "hyena")

            for nt in range(KT):
                dve.wait_ge(S("merge_mm"), nt + 1)
                o = ps[nt % 4]
                V.tensor_tensor(MIX[:, nt, :], GL[:, nt, :], o[:, 0:L], ALU.mult)
                link(V.tensor_tensor(MT[:, nt, :], GL[:, 8 + nt, :], o[:, L:2 * L], ALU.mult))
                V.tensor_tensor(MIX[:, nt, :], MIX[:, nt, :], MT[:, nt, :], ALU.add).then_inc(S("merged"), 1)
            for t in range(KT):
                dve.wait_ge(S("out_mm"), t + 1)
                V.scalar_tensor_tensor(X[:, t, 0:L], ps[4 + t % 2][:, 0:L], mod[:, 0, 16 + t, 0:1], X[:, t, 0:L],
                                       ALU.mult, ALU.add).then_inc(S("out_added"), 1)
            phase_end(dve, "merged")

            norm(1)
            V.memset(SW, 0.0).then_inc(S("sw_zero"), 1)
            V.memset(RKM[:, :, NX:NX + 4], -1.0)
            V.memset(CMB[:, :, NX:NX + 4], 0.0)
            dve.wait_ge(S("logits"), 1)
            dve.wait_ge(S("h_natural"), 4)
            for part in range(3):
                i = V.tensor_copy(HB[:, part], HN)
                if part < 2:
                    link(i)
                    link(V.tensor_tensor(HN, HN, HB[:, part], ALU.subtract))
            i.then_inc(S("h_parts"), 1)
            link(V.tensor_tensor(LG, ps[4][:, 0:2 * NR].rearrange("p (a b) -> p a b", a=2),
                                 bc(vec("rbias", 0, NR).unsqueeze(1), [P, TB, NR]), ALU.add))

            def r3(off, n):
                return RT[:, off:off + 2 * n].rearrange("p (a b) -> p a b", a=2)

            def onehot_of_max(x, n, mx, cum, oh):
                link(V.tensor_reduce(mx, x, AX.X, ALU.max))
                link(V.tensor_tensor(oh, x, bc(mx, [P, TB, n]), ALU.is_equal))
                for b in range(TB):
                    i = V.tensor_tensor_scan(cum[:, b, :], bc(ones[:, 0:1], [P, n]), oh[:, b, :], 0.0, ALU.mult, ALU.add)
                link(i)
                link(V.scalar_tensor_tensor(oh, cum, 1.0, oh, ALU.is_equal, ALU.mult))

            gm, gcum, goh = r3(0, 1), r3(24, 4), r3(32, 4)
            gl_ = LG[:, :, 0:NG]
            onehot_of_max(gl_, NG, gm, gcum, goh)
            V.tensor_tensor(r3(16, 4), gl_, bc(gm, [P, TB, NG]), ALU.subtract).then_inc(S("rt_arg"), 1)
            prod = RT[:, 48:112].rearrange("p (b g e) -> p b g e", b=TB, g=NG)
            for b in range(TB):
                i = V.tensor_tensor(prod[:, b], LG[:, b, NG:NR].rearrange("p (g e) -> p g e", g=NG),
                                    bc(goh[:, b, :].unsqueeze(2), [P, NG, NE]), ALU.mult)
            link(i)
            el = r3(112, NE)
            for b in range(TB):
                i = V.tensor_reduce(el[:, b, :], prod[:, b].rearrange("p g e -> p e g"), AX.X, ALU.add)
            link(i)
            m1, c1, o1 = r3(128, 1), r3(130, NE), r3(146, NE)
            m2, c2, o2, el2 = r3(162, 1), r3(164, NE), r3(180, NE), r3(220, NE)
            onehot_of_max(el, NE, m1, c1, o1)
            link(V.scalar_tensor_tensor(el2, o1, -1e30, el, ALU.mult, ALU.add))
            onehot_of_max(el2, NE, m2, c2, o2)
            ex = r3(200, 1)
            V.tensor_tensor(ex, m2, m1, ALU.subtract).then_inc(S("rt_arg"), 1)
            dve.wait_ge(S("rt_exp"), 2)
            zs, one_e, w1, w2 = r3(240, 1), r3(242, 1), r3(244, 1), r3(246, 1)
            V.tensor_reduce(zs, r3(16, 4), AX.X, ALU.add)
            link(V.tensor_scalar(one_e, ex, 1.0, None, ALU.add))
            link(V.tensor_tensor(zs, zs, one_e, ALU.mult))
            link(V.reciprocal(w1, zs))
            link(V.tensor_tensor(w2, w1, ex, ALU.mult))
            s8, c8, t8 = r3(250, NE), r3(266, NE), r3(282, NE)
            V.tensor_tensor(s8, o1, o2, ALU.add)
            V.tensor_tensor(c8, o1, bc(w1, [P, TB, NE]), ALU.mult)
            link(V.tensor_tensor(t8, o2, bc(w2, [P, TB, NE]), ALU.mult))
            link(V.tensor_tensor(c8, c8, t8, ALU.add))
            for b in range(TB):
                ohb = bc(goh[:, b, :].unsqueeze(2), [P, NG, NE])
                V.tensor_tensor(CMB[:, b, 0:NX].rearrange("p (g e) -> p g e", g=NG), bc(c8[:, b:b + 1, :], [P, NG, NE]), ohb, ALU.mult)
                i = V.tensor_tensor(SELX[:, b, :].rearrange("p (g e) -> p g e", g=NG), bc(s8[:, b:b + 1, :], [P, NG, NE]), ohb, ALU.mult)
            i.then_inc(S("selected"), 1)
            dve.wait_ge(S("ranks"), 1)
            dve.wait_ge(S("selected"), 1)
            link(V.scalar_tensor_tensor(RKM[:, :, 0:NX], ps[5][:, 0:2 * NX].rearrange("p (a b) -> p a b", a=2), 1.0, SELX, ALU.add, ALU.mult))
            link(V.tensor_scalar(RKM[:, :, 0:NX], RKM[:, :, 0:NX], -1.0, None, ALU.add))
            cnt, over = RT[0:1, 300:301], RT[0:1, 301:304]
            link(V.tensor_reduce(cnt, ps[5][0:1, 2 * NX:3 * NX], AX.X, ALU.max))
            for k in range(3):
                i = V.tensor_scalar(over[:, k:k + 1], cnt, float(CAP * (k + 1)), None, ALU.is_gt)
            link(i)
            link(V.tensor_reduce(RT[0:1, 304:305], over, AX.X, ALU.add))
            V.tensor_copy(npass[0:1, 0:1], RT[0:1, 304:305]).then_inc(S("passes_known"), 1)

            def onehot(e, buf, sem=None):
                for tb in range(TB):
                    i = V.tensor_scalar(SGv[:, buf, tb, :], IOTA[:, 0:CAP], RKM[:, tb, bass.ds(e, 1)], None, ALU.is_equal)
                if sem:
                    i.then_inc(S(sem), 1)

            def weighted(e, buf, sem):
                for tb in range(TB):
                    i = V.tensor_scalar(SWv[:, buf, tb, :], IOTA, RKM[:, tb, bass.ds(e, 1)], CMB[:, tb, bass.ds(e, 1)],
                                        ALU.is_equal, ALU.mult)
                i.then_inc(S(sem), 1)

            def scatter_weights(e):
                dve.wait_ge(S("weights_turned"), e + 1)
                V.tensor_copy(SWT, ps[5][:, 0:L]).then_inc(S("weights_out"), 1)

            def low_part(c, cu):
                dve.wait_ge(S("w_high"), c + 1)
                V.tensor_tensor(elow(cu), eslot(cu), EH[cu % 3].bitcast(F32), ALU.subtract).then_inc(S("w_split"), 1)

            def gathered_low(b, e):
                dve.wait_ge(S("hg_high"), e + 1)
                V.tensor_tensor(HGs[b][:, :, CAP:2 * CAP], ps[7][:, :].rearrange("p (a b) -> p a b", a=KT),
                                HGs[b][:, :, 0:CAP].bitcast(F32), ALU.subtract).then_inc(S("hg_low"), 1)

            def expert(i, u):
                e = i * 2 + u
                turns = i * 6
                dve.wait_ge(S("silu"), e + 1)
                V.tensor_tensor(HID, SIL, ps[6][:, 0:256].rearrange("p (a b) -> p a b", a=FT), ALU.mult).then_inc(S("hid_parts"), 1)
                dve.wait_ge(S("hid_parts"), 2 * e + 1)
                V.tensor_copy(HIDs[:, :, 0:CAP], HID).then_inc(S("hid_parts"), 1)
                dve.wait_ge(S("hid_parts"), 2 * e + 2)
                V.tensor_tensor(HIDs[:, :, CAP:2 * CAP], HID, HIDs[:, :, 0:CAP].bitcast(F32), ALU.subtract).then_inc(S("hidden"), 1)
                c = 3 * u + (4 if follow(i, u, 1) else 2)
                low_part(turns + c, c)
                if follow(i, u, 2):
                    gathered_low(u % 2, e + 2)
                if follow(i, u, 1):
                    weighted(e + 1, (u + 1) % 2, "sw_ready")
                if follow(i, u, 3):
                    onehot(e + 3, (u + 1) % 2, "onehot")
                if follow(i, u, 2):
                    low_part(turns + 3 * u + 5, 3 * u + 5)
                if follow(i, u, 1):
                    scatter_weights(e + 1)
                if follow(i, u, 2):
                    low_part(turns + 3 * u + 6, 3 * u + 6)

            dve.wait_ge(S("cleared"), 1)
            onehot(0, 0, "onehot")
            onehot(1, 1, "onehot")
            weighted(0, 0, "sw_ready")
            for c in range(2):
                low_part(c, c)
            for e in range(2):
                gathered_low(e, e)
            dve.wait_ge(S("gathered"), 2)
            onehot(2, 0, "onehot")
            for c in range(2, 4):
                low_part(c, c)
            scatter_weights(0)
            with dve.Fori(0, NX // 2 - 1) as i:
                for u in range(2):
                    expert(i, u)
            for u in range(2):
                expert(NX // 2 - 1, u)
            dve.wait_ge(S("passes_known"), 1)
            more = dve.value_load(npass[0:1, 0:1])
            with dve.If(more > 0):
                with dve.Fori(0, more) as q:
                    dve.wait_ge(S("over_begun"), q * NX + 1)
                    V.tensor_scalar(RKM, RKM, -float(CAP), None, ALU.add).then_inc(S("over_ranked"), 1)
                    with dve.Fori(0, NX) as e:
                        g = q * NX + e
                        dve.wait_ge(S("over_ranked"), q + 1)
                        dve.wait_ge(S("over_begun"), g + 1)
                        onehot(e, 0)
                        weighted(e, 0, "over_onehot")
                        dve.wait_ge(S("over_silu"), g + 1)
                        V.tensor_tensor(HID, SIL, ps[5][:, 256:512].rearrange("p (a b) -> p a b", a=FT), ALU.mult).then_inc(S("over_hidden"), 1)
                        dve.wait_ge(S("over_turned"), g + 1)
                        V.tensor_copy(SWT[0:CAP, :], ps[4][0:CAP, 0:L]).then_inc(S("over_weights"), 1)
            dve.wait_ge(S("experts_done"), 1)
            for k in range(KT):
                i = V.scalar_tensor_tensor(X[:, k, 0:L], ps[k // 2][:, (k % 2) * L:(k % 2 + 1) * L], mod[:, 0, 40 + k, 0:1], X[:, k, 0:L],
                                           ALU.mult, ALU.add)
            i.then_inc(S("experts_added"), 1)
            dve.wait_ge(S("experts_added"), 1)
            norm(2)
            phase_end(dve, "experts")

            ncall = 3
            def split_norm(N, before, per):
                for k in range(KT):
                    dve.wait_ge(S("normed"), before + per * (k + 1))
                    link(V.tensor_copy(Hh[:, k, 0:N], H[:, k, 0:N]))
                    i = V.tensor_tensor(Hl[:, k, 0:N], H[:, k, 0:N], Hh[:, k, 0:N].bitcast(F32), ALU.subtract)
                i.then_inc(S("h_split"), 1)

            def split_chunk(n, c=KT * 512):
                dve.wait_ge(full[n % RING], arrived(n))
                dve.wait_ge(used, n + 1 - RING + 1)
                link(V.tensor_copy(low(n + 1)[:, 0:c], slot(n)[:, 0:c]))
                V.tensor_tensor(low(n)[:, 0:c], slot(n)[:, 0:c], low(n + 1)[:, 0:c].bitcast(F32), ALU.subtract)\
                    .then_inc(full[(n + 1) % RING], 16)

            for l in range(LAYERS):
                W = 2 * L if l == 0 else L
                first = (L0, L1)[l]
                split_chunk(first)
                norm(ncall)
                ncall += 1
                split_norm(2 * L, 32 + 32 * l, 2)
                for j in range(1, 7):
                    split_chunk(first + 2 * j)
                split_chunk(first + 14, KT * 2 * RANK)
                dve.wait_ge(S("lgam"), l + 1)
                dve.wait_ge(S("b2_in"), 16 * (3 + l))
                for k in range(4):
                    i = V.tensor_scalar(lgam[:, 8 + 4 * k:12 + 4 * k], lgam[:, 4 * (k // 2):4 * (k // 2) + 4], COLT[:, k:k + 1], None, ALU.mult)
                i.then_inc(S("col_arg"), 1)
                for m, M in enumerate((RQ, RK)):
                    for a in range(2):
                        dve.wait_ge(S("swapped"), 4 * l + 2 * m + a + 1)
                        i = V.tensor_tensor(ROT[:, 2 * a:2 * a + 2, :], bc(RSIN.unsqueeze(1), [P, 2, L]),
                                            ps[4 + 2 * m + a][:, :].rearrange("p (a b) -> p a b", a=2), ALU.mult)
                    link(i)
                    link(V.tensor_tensor(M[:, :, 0:L], M[:, :, 0:L], bc(RCOS.unsqueeze(1), [P, 4, L]), ALU.mult))
                    link(V.tensor_tensor(M[:, :, 0:L], M[:, :, 0:L], ROT, ALU.add))
                phase_end(dve, f"l{l}_in")

                def head_prep(h):
                    c = l * RT_H + h
                    b = h % 2
                    if h >= 2:
                        dve.wait_ge(S("r_head"), c - 1)
                    lf, lb_ = lgam[:, h:h + 1], lgam[:, 4 + h:5 + h]
                    link(V.tensor_scalar(Wd[b], EF, lf, None, ALU.mult))
                    V.scalar_tensor_tensor(Wd[b], EB, lb_, Wd[b], ALU.mult, ALU.add)
                    V.tensor_scalar(RQD[b][:, 0, :], ROWT[0], lf, None, ALU.mult)
                    V.tensor_scalar(RQD[b][:, 1, :], ROWT[1], lb_, None, ALU.mult).then_inc(S("r_arg"), 1)
                    for d in range(2):
                        for tb in range(2):
                            k = 8 + (2 * d + tb) * 4 + h
                            V.tensor_scalar(RVD[b][:, d, tb, :], RV[:, 2 + tb, h * P:(h + 1) * P], lgam[:, k:k + 1], None, ALU.mult)
                    dve.wait_ge(S("r_exp"), c + 1)
                    V.tensor_tensor(RQD[b], RQD[b], bc(RQ[:, h, 0:L].unsqueeze(1), [P, 2, L]), ALU.mult).then_inc(S("r_prep"), 1)

                dve.wait_ge(S("col_exp"), l + 1)
                head_prep(0)
                for h in range(RT_H):
                    c = l * RT_H + h
                    if h < RT_H - 1:
                        head_prep(h + 1)
                    for side in ((0, 1) if l == 0 else (0,)):
                        q = c * 2 + side if l == 0 else 2 * RT_H + h
                        dve.wait_ge(S("r_scores"), q + 1)
                        V.tensor_tensor(RSC[side], Wd[h % 2], ps[6 + side][:, :].rearrange("p (a b) -> p a b", a=2), ALU.mult)\
                            .then_inc(S("r_decayed"), 1)
                for h in range(RT_H):
                    dve.wait_ge(S("r_mean"), l * 4 + h + 1)
                    V.scalar_tensor_tensor(OB[:, h, 0:W], ps[4 + h][:, 0:W], -1.0 / P, OB[:, h, 0:W], ALU.mult, ALU.add).then_inc(S("r_centred"), 1)
                for h in range(RT_H):
                    dve.wait_ge(S("r_inverse"), l * 4 + h + 1)
                    link(V.tensor_tensor(OB[:, h, 0:W], OB[:, h, 0:W], OQ[:, h, 0:W], ALU.mult))
                    V.tensor_tensor(YT[:, h, 0:W], YT[:, h, 0:W], OB[:, h, 0:W], ALU.mult)
                phase_end(dve, f"l{l}_ret")

                nx = 4 if l == 0 else 2
                for d in range(2):
                    g = 2 * l + d
                    i = V.memset(GSC, 0.0)
                    if d == 0:
                        i.then_inc(S("gsc_clear"), 1)
                    dve.wait_ge(S("g_soft"), g + 1)
                    link(V.scalar_tensor_tensor(GLg, GT1, 0.0, GT2, ALU.min, ALU.subtract))
                    for t in range(2):
                        lg, r = GLg[:, t, :], R128[d]
                        if d:
                            lg, r = lg[:, ::-1], r[:, ::-1]
                        i = V.tensor_tensor_scan(lg, r, lg, 0.0, ALU.mult, ALU.add)
                    link(i)
                    v = lambda a: a.rearrange("p t (c k) -> p (t c) k", k=P)
                    mid, end = (63, 127) if d == 0 else (64, 0)
                    V.tensor_tensor(v(GT1), v(GLg), bc(v(GLg)[:, :, mid:mid + 1], [P, 8, P]), ALU.subtract)
                    V.tensor_tensor(v(GT2), bc(v(GLg)[:, :, end:end + 1], [P, 8, P]), v(GLg), ALU.subtract).then_inc(S("g_arg"), 1)
                    dve.wait_ge(S("g_exp"), 3 * g + 1)
                    V.tensor_tensor(GKE, GKE, GK, ALU.mult).then_inc(S("gke_ready"), 1)
                    dve.wait_ge(S("g_exp"), 3 * g + 2)
                    V.tensor_tensor(GKM, GKM, GK, ALU.mult)
                    V.tensor_tensor(GQM[:, :, 0:W], GQM[:, :, 0:W], GQ[:, :, 0:W], ALU.mult).then_inc(S("gqm_ready"), 1)
                    dve.wait_ge(S("g_exp"), 3 * g + 3)
                    link(V.tensor_tensor(GQD[:, :, 0:W], GQD[:, :, 0:W], GQ[:, :, 0:W], ALU.mult))
                    for ch in range(nx):
                        dve.wait_ge(S("g_scores"), (0, 4, 8, 10)[g] + (ch | 1) + 1)
                        for par in range(2):
                            V.copy_predicated(GSC[:, par * 8 + ch * 2:par * 8 + ch * 2 + 2, :], bc(gmask[:, d, :].unsqueeze(1), [P, 2, P]),
                                              ps[6 + par][:, (ch % 2) * 2 * P:(ch % 2 + 1) * 2 * P].rearrange("p (a b) -> p a b", a=2))\
                                .then_inc(S("g_masked"), 1)
                    order = [2, 3, 0, 1] if d == 0 else [3, 2, 1, 0]
                    for n in range(3):
                        dve.wait_ge(S("g_update"), 3 * g + max(n + 1, 2))
                        U = ps[4 + n // 2][:, (n % 2) * L:(n % 2 + 1) * L].rearrange("p (t v) -> p t v", t=2)
                        if n == 0:
                            V.tensor_copy(GST[:, 0], U).then_inc(S("g_state"), 1)
                            continue
                        dve.wait_ge(S("g_state"), 3 * g + n)
                        e = et[:, 32:40].rearrange("p (t c) -> p t c", t=2)[:, :, order[n]:order[n] + 1]
                        link(V.tensor_tensor(GST[:, n], GST[:, n - 1], bc(e, [P, 2, P]), ALU.mult))
                        V.tensor_tensor(GST[:, n], GST[:, n], U, ALU.add).then_inc(S("g_state"), 1)
                    if d == 0:
                        phase_end(dve, f"l{l}_gf")
                for h in range(4):
                    dve.wait_ge(S("g_inverse"), 4 * l + h + 1)
                    link(V.tensor_tensor(OB[:, h, 0:W], OB[:, h, 0:W], OQ[:, h, 0:W], ALU.mult))
                    V.scalar_tensor_tensor(YT[:, 4 + h, 0:W], OB[:, h, 0:W], vec("gla_g", l), YT[:, 4 + h, 0:W], ALU.mult, ALU.mult)
                phase_end(dve, f"l{l}_gb")

                def add(t, o, gate):
                    for s in range(W // L):
                        i = V.scalar_tensor_tensor(X[:, t, s * L:(s + 1) * L], o[:, s * L:(s + 1) * L], mod[:, 1 + l, gate + t, s:s + 1],
                                                   X[:, t, s * L:(s + 1) * L], ALU.mult, ALU.add)
                    return i

                for t in range(KT):
                    dve.wait_ge(S("w_out_mm"), 8 * l + t + 1)
                    add(t, ps[t % 4], 16).then_inc(S("w_out_added"), 1)
                norm(ncall)
                ncall += 1
                for k in range(2):
                    dve.drain().then_inc(S("mlp_bank_free"), 1)
                split_norm(W, 48 if l == 0 else 80, 2 if l == 0 else 1)
                phase_end(dve, f"l{l}_out")

                with dve.Fori(0, 4) as i:
                    for u in range(2):
                        dve.wait_ge(S("w_high"), NMOE + 16 * l + (i * 2 + u) * 2 + 2)
                        n = mlp_chunks(l, u, 1, i)[0]
                        V.tensor_tensor(low(n), slot(n), W2h.bitcast(F32), ALU.subtract).then_inc(S("w_split"), 1)
                        if l == 0:
                            c = i * 4 + u * 2
                            take_chunk(2, 24 + c, 0, c * 3, ADA_COLS)
                        for t in range(KT):
                            dve.wait_ge(S("mlp_mm"), 64 * l + (i * 2 + u) * 8 + t + 1)
                            add(t, ps[4 + t % 2], 40).then_inc(S("mlp_bank_free"), 1)
                        if l == 0:
                            take_chunk(2, 24 + c + 1, 1, (c + 1) * 3, ADA_COLS)
                if l == 0:
                    dve.wait_ge(S("ada_out"), 2 + 40)
                    gains(2)
                else:
                    norm(ncall)
                    dve.wait_ge(S("normed"), 96)
                phase_end(dve, f"l{l}_mlp")


_OUTS = [((1, L, D), "float32")]


def kernel(**inputs):
    import concourse.bacc as _bacc
    from concourse.bass_utils import run_bass_kernel_spmd as _run

    I = {k: np.asarray(v) for k, v in inputs.items()}
    nc = _bacc.Bacc("TRN2", target_bir_lowering=False, num_devices=1)
    arrays = dict(tables())
    for name in ("x", "ctx", "ctx_2"):
        arrays[name] = np.ascontiguousarray(I[name][0].T)
    for name in ("ada_w", "w_in", "w_proj_a", "w_proj_b", "w_out", "hy_filt_w1", "hy_filt_w2", "hy_filt_w3"):
        arrays[name] = I[name][0]
    for name in ("moe_w_gate", "moe_w_up", "moe_w_down"):
        a = I[name]
        arrays[name] = a.reshape(NX, *a.shape[3:])
    for name in ("ada_w_2", "w_in_2", "w_out_2", "w_mlp1_2", "w_mlp2_2"):
        arrays[name] = I[name]
    arrays["wr"] = np.concatenate([I["moe_router_g_w"][0], I["moe_router_e_w"][0].transpose(1, 0, 2).reshape(D, NX)], axis=1)
    gup = np.zeros((LAYERS, 2, 2 * RANK, GL_H * GL_K), np.float32)
    gup[:, 0, 0:RANK] = I["gla_gate_up_2"][:, 0]
    gup[:, 1, RANK:] = I["gla_gate_up_2"][:, 1]
    arrays["gup"] = gup

    def pad(*vs):
        a = np.zeros((P, len(vs)), np.float32)
        for n, v in enumerate(vs):
            a[0:v.size, n] = v.reshape(-1)
        return a

    def spread(v):
        return np.broadcast_to(v.reshape(1, -1), (P, v.size))

    parts = {
        "ada_b": columns(I["ada_b"]), "n1": columns(I["norm1_g"]), "n2": columns(I["norm2_g"]), "lb": columns(I["hgrn_lb"]),
        "hg_g": columns(I["hgrn_norm_g"]), "conv_w": columns(I["hy_conv_w"]), "conv_b": columns(I["hy_conv_b"]),
        "hy_d": columns(I["hy_d"]), "fin": columns(I["final_norm_g"]), "ada_b2": columns(I["ada_b_2"]),
        "n1_2": columns(I["norm1_g_2"]), "n2_2": columns(I["norm2_g_2"]), "gla_g": columns(I["gla_norm_g_2"]),
        "gate_b": columns(I["gla_gate_b_2"]), "fin2": columns(I["final_g_2"]),
        "c1": np.concatenate([columns(I["c"]), columns(I["c_ctx"])], axis=1),
        "c2": np.concatenate([columns(I["c_2"]), columns(I["c_ctx_2"])], axis=1),
        "decay": spread(I["ret_decay_2"]),
        "rbias": np.concatenate([spread(I["moe_router_g_b"]), spread(I["moe_router_e_b"])], axis=1),
        "eps": np.full((P, 1), EPS, np.float32), "one": np.ones((P, 1), np.float32),
        "f1": pad(I["hy_filt_b1"], I["hy_filt_freq1"]), "f2": pad(I["hy_filt_b2"], I["hy_filt_freq2"]),
    }
    arrays["vecs"] = np.ascontiguousarray(np.concatenate([parts[name] for name, _ in VEC], axis=1))
    T = {}
    feed = {}
    for name, a in arrays.items():
        feed["in_" + name] = a
        T[name] = nc.dram_tensor("in_" + name, a.shape, mybir.dt.from_np(a.dtype), kind="ExternalInput").ap()
    out = nc.dram_tensor("out_0", (D, L), F32, kind="ExternalOutput").ap()
    build(nc, T, out)
    r = _run(nc, [feed], core_ids=[0])
    return np.ascontiguousarray(r.results[0]["out_0"].T).reshape(1, L, D)
```
